# Optimizing a Trainium2 kernel written in Bass

```python
import math
import jax
import jax.numpy as jnp
from jax import lax
import numpy as np

D_MODEL = 1024
BATCH = 1
SEQ = 256
DEPTH = 2

HEAD_DIM = 64
N_HEADS = D_MODEL // HEAD_DIM
N_MIXERS = 4
GROUP_HEADS = N_HEADS // N_MIXERS
GROUP_WIDTH = GROUP_HEADS * HEAD_DIM
D_FF = 4 * D_MODEL
NORM_EPS = 1e-6
Q_BLOCK = 128
NEG_INF = -1e30
FORCE = 1e30
TINY = 1e-30
N_BUCKETS = 32
MAX_DISTANCE = 128
N_BIAS_HEADS = 3 * GROUP_HEADS
MOBA_BLOCK = 256
MOBA_TOPK = 3
MOBA_Q_CHUNK = 64
NSA_KV_DIM = HEAD_DIM
CMP_LEN = 32
CMP_STRIDE = 16
CMP_HIDDEN = 256
SLC_LEN = 64
SLC_TOPN = 4
WINDOW = 512
DIFF_HALF = HEAD_DIM // 2
SPLIT_SIZES = ((GROUP_WIDTH,) * 3
               + (GROUP_WIDTH,) * 3
               + (GROUP_WIDTH,)
               + (NSA_KV_DIM,) * 6
               + (3 * GROUP_HEADS,)
               + (GROUP_WIDTH,) * 3)
D_IN = sum(SPLIT_SIZES)


def _rmsnorm(x, g):
    xf = x.astype(jnp.float32)
    y = xf * lax.rsqrt(jnp.mean(xf * xf, axis=-1, keepdims=True) + NORM_EPS)
    return (y * g.astype(jnp.float32)).astype(x.dtype)

def _masked_softmax(logits, mask):
    s = jnp.where(mask, logits, NEG_INF)
    m = jnp.max(s, axis=-1, keepdims=True)
    e = jnp.where(mask, jnp.exp(s - m), 0.0)
    return e / jnp.maximum(jnp.sum(e, axis=-1, keepdims=True), TINY)

def _t5_bucket(dist):
    n = jnp.maximum(dist, 0)
    max_exact = N_BUCKETS // 2
    nf = jnp.maximum(n, 1).astype(jnp.float32)
    large = max_exact + (jnp.log(nf / max_exact) / math.log(MAX_DISTANCE / max_exact)
                         * (N_BUCKETS - max_exact)).astype(jnp.int32)
    large = jnp.minimum(large, N_BUCKETS - 1)
    return jnp.where(n < max_exact, n, large)

def _rel_bias(dist, table):
    return jnp.moveaxis(table[_t5_bucket(dist)], -1, 0).astype(jnp.float32)

def _rel_bias_per_head(dist, table):
    h = table.shape[1]
    h_idx = jnp.arange(h).reshape((1, h) + (1,) * (dist.ndim - 2))
    return table.T[h_idx, _t5_bucket(dist)].astype(jnp.float32)

def _heads(t, n_heads):
    b, s, _ = t.shape
    return t.reshape(b, s, n_heads, -1).transpose(0, 2, 1, 3)

def _merge_heads(t):
    b, h, s, d = t.shape
    return t.transpose(0, 2, 1, 3).reshape(b, s, h * d)

def _q_blocks(t, block):
    b, h, s = t.shape[:3]
    t = t.reshape((b, h, s // block, block) + t.shape[3:])
    return jnp.moveaxis(t, 2, 0)

def _unblock(t):
    t = jnp.moveaxis(t, 0, 2)
    b, h, n, blk = t.shape[:4]
    return t.reshape((b, h, n * blk) + t.shape[4:])

def stick_breaking_attention(q, k, v):
    b, h, s, d = q.shape
    scale = d ** -0.5
    kpos = jnp.arange(s)

    def one_block(args):
        qb, i = args
        qpos = i * Q_BLOCK + jnp.arange(Q_BLOCK)
        z = jnp.einsum('bhqd,bhkd->bhqk', qb, k).astype(jnp.float32) * scale
        mask = kpos[None, :] < qpos[:, None]
        log_keep = jnp.where(mask, -jax.nn.softplus(z), 0.0)
        suffix = lax.cumsum(log_keep, axis=3, reverse=True) - log_keep
        a = jnp.where(mask, jnp.exp(jax.nn.log_sigmoid(z) + suffix), 0.0)
        return jnp.einsum('bhqk,bhkd->bhqd', a.astype(v.dtype), v)

    out = lax.map(one_block, (_q_blocks(q, Q_BLOCK), jnp.arange(s // Q_BLOCK)))
    return _unblock(out)

def moba_attention(q, k, v, table):
    b, h, s, d = q.shape
    scale = d ** -0.5
    n_blk = -(-s // MOBA_BLOCK)
    pad = n_blk * MOBA_BLOCK - s
    k_blk = jnp.pad(k, ((0, 0), (0, 0), (0, pad), (0, 0))).reshape(b, h, n_blk, MOBA_BLOCK, d)
    v_blk = jnp.pad(v, ((0, 0), (0, 0), (0, pad), (0, 0))).reshape(b, h, n_blk, MOBA_BLOCK, d)
    k_mean = jnp.mean(k_blk.astype(jnp.float32), axis=3)
    n_sel = min(MOBA_TOPK, n_blk - 1)
    blk_ids = jnp.arange(n_blk)
    in_blk = jnp.arange(MOBA_BLOCK)
    b_idx = jnp.arange(b)[:, None, None, None]
    h_idx = jnp.arange(h)[None, :, None, None]

    def one_chunk(args):
        qc, i = args
        qpos = i * MOBA_Q_CHUNK + jnp.arange(MOBA_Q_CHUNK)
        own = (i * MOBA_Q_CHUNK) // MOBA_BLOCK
        k_own = lax.dynamic_index_in_dim(k_blk, own, axis=2, keepdims=False)
        v_own = lax.dynamic_index_in_dim(v_blk, own, axis=2, keepdims=False)
        dist_own = qpos[:, None] - (own * MOBA_BLOCK + in_blk)[None, :]
        s_own = (jnp.einsum('bhqd,bhkd->bhqk', qc, k_own).astype(jnp.float32) * scale
                 + _rel_bias(dist_own, table)[None])
        m_own = jnp.broadcast_to(dist_own >= 0, s_own.shape)
        if n_sel == 0:
            p = _masked_softmax(s_own, m_own)
            return jnp.einsum('bhqk,bhkd->bhqd', p.astype(v.dtype), v_own)
        gate = jnp.einsum('bhqd,bhnd->bhqn', qc.astype(jnp.float32), k_mean)
        gate = jnp.where(blk_ids < own, gate, NEG_INF)
        _, sel = lax.top_k(gate, n_sel)
        k_sel = k_blk[b_idx, h_idx, sel]
        v_sel = v_blk[b_idx, h_idx, sel]
        sel_pos = sel[..., None] * MOBA_BLOCK + in_blk
        dist_sel = qpos[:, None, None] - sel_pos
        s_sel = (jnp.einsum('bhqd,bhqnkd->bhqnk', qc, k_sel).astype(jnp.float32) * scale
                 + _rel_bias_per_head(dist_sel, table))
        m_sel = jnp.broadcast_to((sel < own)[..., None], s_sel.shape)
        n_flat = n_sel * MOBA_BLOCK
        s_all = jnp.concatenate([s_sel.reshape(b, h, MOBA_Q_CHUNK, n_flat), s_own], axis=-1)
        m_all = jnp.concatenate([m_sel.reshape(b, h, MOBA_Q_CHUNK, n_flat), m_own], axis=-1)
        p = _masked_softmax(s_all, m_all)
        p_sel = p[..., :n_flat].reshape(s_sel.shape)
        p_own = p[..., n_flat:]
        return (jnp.einsum('bhqnk,bhqnkd->bhqd', p_sel.astype(v.dtype), v_sel)
                + jnp.einsum('bhqk,bhkd->bhqd', p_own.astype(v.dtype), v_own))

    out = lax.map(one_chunk, (_q_blocks(q, MOBA_Q_CHUNK), jnp.arange(s // MOBA_Q_CHUNK)))
    return _unblock(out)

def nsa_attention(q, k_c, v_c, k_s, v_s, k_w, v_w, gates, pos_k, pos_v, wk1, wk2, wv1, wv2, table):
    b, h, s, d = q.shape
    scale = d ** -0.5
    tpos = jnp.arange(s)
    n_cmp = (s - CMP_LEN) // CMP_STRIDE + 1
    cmp_idx = np.arange(n_cmp)[:, None] * CMP_STRIDE + np.arange(CMP_LEN)[None, :]
    cmp_end = jnp.asarray(cmp_idx[:, -1])

    def compress(t, pos, w1, w2):
        blocks = t[:, cmp_idx] + pos
        return jax.nn.gelu(blocks.reshape(b, n_cmp, CMP_LEN * d) @ w1) @ w2

    kc = compress(k_c, pos_k, wk1, wk2)
    vc = compress(v_c, pos_v, wv1, wv2)
    dist_c = tpos[:, None] - cmp_end[None, :]
    s_c = (jnp.einsum('bhtd,bcd->bhtc', q, kc).astype(jnp.float32) * scale
           + _rel_bias(dist_c, table)[None])
    p_c = _masked_softmax(s_c, dist_c >= 0)
    o_cmp = jnp.einsum('bhtc,bcd->bhtd', p_c.astype(vc.dtype), vc)
    n_slc = s // SLC_LEN
    n_top = min(SLC_TOPN, n_slc)
    s_start = np.arange(n_slc) * SLC_LEN
    cover = np.clip(np.minimum(cmp_idx[:, -1][:, None], (s_start + SLC_LEN - 1)[None, :])
                    - np.maximum(cmp_idx[:, 0][:, None], s_start[None, :]) + 1, 0, None) / CMP_LEN
    importance = jnp.einsum('btc,cj->btj', jnp.sum(p_c, axis=1), jnp.asarray(cover, jnp.float32))
    own = tpos // SLC_LEN
    blk = jnp.arange(n_slc)
    imp = jnp.where(blk[None, :] == own[:, None], FORCE,
                    jnp.where(blk[None, :] < own[:, None], importance, NEG_INF))
    _, sel = lax.top_k(imp, n_top)
    n_qb = s // Q_BLOCK
    sel_b = sel.reshape(b, n_qb, Q_BLOCK, n_top).transpose(1, 0, 2, 3)
    ks_blk = k_s.reshape(b, n_slc, SLC_LEN, d)
    vs_blk = v_s.reshape(b, n_slc, SLC_LEN, d)
    kw_pad = jnp.pad(k_w, ((0, 0), (WINDOW, 0), (0, 0)))
    vw_pad = jnp.pad(v_w, ((0, 0), (WINDOW, 0), (0, 0)))
    b_idx = jnp.arange(b)[:, None, None]
    in_slc = jnp.arange(SLC_LEN)
    in_win = jnp.arange(WINDOW + Q_BLOCK)

    def one_block(args):
        qb, selc, i = args
        qpos = i * Q_BLOCK + jnp.arange(Q_BLOCK)
        k_sel = ks_blk[b_idx, selc]
        v_sel = vs_blk[b_idx, selc]
        dist_s = qpos[:, None, None] - (selc[..., None] * SLC_LEN + in_slc)
        s_s = (jnp.einsum('bhqd,bqnkd->bhqnk', qb, k_sel).astype(jnp.float32) * scale
               + jnp.moveaxis(table[_t5_bucket(dist_s)], -1, 1).astype(jnp.float32))
        m_s = jnp.broadcast_to((dist_s >= 0)[:, None], s_s.shape)
        flat = (b, h, Q_BLOCK, n_top * SLC_LEN)
        p_s = _masked_softmax(s_s.reshape(flat), m_s.reshape(flat)).reshape(s_s.shape)
        o_s = jnp.einsum('bhqnk,bqnkd->bhqd', p_s.astype(v_sel.dtype), v_sel)
        kw = lax.dynamic_slice_in_dim(kw_pad, i * Q_BLOCK, WINDOW + Q_BLOCK, axis=1)
        vw = lax.dynamic_slice_in_dim(vw_pad, i * Q_BLOCK, WINDOW + Q_BLOCK, axis=1)
        kpos = i * Q_BLOCK - WINDOW + in_win
        dist_w = qpos[:, None] - kpos[None, :]
        m_w = (dist_w >= 0) & (dist_w < WINDOW) & (kpos[None, :] >= 0)
        s_w = (jnp.einsum('bhqd,bkd->bhqk', qb, kw).astype(jnp.float32) * scale
               + _rel_bias(dist_w, table)[None])
        p_w = _masked_softmax(s_w, m_w)
        o_w = jnp.einsum('bhqk,bkd->bhqd', p_w.astype(vw.dtype), vw)
        return o_s, o_w

    o_slc, o_win = lax.map(one_block, (_q_blocks(q, Q_BLOCK), sel_b, jnp.arange(n_qb)))
    o_slc, o_win = _unblock(o_slc), _unblock(o_win)
    g = jax.nn.sigmoid(gates.astype(jnp.float32)).reshape(b, s, 3, h).transpose(2, 0, 3, 1)[..., None]
    g = g.astype(q.dtype)
    return g[0] * o_cmp + g[1] * o_slc + g[2] * o_win

def diff_attention(q, k, v, lam, table):
    s = q.shape[2]
    scale = q.shape[-1] ** -0.5
    kpos = jnp.arange(s)

    def one_block(args):
        qb, i = args
        qpos = i * Q_BLOCK + jnp.arange(Q_BLOCK)
        dist = qpos[:, None] - kpos[None, :]
        sc = (jnp.einsum('bhqcd,bhkcd->bhcqk', qb, k).astype(jnp.float32) * scale
              + _rel_bias(dist, table)[None, :, None])
        p = _masked_softmax(sc, dist >= 0)
        w = p[:, :, 0] - lam * p[:, :, 1]
        return jnp.einsum('bhqk,bhkd->bhqd', w.astype(v.dtype), v)

    out = lax.map(one_block, (_q_blocks(q, Q_BLOCK), jnp.arange(s // Q_BLOCK)))
    return _unblock(out)

def first_inputs(seed: int = 0) -> dict:
    key = jax.random.key(seed)
    ks = jax.random.split(key, 17)
    f32 = jnp.float32

    def nrm(k, shape, scale):
        return jax.random.normal(k, shape, f32) * scale

    return {
        "x": nrm(ks[0], (BATCH, SEQ, D_MODEL), 1.0),
        "w_in": nrm(ks[1], (DEPTH, D_MODEL, D_IN), D_MODEL ** -0.5),
        "w_out": nrm(ks[2], (DEPTH, D_MODEL, D_MODEL), D_MODEL ** -0.5),
        "w_up": nrm(ks[3], (DEPTH, D_MODEL, D_FF), D_MODEL ** -0.5),
        "w_down": nrm(ks[4], (DEPTH, D_FF, D_MODEL), D_FF ** -0.5),
        "norm_attn": 1.0 + nrm(ks[5], (DEPTH, D_MODEL), 0.05),
        "norm_mlp": 1.0 + nrm(ks[6], (DEPTH, D_MODEL), 0.05),
        "cmp_pos_k": nrm(ks[7], (DEPTH, CMP_LEN, HEAD_DIM), 0.1),
        "cmp_pos_v": nrm(ks[8], (DEPTH, CMP_LEN, HEAD_DIM), 0.1),
        "cmp_k_w1": nrm(ks[9], (DEPTH, CMP_LEN * HEAD_DIM, CMP_HIDDEN), (CMP_LEN * HEAD_DIM) ** -0.5),
        "cmp_k_w2": nrm(ks[10], (DEPTH, CMP_HIDDEN, HEAD_DIM), CMP_HIDDEN ** -0.5),
        "cmp_v_w1": nrm(ks[11], (DEPTH, CMP_LEN * HEAD_DIM, CMP_HIDDEN), (CMP_LEN * HEAD_DIM) ** -0.5),
        "cmp_v_w2": nrm(ks[12], (DEPTH, CMP_HIDDEN, HEAD_DIM), CMP_HIDDEN ** -0.5),
        "diff_lambda": nrm(ks[13], (DEPTH, 4, DIFF_HALF), 0.1),
        "diff_subln": 1.0 + nrm(ks[14], (DEPTH, HEAD_DIM), 0.05),
        "rel_bias": nrm(ks[15], (N_BUCKETS, N_BIAS_HEADS), 0.2),
        "final_norm": 1.0 + nrm(ks[16], (D_MODEL,), 0.05),
    }

def first_block(x, w_in, w_out, w_up, w_down, norm_attn, norm_mlp, cmp_pos_k, cmp_pos_v,
              cmp_k_w1, cmp_k_w2, cmp_v_w1, cmp_v_w2, diff_lambda, diff_subln, rel_bias, final_norm):
    bias_moba = rel_bias[:, :GROUP_HEADS]
    bias_nsa = rel_bias[:, GROUP_HEADS:2 * GROUP_HEADS]
    bias_diff = rel_bias[:, 2 * GROUP_HEADS:]
    split_at = np.cumsum(SPLIT_SIZES)[:-1].tolist()
    b, s, _ = x.shape
    for layer in range(DEPTH):
        h = _rmsnorm(x, norm_attn[layer])
        proj = h @ w_in[layer]
        (sb_q, sb_k, sb_v, mb_q, mb_k, mb_v, ns_q, ns_kc, ns_vc, ns_ks, ns_vs, ns_kw, ns_vw,
         ns_g, df_q, df_k, df_v) = jnp.split(proj, split_at, axis=-1)
        o_sb = stick_breaking_attention(_heads(sb_q, GROUP_HEADS), _heads(sb_k, GROUP_HEADS),
                                        _heads(sb_v, GROUP_HEADS))
        o_mb = moba_attention(_heads(mb_q, GROUP_HEADS), _heads(mb_k, GROUP_HEADS),
                              _heads(mb_v, GROUP_HEADS), bias_moba)
        o_ns = nsa_attention(_heads(ns_q, GROUP_HEADS), ns_kc, ns_vc, ns_ks, ns_vs, ns_kw, ns_vw, ns_g,
                             cmp_pos_k[layer], cmp_pos_v[layer], cmp_k_w1[layer], cmp_k_w2[layer],
                             cmp_v_w1[layer], cmp_v_w2[layer], bias_nsa)
        lambda_init = 0.8 - 0.6 * math.exp(-0.3 * layer)
        lv = diff_lambda[layer].astype(jnp.float32)
        lam = jnp.exp(jnp.sum(lv[0] * lv[1])) - jnp.exp(jnp.sum(lv[2] * lv[3])) + lambda_init
        dq = df_q.reshape(b, s, GROUP_HEADS, 2, DIFF_HALF).transpose(0, 2, 1, 3, 4)
        dk = df_k.reshape(b, s, GROUP_HEADS, 2, DIFF_HALF).transpose(0, 2, 1, 3, 4)
        o_df = diff_attention(dq, dk, _heads(df_v, GROUP_HEADS), lam, bias_diff)
        o_df = _rmsnorm(o_df, diff_subln[layer]) * (1.0 - lambda_init)
        mixed = jnp.concatenate([_merge_heads(o_sb), _merge_heads(o_mb),
                                 _merge_heads(o_ns), _merge_heads(o_df)], axis=-1)
        x = x + mixed @ w_out[layer]
        h2 = _rmsnorm(x, norm_mlp[layer])
        x = x + jnp.square(jax.nn.relu(h2 @ w_up[layer])) @ w_down[layer]
    return _rmsnorm(x, final_norm)


GRID_W = 64
CTX_LEN = 256
N_MIXERS_2 = 3
CHUNK = 64
EPS = 1e-6
ALPHA = (2 * DEPTH) ** 0.25
BETA = (8 * DEPTH) ** -0.25

M_INNER = 2 * D_MODEL
M_HEADS = 4
M_DV = M_INNER // M_HEADS
M_DQK = M_DV // 2
M_CONV = 3

A_HEADS = 8
A_QLORA = 384
A_KVLORA = 256
A_DNOPE = 128
A_DROPE = 64
A_DV = 128
ROPE_BASE = 10000.0

G_HEADS = 4
G_DK = D_MODEL // (2 * G_HEADS)
G_DV = D_MODEL // G_HEADS
G_RANK = 16
G_TAU = 16.0

FFN_DIM = 2816
FFN_CONV = 3


def _count(kind):
    return len(range(kind, DEPTH, N_MIXERS_2))

def _layer_norm(x, g, b):
    xf = x.astype(jnp.float32)
    mu = jnp.mean(xf, -1, keepdims=True)
    var = jnp.mean(jnp.square(xf - mu), -1, keepdims=True)
    return ((xf - mu) * lax.rsqrt(var + EPS)).astype(x.dtype) * g + b

def _rms_norm(x, g):
    xf = x.astype(jnp.float32)
    return (xf * lax.rsqrt(jnp.mean(jnp.square(xf), -1, keepdims=True) + EPS)).astype(x.dtype) * g

def _head_rms_norm(x, g):
    B, T, H, d = x.shape
    return _rms_norm(x, g.reshape(H, d)).reshape(B, T, H * d)

def _dwconv(x, w, b):
    k = w.shape[0]
    y = lax.conv_general_dilated(x, w[:, None, :].astype(x.dtype), (1,), [(k // 2, k // 2)],
                                 dimension_numbers=("NWC", "WIO", "NWC"),
                                 feature_group_count=x.shape[-1])
    return y + b

def _modulation(cond, w, b):
    m = jax.nn.silu(cond) @ w + b
    return jnp.split(m[:, None, :], 6, axis=-1)

def _modulate(x, shift, scale):
    return x * (1 + scale) + shift

def _axial_angles(n_tokens):
    rows = n_tokens // GRID_W
    row = jnp.repeat(jnp.arange(rows, dtype=jnp.float32), GRID_W)
    col = jnp.tile(jnp.arange(GRID_W, dtype=jnp.float32), rows)
    n_freq = A_DROPE // 4
    inv_freq = ROPE_BASE ** (-jnp.arange(n_freq, dtype=jnp.float32) / n_freq)
    return row[:, None] * inv_freq, col[:, None] * inv_freq

def _rope_half(x, ang):
    x1, x2 = jnp.split(x, 2, axis=-1)
    cos = jnp.cos(ang).astype(x.dtype)
    sin = jnp.sin(ang).astype(x.dtype)
    return jnp.concatenate([x1 * cos - x2 * sin, x2 * cos + x1 * sin], -1)

def _axial_rope(x, ang_row, ang_col):
    xr, xc = jnp.split(x, 2, axis=-1)
    return jnp.concatenate([_rope_half(xr, ang_row), _rope_half(xc, ang_col)], -1)

def _time_flip(a, direction):
    return jnp.flip(a, axis=2) if direction == 1 else a

def _two_way(scan_fn, shared_c, gates_c, shared_l, gates_l, init):
    out_c, out_l = None, None
    for d in range(2):
        args_c = [_time_flip(a, d) for a in shared_c + tuple(g[d] for g in gates_c)]
        hc, state = scan_fn(*args_c, init)
        args_l = [_time_flip(a, d) for a in shared_l + tuple(g[d] for g in gates_l)]
        hl, _ = scan_fn(*args_l, state)
        hc, hl = _time_flip(hc, d), _time_flip(hl, d)
        out_c = hc if out_c is None else out_c + hc
        out_l = hl if out_l is None else out_l + hl
    return out_c, out_l

def _mlstm_chunk_scan(q, k, v, li, lf, state):
    B, H, T, _ = q.shape
    nc = T // CHUNK

    def chunks(a):
        a = a.astype(jnp.float32)
        return jnp.moveaxis(a.reshape(B, H, nc, CHUNK, *a.shape[3:]), 2, 0)

    tril = jnp.tril(jnp.ones((CHUNK, CHUNK), bool))

    def step(carry, inp):
        C, n, m = carry
        qc, kc, vc, ic, fc = inp
        b = jnp.cumsum(fc, axis=-1)
        dmat = jnp.where(tril, b[..., :, None] - b[..., None, :] + ic[..., None, :], -jnp.inf)
        inter = b + m[..., None]
        mj = jnp.maximum(inter, jnp.max(dmat, -1))
        wmat = jnp.exp(dmat - mj[..., None]) * jnp.einsum("bhjd,bhsd->bhjs", qc, kc)
        g = jnp.exp(inter - mj)
        num = g[..., None] * jnp.einsum("bhjd,bhde->bhje", qc, C) + jnp.einsum("bhjs,bhse->bhje", wmat, vc)
        den = g * jnp.einsum("bhjd,bhd->bhj", qc, n) + jnp.sum(wmat, -1)
        h = num / jnp.maximum(jnp.abs(den), jnp.exp(-mj))[..., None]
        bl = b[..., -1]
        ds = bl[..., None] - b + ic
        m_new = jnp.maximum(bl + m, jnp.max(ds, -1))
        kw = kc * jnp.exp(ds - m_new[..., None])[..., None]
        decay = jnp.exp(bl + m - m_new)
        C = decay[..., None, None] * C + jnp.einsum("bhsd,bhse->bhde", kw, vc)
        n = decay[..., None] * n + jnp.sum(kw, axis=2)
        return (C, n, m_new), h

    state, hs = lax.scan(step, state, tuple(chunks(a) for a in (q, k, v, li, lf)))
    return jnp.moveaxis(hs, 0, 2).reshape(B, H, T, -1), state

def _mlstm_inputs(h, w_up, conv_w, conv_b, w_qk, w_v, w_gates, b_gates):
    B, T, _ = h.shape
    x_m = h @ w_up
    x_c = jax.nn.silu(_dwconv(x_m, conv_w, conv_b))
    q, k = jnp.split(x_c @ w_qk, 2, axis=-1)
    q = q.reshape(B, T, M_HEADS, M_DQK).transpose(0, 2, 1, 3)
    k = k.reshape(B, T, M_HEADS, M_DQK).transpose(0, 2, 1, 3) * (M_DQK ** -0.5)
    v = (x_m @ w_v).reshape(B, T, M_HEADS, M_DV).transpose(0, 2, 1, 3)
    gates = jnp.einsum("bti,zig->zbgt", x_c, w_gates) + b_gates[:, None, :, None]
    li = gates[:, :, :M_HEADS].astype(jnp.float32)
    lf = jax.nn.log_sigmoid(gates[:, :, M_HEADS:].astype(jnp.float32))
    return (q, k, v), (li, lf)

def _mlstm_mixer(hl, hc, need_ctx, w_up, conv_w, conv_b, w_qk, w_v, w_gates, b_gates, w_og, norm_g, w_out):
    sh_l, gt_l = _mlstm_inputs(hl, w_up, conv_w, conv_b, w_qk, w_v, w_gates, b_gates)
    sh_c, gt_c = _mlstm_inputs(hc, w_up, conv_w, conv_b, w_qk, w_v, w_gates, b_gates)
    B = hl.shape[0]
    init = (jnp.zeros((B, M_HEADS, M_DQK, M_DV), jnp.float32),
            jnp.zeros((B, M_HEADS, M_DQK), jnp.float32),
            jnp.zeros((B, M_HEADS), jnp.float32))
    s_c, s_l = _two_way(_mlstm_chunk_scan, sh_c, gt_c, sh_l, gt_l, init)

    def out(h_in, s):
        Bq, T, _ = h_in.shape
        o = jax.nn.sigmoid(h_in @ w_og).reshape(Bq, T, M_HEADS, M_DV)
        hsum = o * s.transpose(0, 2, 1, 3).astype(h_in.dtype)
        return _head_rms_norm(hsum, norm_g) @ w_out

    return out(hl, s_l), (out(hc, s_c) if need_ctx else None)

def _mla_q(h, w_dq, q_norm, w_uq, ang):
    B, T, _ = h.shape
    q = (_rms_norm(h @ w_dq, q_norm) @ w_uq).reshape(B, T, A_HEADS, A_DNOPE + A_DROPE)
    if ang is None:
        return q
    q_nope, q_rope = jnp.split(q, [A_DNOPE], axis=-1)
    return jnp.concatenate([q_nope, _axial_rope(q_rope, ang[0][:, None], ang[1][:, None])], -1)

def _mla_kv(h, w_dkv, kv_norm, w_ukv, ang):
    B, T, _ = h.shape
    ckv, k_rope = jnp.split(h @ w_dkv, [A_KVLORA], axis=-1)
    if ang is not None:
        k_rope = _axial_rope(k_rope, ang[0], ang[1])
    kv = (_rms_norm(ckv, kv_norm) @ w_ukv).reshape(B, T, A_HEADS, A_DNOPE + A_DV)
    k_nope, v = jnp.split(kv, [A_DNOPE], axis=-1)
    k = jnp.concatenate([k_nope, jnp.broadcast_to(k_rope[:, :, None], (B, T, A_HEADS, A_DROPE))], -1)
    return k, v

def _attend(q, k, v):
    s = jnp.einsum("bqhd,bkhd->bhqk", q, k).astype(jnp.float32) * ((A_DNOPE + A_DROPE) ** -0.5)
    p = jax.nn.softmax(s, axis=-1).astype(v.dtype)
    return jnp.einsum("bhqk,bkhd->bqhd", p, v)

def _blocked_attend(q, k, v):
    B, T, H, d = q.shape
    qb = q.reshape(B, T // Q_BLOCK, Q_BLOCK, H, d).transpose(1, 0, 2, 3, 4)
    o = lax.map(lambda qi: _attend(qi, k, v), qb)
    return o.transpose(1, 0, 2, 3, 4).reshape(B, T, H, -1)

def _mla_mixer(hl, hc, need_ctx, ang, w_dq, q_norm, w_uq, w_dkv, kv_norm, w_ukv, w_out):
    B, T, _ = hl.shape
    kc, vc = _mla_kv(hc, w_dkv, kv_norm, w_ukv, None)
    kl, vl = _mla_kv(hl, w_dkv, kv_norm, w_ukv, ang)
    ql = _mla_q(hl, w_dq, q_norm, w_uq, ang)
    k_all = jnp.concatenate([kc, kl], axis=1)
    v_all = jnp.concatenate([vc, vl], axis=1)
    yl = _blocked_attend(ql, k_all, v_all).reshape(B, T, -1) @ w_out
    yc = None
    if need_ctx:
        qc = _mla_q(hc, w_dq, q_norm, w_uq, None)
        yc = _attend(qc, kc, vc).reshape(B, hc.shape[1], -1) @ w_out
    return yl, yc

def _gla_chunk_scan(q, k, v, la, S):
    B, H, T, _ = q.shape
    nc = T // CHUNK

    def chunks(a):
        a = a.astype(jnp.float32)
        return jnp.moveaxis(a.reshape(B, H, nc, CHUNK, *a.shape[3:]), 2, 0)

    tril = jnp.tril(jnp.ones((CHUNK, CHUNK), bool))

    def step(S, inp):
        qc, kc, vc, ac = inp
        b = jnp.cumsum(ac, axis=-2)
        inter = jnp.einsum("bhjd,bhde->bhje", qc * jnp.exp(b), S)
        rel = jnp.where(tril[:, :, None], b[:, :, :, None, :] - b[:, :, None, :, :], -jnp.inf)
        att = jnp.sum(qc[:, :, :, None, :] * kc[:, :, None, :, :] * jnp.exp(rel), axis=-1)
        o = inter + jnp.einsum("bhjs,bhse->bhje", att, vc)
        bl = b[:, :, -1:, :]
        S = jnp.exp(bl[:, :, 0, :, None]) * S + jnp.einsum("bhsd,bhse->bhde", kc * jnp.exp(bl - b), vc)
        return S, o

    S, os_ = lax.scan(step, S, tuple(chunks(a) for a in (q, k, v, la)))
    return jnp.moveaxis(os_, 0, 2).reshape(B, H, T, -1), S

def _gla_inputs(h, w_qk, w_v, w_a1, w_a2, b_a):
    B, T, _ = h.shape
    q, k = jnp.split(h @ w_qk, 2, axis=-1)
    q = q.reshape(B, T, G_HEADS, G_DK).transpose(0, 2, 1, 3) * (G_DK ** -0.5)
    k = k.reshape(B, T, G_HEADS, G_DK).transpose(0, 2, 1, 3)
    v = (h @ w_v).reshape(B, T, G_HEADS, G_DV).transpose(0, 2, 1, 3)
    z = jnp.einsum("zbtr,zrk->zbtk", jnp.einsum("btd,zdr->zbtr", h, w_a1), w_a2) + b_a[:, None, None, :]
    la = jax.nn.log_sigmoid(z.astype(jnp.float32)) / G_TAU
    la = la.reshape(2, B, T, G_HEADS, G_DK).transpose(0, 1, 3, 2, 4)
    return (q, k, v), (la,)

def _gla_mixer(hl, hc, need_ctx, w_qk, w_v, w_r, w_a1, w_a2, b_a, norm_g, w_out):
    sh_l, gt_l = _gla_inputs(hl, w_qk, w_v, w_a1, w_a2, b_a)
    sh_c, gt_c = _gla_inputs(hc, w_qk, w_v, w_a1, w_a2, b_a)
    init = jnp.zeros((hl.shape[0], G_HEADS, G_DK, G_DV), jnp.float32)
    s_c, s_l = _two_way(_gla_chunk_scan, sh_c, gt_c, sh_l, gt_l, init)

    def out(h_in, s):
        o = _head_rms_norm(s.transpose(0, 2, 1, 3).astype(h_in.dtype), norm_g)
        return (o * jax.nn.silu(h_in @ w_r)) @ w_out

    return out(hl, s_l), (out(hc, s_c) if need_ctx else None)

def _conv_ffn(h, w_in, conv_w, conv_b, w_out):
    gate, up = jnp.split(h @ w_in, 2, axis=-1)
    return (jax.nn.silu(_dwconv(gate, conv_w, conv_b)) * up) @ w_out

def second_inputs(seed: int = 0) -> dict:
    key = jax.random.key(seed)
    keys = iter(jax.random.split(key, 48))
    D = D_MODEL
    nA, nB, nC = _count(0), _count(1), _count(2)

    def normal(shape):
        return jax.random.normal(next(keys), shape, jnp.float32)

    def dense(shape, fan_in, scale=1.0):
        return normal(shape) * (scale * fan_in ** -0.5)

    def gain(shape):
        return 1.0 + 0.05 * normal(shape)

    def bias(shape, s=0.02):
        return s * normal(shape)

    f_bias = jnp.asarray(np.linspace(3.0, 6.0, M_HEADS), jnp.float32)
    w_ukv = dense((nB, A_KVLORA, A_HEADS, A_DNOPE + A_DV), A_KVLORA)
    w_ukv = w_ukv.at[..., A_DNOPE:].multiply(BETA).reshape(nB, A_KVLORA, A_HEADS * (A_DNOPE + A_DV))
    return {
        "x": normal((BATCH, SEQ, D)),
        "c": normal((BATCH, D)),
        "ctx": normal((BATCH, CTX_LEN, D)),
        "c_ctx": normal((D,)),
        "ada_w": dense((DEPTH, D, 6 * D), D, 0.5),
        "ada_b": bias((DEPTH, 6 * D)),
        "ln_g": gain((DEPTH, 2, D)),
        "ln_b": bias((DEPTH, 2, D)),
        "ffn_w_in": dense((DEPTH, D, 2 * FFN_DIM), D, BETA),
        "ffn_conv_w": dense((DEPTH, FFN_CONV, FFN_DIM), FFN_CONV),
        "ffn_conv_b": bias((DEPTH, FFN_DIM)),
        "ffn_w_out": dense((DEPTH, FFN_DIM, D), FFN_DIM, BETA),
        "m_w_up": dense((nA, D, M_INNER), D),
        "m_conv_w": dense((nA, M_CONV, M_INNER), M_CONV),
        "m_conv_b": bias((nA, M_INNER)),
        "m_w_qk": dense((nA, M_INNER, 2 * M_HEADS * M_DQK), M_INNER),
        "m_w_v": dense((nA, M_INNER, M_HEADS * M_DV), M_INNER, BETA),
        "m_w_gates": dense((nA, 2, M_INNER, 2 * M_HEADS), M_INNER, 0.5),
        "m_b_gates": jnp.concatenate([0.1 * normal((nA, 2, M_HEADS)),
                                      f_bias + 0.1 * normal((nA, 2, M_HEADS))], axis=-1),
        "m_w_og": dense((nA, D, M_HEADS * M_DV), D),
        "m_norm_g": gain((nA, M_HEADS * M_DV)),
        "m_w_out": dense((nA, M_HEADS * M_DV, D), M_HEADS * M_DV, BETA),
        "a_w_dq": dense((nB, D, A_QLORA), D),
        "a_q_norm": gain((nB, A_QLORA)),
        "a_w_uq": dense((nB, A_QLORA, A_HEADS * (A_DNOPE + A_DROPE)), A_QLORA),
        "a_w_dkv": dense((nB, D, A_KVLORA + A_DROPE), D),
        "a_kv_norm": gain((nB, A_KVLORA)),
        "a_w_ukv": w_ukv,
        "a_w_out": dense((nB, A_HEADS * A_DV, D), A_HEADS * A_DV, BETA),
        "g_w_qk": dense((nC, D, 2 * G_HEADS * G_DK), D),
        "g_w_v": dense((nC, D, G_HEADS * G_DV), D, BETA),
        "g_w_r": dense((nC, D, G_HEADS * G_DV), D),
        "g_w_a1": dense((nC, 2, D, G_RANK), D),
        "g_w_a2": dense((nC, 2, G_RANK, G_HEADS * G_DK), G_RANK),
        "g_b_a": bias((nC, 2, G_HEADS * G_DK), 0.1),
        "g_norm_g": gain((nC, G_HEADS * G_DV)),
        "g_w_out": dense((nC, G_HEADS * G_DV, D), G_HEADS * G_DV, BETA),
    }

def second_block(x, c, ctx, c_ctx, ada_w, ada_b, ln_g, ln_b,
              ffn_w_in, ffn_conv_w, ffn_conv_b, ffn_w_out,
              m_w_up, m_conv_w, m_conv_b, m_w_qk, m_w_v, m_w_gates, m_b_gates, m_w_og, m_norm_g, m_w_out,
              a_w_dq, a_q_norm, a_w_uq, a_w_dkv, a_kv_norm, a_w_ukv, a_w_out,
              g_w_qk, g_w_v, g_w_r, g_w_a1, g_w_a2, g_b_a, g_norm_g, g_w_out):
    ang = _axial_angles(x.shape[1])
    xc = ctx
    for i in range(DEPTH):
        need_ctx = i < DEPTH - 1
        kind, j = i % N_MIXERS_2, i // N_MIXERS_2
        ml = _modulation(c, ada_w[i], ada_b[i])
        mc = _modulation(c_ctx[None, :], ada_w[i], ada_b[i])
        hl = _modulate(x, ml[0], ml[1])
        hc = _modulate(xc, mc[0], mc[1])
        if kind == 0:
            yl, yc = _mlstm_mixer(hl, hc, need_ctx, m_w_up[j], m_conv_w[j], m_conv_b[j], m_w_qk[j], m_w_v[j],
                                  m_w_gates[j], m_b_gates[j], m_w_og[j], m_norm_g[j], m_w_out[j])
        elif kind == 1:
            yl, yc = _mla_mixer(hl, hc, need_ctx, ang, a_w_dq[j], a_q_norm[j], a_w_uq[j], a_w_dkv[j],
                                a_kv_norm[j], a_w_ukv[j], a_w_out[j])
        else:
            yl, yc = _gla_mixer(hl, hc, need_ctx, g_w_qk[j], g_w_v[j], g_w_r[j], g_w_a1[j], g_w_a2[j],
                                g_b_a[j], g_norm_g[j], g_w_out[j])
        x = _layer_norm(ALPHA * x + ml[2] * yl, ln_g[i, 0], ln_b[i, 0])
        f = _conv_ffn(_modulate(x, ml[3], ml[4]), ffn_w_in[i], ffn_conv_w[i], ffn_conv_b[i], ffn_w_out[i])
        x = _layer_norm(ALPHA * x + ml[5] * f, ln_g[i, 1], ln_b[i, 1])
        if need_ctx:
            xc = _layer_norm(ALPHA * xc + mc[2] * yc, ln_g[i, 0], ln_b[i, 0])
            fc = _conv_ffn(_modulate(xc, mc[3], mc[4]), ffn_w_in[i], ffn_conv_w[i], ffn_conv_b[i], ffn_w_out[i])
            xc = _layer_norm(ALPHA * xc + mc[5] * fc, ln_g[i, 1], ln_b[i, 1])
    return x


def setup_inputs(seed=0):
    out = dict(first_inputs(seed))
    for name, value in second_inputs(seed + 1).items():
        if name != "x":
            out[name + "_2"] = value
    return out


def reference(
    x, w_in, w_out, w_up, w_down, norm_attn, norm_mlp, cmp_pos_k, cmp_pos_v, cmp_k_w1, cmp_k_w2,
    cmp_v_w1, cmp_v_w2, diff_lambda, diff_subln, rel_bias, final_norm, c_2, ctx_2, c_ctx_2,
    ada_w_2, ada_b_2, ln_g_2, ln_b_2, ffn_w_in_2, ffn_conv_w_2, ffn_conv_b_2, ffn_w_out_2,
    m_w_up_2, m_conv_w_2, m_conv_b_2, m_w_qk_2, m_w_v_2, m_w_gates_2, m_b_gates_2, m_w_og_2,
    m_norm_g_2, m_w_out_2, a_w_dq_2, a_q_norm_2, a_w_uq_2, a_w_dkv_2, a_kv_norm_2, a_w_ukv_2,
    a_w_out_2, g_w_qk_2, g_w_v_2, g_w_r_2, g_w_a1_2, g_w_a2_2, g_b_a_2, g_norm_g_2, g_w_out_2,
):
    x = first_block(
        x, w_in, w_out, w_up, w_down, norm_attn, norm_mlp, cmp_pos_k, cmp_pos_v, cmp_k_w1,
        cmp_k_w2, cmp_v_w1, cmp_v_w2, diff_lambda, diff_subln, rel_bias, final_norm,
    )
    return second_block(
        x, c_2, ctx_2, c_ctx_2, ada_w_2, ada_b_2, ln_g_2, ln_b_2, ffn_w_in_2, ffn_conv_w_2,
        ffn_conv_b_2, ffn_w_out_2, m_w_up_2, m_conv_w_2, m_conv_b_2, m_w_qk_2, m_w_v_2,
        m_w_gates_2, m_b_gates_2, m_w_og_2, m_norm_g_2, m_w_out_2, a_w_dq_2, a_q_norm_2,
        a_w_uq_2, a_w_dkv_2, a_kv_norm_2, a_w_ukv_2, a_w_out_2, g_w_qk_2, g_w_v_2, g_w_r_2,
        g_w_a1_2, g_w_a2_2, g_b_a_2, g_norm_g_2, g_w_out_2,
    )


_drawn_inputs = setup_inputs


def setup_inputs(seed=0):
    import zlib

    import numpy as np

    out = dict(_drawn_inputs(seed))
    spreads = {}
    factors = {'cmp_pos_k': 8.0,
     'cmp_pos_v': 3.117,
     'diff_lambda': 3.555,
     'ada_b_2': 5.054,
     'ffn_conv_b_2': 8.0,
     'm_conv_b_2': 8.0,
     'm_w_gates_2': 3.162,
     'm_norm_g_2': 8.0,
     'a_w_dq_2': 8.0,
     'a_q_norm_2': 8.0,
     'a_w_uq_2': 8.0,
     'a_w_dkv_2': 3.552,
     'a_kv_norm_2': 8.0,
     'a_w_out_2': 3.721}
    for name, (base, spread) in spreads.items():
        noise = np.random.default_rng([zlib.crc32(name.encode()), seed]).standard_normal(out[name].shape)
        drawn = base * np.exp(spread * noise) if base else spread * noise
        out[name] = jnp.asarray(drawn.astype(out[name].dtype))
    for name, factor in factors.items():
        out[name] = (out[name] * factor).astype(out[name].dtype)
    return out
```

```python
import math
from contextlib import ExitStack

import numpy as np
import concourse.bass as bass
from concourse import mybir

P = 128
F32 = mybir.dt.float32
ALU = mybir.AluOpType
ACT = mybir.ActivationFunctionType
AX = mybir.AxisListType.X

D = 1024
KD = D // P
T = 256
T2 = 2 * T
LAT = T
DEPTH = 2
EPS = 1e-6
NEG = -1e30
HD = 64
CMP_N = 15
SLOT = 2048
R = 4
BANKS = 8
ALPHA = (2 * DEPTH) ** 0.25
NFF = 22
MH = 4
MK = 16
AH = 8
A_SCALE = 192 ** -0.5
OFF = (0, 512, 1024, 1280)
T_AT = (0, 0, T, T)


class Plan:

    def __init__(self):
        self.at, self.n = {}, 0

    def add(self, name, count=1):
        self.at[name] = self.n
        self.n += count

    def __call__(self, name, i=0):
        return self.at[name] + i


def units():
    out = []
    for h in range(4):
        out.append(dict(kind="sb", h=h, q=h // 2, k=2 + h // 2, r=64 * (h % 2), kk=64, v=("vn", 0), first=True,
                        last=True, chunk=h // 2, row=64 * (h % 2)))
    for h in range(4):
        out.append(dict(kind="mb", h=h, q=4 + h // 2, k=6 + h // 2, r=64 * (h % 2), kk=64, v=("vn", 1), bias=h,
                        first=True, last=True, chunk=2 + h // 2, row=64 * (h % 2)))
    for h in range(4):
        for b, kind in enumerate(("cmp", "slc", "win")):
            out.append(dict(kind=kind, h=h, q=8 + h // 2, k=13 + b, r=64 * (h % 2), kk=64, v=(kind, 0), bias=4 + h,
                            first=b == 0, last=b == 2, chunk=4 + h // 2, row=64 * (h % 2), gate=4 * b + h))
    for h in range(4):
        for c in range(2):
            out.append(dict(kind="df", h=h, q=10 + h // 2, k=12 + h // 2, r=64 * (h % 2) + 32 * c, kk=32, v=("vn", 2),
                            bias=8 + h, first=c == 0, last=c == 1, chunk=6 + h // 2, row=64 * (h % 2), c=c))
    return out


UNITS = units()
NU = len(UNITS)


def params_layout():
    p = Plan()
    for l in range(DEPTH):
        p.add(("g_attn", l), KD)
        p.add(("g_mlp", l), KD)
        p.add(("subln", l), 1)
        p.add(("pos", l), 32)
        p.add(("w2k", l), 256)
        p.add(("w2v", l), 128)
        p.add(("dlam", l), 128)
        p.add(("ada_b", l), 48)
        for s in range(2):
            p.add(("ln_g", l, s), KD)
            p.add(("ln_b", l, s), KD)
        p.add(("fconv_w", l), 3 * NFF)
        p.add(("fconv_b", l), NFF)
    p.add("g_final", KD)
    p.add("table", 12)
    p.add("cond", 16)
    p.add("mconv_w", 48)
    p.add("mconv_b", 16)
    p.add("b_gates", 1)
    p.add("m_norm", 16)
    p.add("q_norm", 3)
    p.add("kv_norm", 2)
    return p


def consts_layout():
    p = Plan()
    p.add("ident", 128)
    p.add("ones", 128)
    p.add("halves", 128)
    p.add("strict", 384)
    p.add("cmask", 32)
    p.add("rope", 256)
    p.add("tri", 256)
    p.add("pick", 127)
    return p


PAR = params_layout()
CON = consts_layout()


def slot_plan():
    w = Plan()
    for l in range(DEPTH):
        w.add(("proj", l), 9)
        w.add(("nat", l), 4)
        w.add(("cmp", l), 4)
        w.add(("ada", l), 24)
        w.add(("out", l), 4)
        w.add(("up", l), 16)
        w.add(("down", l), 16)
    w.add("m_up", 8)
    w.add("m_gates")
    w.add("m_v", 16)
    for h in range(MH):
        w.add(("m_qk", h), 4)
        w.add(("m_og", h), 2)
    w.add("m_out", 8)
    w.add(("ffn_in", 0), NFF)
    w.add(("ffn_out", 0), NFF // 2)
    w.add("a_dkv", 2)
    w.add("a_dq", 2)
    w.add("a_ukv", 2)
    w.add("a_uq", 4)
    w.add("a_out", 4)
    w.add(("ffn_in", 1), NFF)
    w.add(("ffn_out", 1), NFF // 2)
    w.add("padding", -w.n % R)
    return w


def ticket_plan():
    n = Plan()
    n.add("bias")
    n.add("xT", KD)
    for l in range(DEPTH):
        n.add(("rms1", l))
        n.add(("proj", l), 9)
        n.add(("nat", l), 4)
        n.add(("hid", l), 4)
        n.add(("kc", l))
        n.add(("vc", l))
        for i in range(NU + 3):
            if i < NU:
                n.add(("S", l, i))
            if i < 24:
                n.add(("ada", l, i))
            if 0 <= i - 2 < NU:
                n.add(("PT", l, i - 2))
            if 0 <= i - 3 < NU and UNITS[i - 3]["first"]:
                n.add(("O", l, i - 3))
            elif 0 <= i - 3 < NU:
                n.at[("O", l, i - 3)] = n.at[("O", l, i - 4)]
        n.add(("dfn", l))
        n.add(("out", l), 8)
        n.add(("rms2", l))
        n.add(("up", l), 16)
        n.add(("down", l), 8)
    n.add("rmsf")
    n.add("m_up", 16)
    n.add("m_gates")
    n.add("m_aT")
    n.add("m_v", 16)
    for h in range(MH):
        n.add(("m_q", h), 2)
        n.add(("m_k", h), 2)
        n.add(("m_QK", h), 4)
        n.add(("m_max", h), 2)
        n.add(("m_og", h), 4)
        n.add(("m_den", h))
        n.add(("m_rec", h), 2)
        n.add(("m_PV", h), 4)
        n.add(("m_rms", h))
    n.add("m_out", 8)
    n.add(("mean", 0))
    n.add(("var", 0))
    n.add(("ffn_in", 0), 2 * NFF)
    n.add(("ffn_out", 0), 8)
    n.add(("mean", 1))
    n.add(("var", 1))
    n.add("a_ckv", 2)
    n.add("a_kr")
    n.add("a_cq", 2)
    n.add("a_kvn")
    n.add("a_qn")
    n.add("a_kn", AH)
    n.add("a_v", 8)
    n.add("a_qnope", 4)
    n.add("a_qrope", 4)
    for i in range(2 * AH + 4):
        if i < 2 * AH:
            n.add(("aS", i))
        if 0 <= i - 2 < 2 * AH:
            n.add(("aPT", i - 2))
        if i >= 4 and i % 2 == 0 and (i - 4) // 2 < AH:
            n.add(("aO", (i - 4) // 2))
    n.add("a_out", 8)
    n.add(("mean", 2))
    n.add(("var", 2))
    n.add(("ffn_in", 1), 2 * NFF)
    n.add(("ffn_out", 1), 8)
    n.add(("mean", 3))
    n.add(("var", 3))
    n.add("oT", 4)
    return n


W = slot_plan()
N = ticket_plan()


class Count:

    def __init__(self):
        self.n = {}

    def __call__(self, sem, more=1):
        self.n[id(sem)] = self.n.get(id(sem), 0) + more
        return self.n[id(sem)]


def build(nc, tokens, stream, params, consts, onehot, out, scratch):
    with ExitStack() as ctx:
        def sb(name, shape):
            return ctx.enter_context(nc.sbuf_tensor(name, shape, F32))

        def sem(name):
            return ctx.enter_context(nc.semaphore(name))

        bank = [ctx.enter_context(nc.psum_tensor(f"bank{i}", [P, 512], F32)) for i in range(BANKS)]
        ring = sb("ring", [P, R, SLOT])
        slot_full = [sem(f"slot_full{i}") for i in range(R)]
        slot_free = [sem(f"slot_free{i}") for i in range(R)]
        bank_full = [sem(f"bank_full{i}") for i in range(BANKS)]
        bank_free = [sem(f"bank_free{i}") for i in range(BANKS)]

        xT = sb("xT", [P, KD, T2])
        hT = sb("hT", [P, KD, T2])
        par = sb("par", [P, PAR.n])
        con = sb("con", [P, CON.n])
        eps = sb("eps", [P, 1])
        one = sb("one", [P, 1])
        stat = sb("stat", [P, 3, T2])
        A1 = 31840
        arena = sb("arena", [P, A1])

        def region(off, shape):
            n = int(np.prod(shape))
            ap = arena[:, off:off + n]
            if len(shape) == 2:
                ap = ap.rearrange("p (a b) -> p a b", a=shape[0])
            if len(shape) == 3:
                ap = ap.rearrange("p (a b c) -> p a b c", a=shape[0], b=shape[1])
            return ap

        def par_at(name, i=0, n=1):
            return par[:, PAR(name, i):PAR(name, i) + n]

        def con_at(name, n):
            return con[:, CON(name):CON(name) + n]

        ident = con_at("ident", 128)
        ones = con_at("ones", 128)
        halves = con_at("halves", 128)

        o = Plan()
        for name, n in (("qk", 16 * T), ("x2", 2 * T), ("x3", 512), ("vn", 6 * T), ("vsw", 280), ("mixed", KD * T),
                        ("act", 32 * T), ("bias", 12 * 384), ("cbias", 128), ("hid", 64), ("hidg", 64), ("lamp", 64), ("kc", 32), ("vc", 64),
                        ("s", 3 * 384), ("t", 4 * 384), ("pt", 2 * 384), ("st", 8 * NU), ("lam", 64),
                        ("relu", 2 * 512)):
            o.add(name, n)
        qk = region(o("qk"), (16, T))
        x2 = region(o("x2"), (2, T))
        x3 = region(o("x3"), (2, 16, 16))
        vn = region(o("vn"), (3, 2, T))
        vsw = region(o("vsw"), (2, 140))
        mixed = region(o("mixed"), (KD, T))
        act = region(o("act"), (32, T))
        bias = region(o("bias"), (12, 384))
        cbias = region(o("cbias"), (4, 32))
        hid = region(o("hid"), (4, 16))
        hidg = region(o("hidg"), (4, 16))
        lamp = region(o("lamp"), (64,))
        kcT = region(o("kc"), (16,))
        vc = region(o("vc"), (64,))
        sbuf = region(o("s"), (3, 384))
        tbuf = region(o("t"), (4, 384))
        ptb = region(o("pt"), (2, 384))
        st = region(o("st"), (NU, 8))
        lam = region(o("lam"), (64,))
        xnat = region(o("act") + 4096, (4, D))
        hankel = region(o("act") + 4096, (12, T))
        tz = region(o("mixed"), (4 * 353,)).rearrange("p (a b) -> p a b", a=4)
        relu = region(o("relu"), (2, 512))
        assert o.n <= A1, o.n

        mod = sb("mod", [P, DEPTH, 96])
        cs = sb("cs", [P, 16])
        o = Plan()
        for name, n in (("xm", MK * T2), ("xc", MK * T2), ("v", MK * T2), ("qk", 4 * T2), ("P", 6 * T2),
                        ("rows", 3 * T2), ("aT", 4 * 64)):
            o.add(name, n)
        assert o.n <= A1, o.n
        xm = region(o("xm"), (MK, T2))
        hs = xm
        xc = region(o("xc"), (MK, T2))
        mv = region(o("v"), (4, MH * T2))
        mqk = region(o("qk"), (4, T2))
        og = mqk
        mP = region(o("P"), (2, 3 * T2))
        grow = region(o("P"), (6, T2))
        rows = region(o("rows"), (3, T2))
        aT = region(o("aT"), (4, 64))
        sq2 = region(o("xc"), (KD, T2))
        ctmp = region(o("xm"), (4, T2))
        ffa = region(o("xc") + KD * T2, (NFF, T2))
        o = Plan()
        for name, n in (("ckv", 2 * T2), ("cq", 3 * T), ("kr", T2), ("rt", 2 * T), ("kn", AH * T2), ("v", 4 * D), ("qn", AH * T),
                        ("qr", AH * T), ("oT", AH * T), ("ap", 3 * T2), ("apt", 2 * 4 * T), ("ast", 16 * 4),
                        ("cks", 3 * T2), ("osb", 2 * D)):
            o.add(name, n)
        assert o.n <= A1, o.n
        ckv = region(o("ckv"), (2, T2))
        cq = region(o("cq"), (3, T))
        krope = region(o("kr"), (T2,))
        rt = region(o("rt"), (2, T))
        kn = region(o("kn"), (AH, T2))
        av = region(o("v"), (4, D))
        qn = region(o("qn"), (AH, T))
        qr = region(o("qr"), (AH, T))
        aoT = region(o("oT"), (AH, T))
        ap_ = region(o("ap"), (3, T2))
        apt = region(o("apt"), (2, 4, T))
        ast = region(o("ast"), (16, 4))
        cks = region(o("cks"), (3, T2))
        osb = region(o("osb"), (2, D))

        cs_ready = sem("condition_ready")
        mod_ready = sem("modulation_ready")
        conv_ready = sem("conv_ready")
        silu_ready = sem("silu_ready")
        lng_ready = sem("log_gate_terms_ready")
        rows_ready = sem("gate_rows_ready")
        floor_ready = sem("denominator_floor_ready")
        D_ready = sem("exponents_ready")
        E_ready = sem("decays_ready")
        rden_ready = sem("reciprocal_denominators_ready")
        W_ready = sem("mlstm_weights_ready")
        hs_ready = sem("mixer_output_ready")
        ln_ready = sem("layer_norm_ready")
        ckn_ready = sem("latents_normed")
        amax_ready = sem("max_ready")
        aexp_ready = sem("attention_exp_ready")
        ap_ready = sem("attention_weights_ready")
        dma_x, dma_con, dma_par, dma_oh = sem("dma_x"), sem("dma_con"), sem("dma_par"), sem("dma_onehot")
        dma_bv, dma_bias, dma_out = sem("dma_bias_vector"), sem("dma_bias"), sem("dma_out")
        dve_own, act_own = sem("dve_own"), sem("act_own")
        small_ready = sem("small_constants_ready")
        cbias_ready = sem("compressed_bias_ready")
        sq_ready = sem("squares_ready")
        rstd_ready = sem("rstd_ready")
        h_ready = sem("h_ready")
        x3_ready = sem("x3_ready")
        hid_ready = sem("hidden_ready")
        logits_ready = sem("logits_ready")
        exp_ready = sem("exp_ready")
        arg_ready = sem("log_weights_ready")
        sb_ready = sem("stick_weights_ready")
        p_ready = sem("softmax_weights_ready")
        dfn_ready = sem("diff_normed")
        act_ready = sem("activations_ready")
        gate_exp = sem("gate_exp_ready")
        lam_sum = sem("lambda_sums_ready")
        lam_exp = sem("lambda_exp_ready")
        out_copied = sem("out_copied")

        def ps(n, lo=0, hi=512):
            return bank[n % BANKS][:, lo:hi]

        block = ctx.enter_context(nc.Block())

        @block.sync
        def _(sp):
            sp.dma_start(con[:, :], consts).then_inc(dma_con, 16)
            sp.dma_start(par[:, :], params).then_inc(dma_par, 16)
            sp.dma_start(act.rearrange("p a b -> p (a b)")[0:33, 0:512], onehot).then_inc(dma_oh, 16)
            sp.dma_start(xnat, tokens.rearrange("(a p) d -> p a d", p=P)).then_inc(dma_x, 16)
            for i in range(R):
                sp.dma_start(ring[:, i, :], stream[i]).then_inc(slot_full[i], 16)
            sp.wait_ge(bank_free[N("bias") % BANKS], N("bias") // BANKS + 1)
            sp.dma_start(scratch, relu[0:12, 0, :]).then_inc(dma_bv, 16)
            sp.wait_ge(dma_bv, 16)
            for k in range(KD):
                sp.wait_ge(bank_free[N("xT", k) % BANKS], N("xT", k) // BANKS + 1)
            hnd = scratch.tensor
            sp.dma_start(hankel, bass.AP(tensor=hnd, offset=128, ap=[[1, P], [512, 12], [1, T]])).then_inc(dma_bias, 16)
            sp.dma_start(tz, bass.AP(tensor=hnd, offset=4 * 512, ap=[[1, P], [512, 4], [1, 353]])).then_inc(dma_bias, 16)
            with sp.Fori(1, W.n // R) as turn:
                for i in range(R):
                    sp.wait_ge(slot_free[i], turn)
                    sp.dma_start(ring[:, i, :], stream[turn * R + i]).then_inc(slot_full[i], 16)
            sp.wait_ge(out_copied, 1)
            sp.dma_start(out.rearrange("b (a p) d -> p (b a) d", p=P), osb).then_inc(dma_out, 16)
            sp.wait_ge(dma_out, 16)

        @block.tensor
        def _(pe):
            seen = Count()
            mm = nc.tensor.matmul

            def slot(w, kc):
                n = SLOT // kc
                return ring[:, w % R, 0:kc * n].rearrange("p (k n) -> p k n", k=kc)

            used = []

            def free(w):
                used.append(w)

            def feature_major(w, n, kc, pieces, rhs, cols):
                pe.wait_ge(slot_full[w % R], 16 * (w // R + 1))
                ws = slot(w, kc)
                per = 512 // cols
                for g in range(pieces):
                    if g % per == 0:
                        if n + g // per >= BANKS:
                            pe.wait_ge(bank_free[(n + g // per) % BANKS], (n + g // per) // BANKS)
                    for k in range(kc):
                        ins = mm(ps(n + g // per, (g % per) * cols, (g % per + 1) * cols),
                                 ws[:, k, g * P:(g + 1) * P], rhs(k), start=(k == 0), stop=(k == kc - 1))
                        if g == k == 0:
                            if used:
                                ins.then_inc(slot_free[used.pop() % R], 1)
                    if g == pieces - 1:
                        free(w)
                    if g % per == per - 1 or g == pieces - 1:
                        ins.then_inc(bank_full[(n + g // per) % BANKS], 1)

            def to_residual(w, n, slots, rhs, cols, kc=2):
                for s in range(slots):
                    pe.wait_ge(slot_full[(w + s) % R], 16 * ((w + s) // R + 1))
                    ws = slot(w + s, kc)
                    for g in range(KD):
                        if s == 0:
                            if n + g >= BANKS:
                                pe.wait_ge(bank_free[(n + g) % BANKS], (n + g) // BANKS)
                        for k in range(kc):
                            ins = mm(ps(n + g, 0, cols), ws[:, k, g * P:(g + 1) * P], rhs(s * kc + k),
                                     start=(s + k == 0), stop=(s == slots - 1 and k == kc - 1))
                            if g == k == 0:
                                if used:
                                    ins.then_inc(slot_free[used.pop() % R], 1)
                        if s == slots - 1:
                            ins.then_inc(bank_full[(n + g) % BANKS], 1)
                    free(w + s)

            def sum_squares(n, src, chunks, cols, stationary):
                pe.wait_ge(sq_ready, seen(sq_ready))
                if n >= BANKS:
                    pe.wait_ge(bank_free[n % BANKS], n // BANKS)
                for k in range(chunks):
                    ins = mm(ps(n, 0, cols), stationary, src(k), start=(k == 0), stop=(k == chunks - 1))
                ins.then_inc(bank_full[n % BANKS], 1)

            pe.wait_ge(dma_con, 16)
            pe.wait_ge(dma_par, 16)
            pe.wait_ge(dma_oh, 16)
            oh = act.rearrange("p a b -> p (a b)")[0:33, 0:512]
            n = N("bias")
            if n >= BANKS:
                pe.wait_ge(bank_free[n % BANKS], n // BANKS)
            mm(bank[n % BANKS][0:12, :], par[0:33, PAR("table"):PAR("table") + 12], oh, start=True, stop=True).then_inc(bank_full[n % BANKS], 1)
            pe.wait_ge(dma_x, 16)
            for k in range(KD):
                n = N("xT", k)
                if n >= BANKS:
                    pe.wait_ge(bank_free[n % BANKS], n // BANKS)
                for t in range(4):
                    ins = nc.tensor.transpose(ps(n, t * P, (t + 1) * P), xnat[:, t, k * P:(k + 1) * P], ident)
                ins.then_inc(bank_full[n % BANKS], 1)

            for l in range(DEPTH):
                sum_squares(N(("rms1", l)), lambda k: act[:, k, :], KD, T, ones)
                pe.wait_ge(h_ready, seen(h_ready))
                for g in range(9):
                    feature_major(W(("proj", l), g), N(("proj", l), g), KD, 2, lambda k: hT[:, k, LAT:], T)
                for g in range(4):
                    w, n = W(("nat", l), g), N(("nat", l), g)
                    pe.wait_ge(slot_full[w % R], 16 * (w // R + 1))
                    ws = slot(w, KD)
                    cols = 140 if g == 3 else T
                    if n >= BANKS:
                        pe.wait_ge(bank_free[n % BANKS], n // BANKS)
                    for t in range(2):
                        for k in range(KD):
                            ins = mm(ps(n, t * T, t * T + cols), hT[:, k, LAT + t * P:LAT + (t + 1) * P],
                                     ws[:, k, 0:cols], start=(k == 0), stop=(k == KD - 1))
                            if t == k == 0:
                                if used:
                                    ins.then_inc(slot_free[used.pop() % R], 1)
                    free(w)
                    ins.then_inc(bank_full[n % BANKS], 1)
                pe.wait_ge(x3_ready, seen(x3_ready))
                for i in range(4):
                    w, n = W(("cmp", l), i), N(("hid", l), i)
                    pe.wait_ge(slot_full[w % R], 16 * (w // R + 1))
                    ws = slot(w, 16)
                    if n >= BANKS:
                        pe.wait_ge(bank_free[n % BANKS], n // BANKS)
                    for j in range(16):
                        ins = mm(ps(n, 0, 16), ws[:, j, :], x3[:, i // 2, j, :], start=(j == 0), stop=(j == 15))
                        if j == 0:
                            if used:
                                ins.then_inc(slot_free[used.pop() % R], 1)
                    free(w)
                    ins.then_inc(bank_full[n % BANKS], 1)
                pe.wait_ge(hid_ready, seen(hid_ready, 4))
                n = N(("kc", l))
                if n >= BANKS:
                    pe.wait_ge(bank_free[n % BANKS], n // BANKS)
                for j in range(2):
                    ins = mm(ps(n, 0, 16), par[:, PAR(("w2k", l), 128 * j):PAR(("w2k", l), 128 * j) + 128], hidg[:, j, :],
                             start=(j == 0), stop=(j == 1))
                ins.then_inc(bank_full[n % BANKS], 1)
                n = N(("vc", l))
                if n >= BANKS:
                    pe.wait_ge(bank_free[n % BANKS], n // BANKS)
                for j in range(2):
                    ins = mm(bank[n % BANKS][0:16, 0:64], hidg[:, 2 + j, :],
                             par[:, PAR(("w2v", l), 64 * j):PAR(("w2v", l), 64 * j) + 64], start=(j == 0), stop=(j == 1))
                ins.then_inc(bank_full[n % BANKS], 1)
                for n in range(N(("proj", l)), N(("vc", l)) + 1):
                    pe.wait_ge(bank_free[n % BANKS], n // BANKS + 1)
                for i in range(NU + 3):
                    if i < NU:
                        u, n = UNITS[i], N(("S", l, i))
                        lo, hi = u["r"], u["r"] + u["kk"]
                        if n >= BANKS:
                            pe.wait_ge(bank_free[n % BANKS], n // BANKS)
                        if u["kind"] == "cmp":
                            mm(ps(n, 0, 16), qk[lo:hi, u["q"], 0:128], kcT[lo:hi, :], start=True, stop=True)
                            ins = mm(ps(n, 16, 32), qk[lo:hi, u["q"], 128:256], kcT[lo:hi, :], start=True, stop=True)
                        else:
                            ins = mm(ps(n, 0, 128), qk[lo:hi, u["q"], 0:128], qk[lo:hi, u["k"], 0:128], start=True, stop=True)
                            if used:
                                ins.then_inc(slot_free[used.pop() % R], 1)
                            ins = mm(ps(n, 128, 384), qk[lo:hi, u["q"], 128:256], qk[lo:hi, u["k"], :],
                                     start=True, stop=True)
                        ins.then_inc(bank_full[n % BANKS], 1)
                    if i < 24:
                        w, n = W(("ada", l), i), N(("ada", l, i))
                        if l == i == 0:
                            pe.wait_ge(cs_ready, seen(cs_ready))
                        pe.wait_ge(slot_full[w % R], 16 * (w // R + 1))
                        ws = slot(w, KD)
                        if n >= BANKS:
                            pe.wait_ge(bank_free[n % BANKS], n // BANKS)
                        for g in range(2):
                            for k in range(KD):
                                ins = mm(ps(n, 2 * g, 2 * g + 2), ws[:, k, g * P:(g + 1) * P], cs[:, 2 * k:2 * k + 2],
                                         start=(k == 0), stop=(k == KD - 1))
                                if g == k == 0:
                                    if used:
                                        ins.then_inc(slot_free[used.pop() % R], 1)
                        free(w)
                        ins.then_inc(bank_full[n % BANKS], 1)
                    if 0 <= i - 2 < NU:
                        j = i - 2
                        u, n = UNITS[j], N(("PT", l, j))
                        pe.wait_ge(sb_ready if u["kind"] == "sb" else p_ready, seen(sb_ready if u["kind"] == "sb" else p_ready))
                        if n >= BANKS:
                            pe.wait_ge(bank_free[n % BANKS], n // BANKS)
                        s = sbuf[:, j % 3, :]
                        if u["kind"] == "cmp":
                            for t in range(2):
                                ins = nc.tensor.transpose(bank[n % BANKS][0:16, t * P:(t + 1) * P],
                                                          s[:, 16 * t:16 * t + 16], ident)
                        else:
                            for t in range(3):
                                ins = nc.tensor.transpose(ps(n, t * P, (t + 1) * P), s[:, t * P:(t + 1) * P], ident)
                        ins.then_inc(bank_full[n % BANKS], 1)
                    if 0 <= i - 3 < NU:
                        j = i - 3
                        u, n = UNITS[j], N(("O", l, j))
                        if u["first"]:
                            if n >= BANKS:
                                pe.wait_ge(bank_free[n % BANKS], n // BANKS)
                        pe.wait_ge(bank_free[N(("PT", l, j)) % BANKS], N(("PT", l, j)) // BANKS + 1)
                        pt = ptb[:, j % 2, :]
                        ob = bank[n % BANKS][u["row"]:u["row"] + 64, :]
                        if u["kind"] == "cmp":
                            ins = mm(ob[:, 0:256], vc[0:16, :], pt[0:16, 0:256], start=u["first"], stop=u["last"])
                        else:
                            if u["v"][0] == "vn":
                                v = [vn[:, u["v"][1], t, 64 * u["h"]:64 * u["h"] + 64] for t in range(2)]
                            else:
                                v0 = 0 if u["kind"] == "slc" else 64
                                v = [vsw[:, t, v0:v0 + 64] for t in range(2)]
                            mm(ob[:, 0:256], v[0], pt[:, 0:256], start=u["first"], stop=False)
                            ins = mm(ob[:, 128:256], v[1], pt[:, 256:384], start=False, stop=u["last"])
                        if u["last"]:
                            ins.then_inc(bank_full[n % BANKS], 1)
                n = N(("dfn", l))
                pe.wait_ge(sq_ready, seen(sq_ready))
                if n >= BANKS:
                    pe.wait_ge(bank_free[n % BANKS], n // BANKS)
                mm(ps(n), halves, relu[:, 0, :], start=True, stop=True).then_inc(bank_full[n % BANKS], 1)
                pe.wait_ge(bank_free[N(("O", l, NU - 1)) % BANKS], N(("O", l, NU - 1)) // BANKS + 1)
                pe.wait_ge(dfn_ready, seen(dfn_ready))
                to_residual(W(("out", l)), N(("out", l)), 4, lambda k: mixed[:, k, :], T)
                sum_squares(N(("rms2", l)), lambda k: act[:, k, :], KD, T, ones)
                pe.wait_ge(h_ready, seen(h_ready))
                for g in range(16):
                    feature_major(W(("up", l), g), N(("up", l), g), KD, 2, lambda k: hT[:, k, LAT:], T)
                pe.wait_ge(act_ready, seen(act_ready, 16))
                to_residual(W(("down", l)), N(("down", l)), 16, lambda k: act[:, k, :], T)
            sum_squares(N("rmsf"), lambda k: act[:, k, :], KD, T, ones)

            pe.wait_ge(h_ready, seen(h_ready))
            pe.wait_ge(h_ready, seen(h_ready))
            for g in range(8):
                feature_major(W("m_up", g), N("m_up", 2 * g), KD, 2, lambda k: hT[:, k, :], T2)
            pe.wait_ge(silu_ready, seen(silu_ready, MK))
            feature_major(W("m_gates"), N("m_gates"), MK, 1, lambda k: xc[:, k, :], T2)
            pe.wait_ge(rows_ready, seen(rows_ready))
            n = N("m_aT")
            if n >= BANKS:
                pe.wait_ge(bank_free[n % BANKS], n // BANKS)
            for t in range(4):
                ins = nc.tensor.transpose(ps(n, 64 * t, 64 * t + 64), grow[0:64, 5, t * P:(t + 1) * P], ident[0:64, 0:64])
            ins.then_inc(bank_full[n % BANKS], 1)
            for h in range(MH):
                for s in range(4):
                    w = W("m_v", 4 * h + s)
                    pe.wait_ge(slot_full[w % R], 16 * (w // R + 1))
                    ws = slot(w, 4)
                    for t in range(4):
                        n = N("m_v", 4 * h + t)
                        if s == 0:
                            if n >= BANKS:
                                pe.wait_ge(bank_free[n % BANKS], n // BANKS)
                        for k in range(4):
                            ins = mm(ps(n), xm[:, 4 * s + k, t * P:(t + 1) * P], ws[:, k, :], start=(s + k == 0),
                                     stop=(s == 3 and k == 3))
                            if t == k == 0:
                                if used:
                                    ins.then_inc(slot_free[used.pop() % R], 1)
                        if s == 3:
                            ins.then_inc(bank_full[n % BANKS], 1)
                    free(w)
            pe.wait_ge(bank_free[N("m_aT") % BANKS], N("m_aT") // BANKS + 1)
            for h in range(MH):
                for j, name in enumerate(("m_q", "m_k")):
                    for s in range(2):
                        w = W(("m_qk", h), 2 * j + s)
                        pe.wait_ge(slot_full[w % R], 16 * (w // R + 1))
                        ws = slot(w, KD)
                        for g in range(2):
                            n = N((name, h), g)
                            if s == 0:
                                if n >= BANKS:
                                    pe.wait_ge(bank_free[n % BANKS], n // BANKS)
                            for k in range(KD):
                                ins = mm(ps(n), ws[:, k, g * P:(g + 1) * P], xc[:, KD * s + k, :], start=(s + k == 0),
                                         stop=(s == 1 and k == KD - 1))
                                if g == k == 0:
                                    if used:
                                        ins.then_inc(slot_free[used.pop() % R], 1)
                            if s == 1:
                                ins.then_inc(bank_full[n % BANKS], 1)
                        free(w)
                for n in range(N(("m_q", h)), N(("m_q", h)) + 4):
                    pe.wait_ge(bank_free[n % BANKS], n // BANKS + 1)
                for st_ in range(4):
                    n = N(("m_QK", h), st_)
                    if n >= BANKS:
                        pe.wait_ge(bank_free[n % BANKS], n // BANKS)
                    for c in range(2):
                        ins = mm(ps(n, 0, T2 - T_AT[st_]), mqk[:, 2 + c, st_ * P:(st_ + 1) * P], mqk[:, c, T_AT[st_]:],
                                 start=(c == 0), stop=(c == 1))
                    ins.then_inc(bank_full[n % BANKS], 1)
                for z in range(2):
                    n = N(("m_max", h), z)
                    if n >= BANKS:
                        pe.wait_ge(bank_free[n % BANKS], n // BANKS)
                    r = 32 * z + h
                    mm(ps(n), ident[0:64, r:r + 1].to_broadcast([64, P]), rows[0:64, 0, :], start=True, stop=True).then_inc(bank_full[n % BANKS], 1)
                for g in range(2):
                    feature_major(W(("m_og", h), g), N(("m_og", h), 2 * g), KD, 2, lambda k: hT[:, k, :], T2)
                pe.wait_ge(bank_free[N(("m_QK", h), 3) % BANKS], N(("m_QK", h), 3) // BANKS + 1)
                n = N(("m_den", h))
                if n >= BANKS:
                    pe.wait_ge(bank_free[n % BANKS], n // BANKS)
                for z in range(2):
                    r = 32 * z + h
                    for st_ in range(4):
                        ins = mm(bank[n % BANKS][0:64, T_AT[st_]:T2], con[:, CON("pick") + 63 - r:CON("pick") + 127 - r],
                                 mP[:, z, OFF[st_]:OFF[st_] + T2 - T_AT[st_]], start=(z + st_ == 0), stop=(z == 1 and st_ == 3))
                ins.then_inc(bank_full[n % BANKS], 1)
                pe.wait_ge(rden_ready, seen(rden_ready))
                for z in range(2):
                    n = N(("m_rec", h), z)
                    if n >= BANKS:
                        pe.wait_ge(bank_free[n % BANKS], n // BANKS)
                    r = 32 * z + h
                    mm(ps(n), ident[0:64, r:r + 1].to_broadcast([64, P]), rows[0:64, 2, :], start=True, stop=True).then_inc(bank_full[n % BANKS], 1)
                pe.wait_ge(W_ready, seen(W_ready))
                for e in range(4):
                    n = N(("m_PV", h), e)
                    if n >= BANKS:
                        pe.wait_ge(bank_free[n % BANKS], n // BANKS)
                    for st_ in range(4):
                        ins = mm(ps(n, T_AT[st_], T2), mv[:, st_, h * T2 + e * P:h * T2 + (e + 1) * P],
                                 mP[:, 0, OFF[st_]:OFF[st_] + T2 - T_AT[st_]], start=(st_ == 0), stop=(st_ == 3))
                    ins.then_inc(bank_full[n % BANKS], 1)
                sum_squares(N(("m_rms", h)), lambda k: mqk[:, k, :], 4, T2, ones)
            pe.wait_ge(hs_ready, seen(hs_ready, MH))
            to_residual(W("m_out"), N("m_out"), 8, lambda k: hs[:, k, :], T2)

            def layer_norm(i, lo, name):
                pe.wait_ge(bank_free[N(name, KD - 1) % BANKS], N(name, KD - 1) // BANKS + 1)
                n = N(("mean", i))
                if n >= BANKS:
                    pe.wait_ge(bank_free[n % BANKS], n // BANKS)
                for k in range(KD):
                    ins = mm(ps(n, 0, T2 - lo), ones, xT[:, k, lo:], start=(k == 0), stop=(k == KD - 1))
                ins.then_inc(bank_full[n % BANKS], 1)
                sum_squares(N(("var", i)), lambda k: sq2[:, k, lo:], KD, T2 - lo, ones)

            def ffn(l, lo):
                pe.wait_ge(h_ready, seen(h_ready))
                for j in range(NFF):
                    w, n = W(("ffn_in", l), j), N(("ffn_in", l), 2 * j)
                    pe.wait_ge(slot_full[w % R], 16 * (w // R + 1))
                    ws = slot(w, KD)
                    for g in range(2):
                        if n + g >= BANKS:
                            pe.wait_ge(bank_free[(n + g) % BANKS], (n + g) // BANKS)
                        for k in range(KD):
                            ins = mm(ps(n + g, 0, T2 - lo), ws[:, k, g * P:(g + 1) * P], hT[:, k, lo:], start=(k == 0),
                                     stop=(k == KD - 1))
                            if g == k == 0:
                                if used:
                                    ins.then_inc(slot_free[used.pop() % R], 1)
                        ins.then_inc(bank_full[(n + g) % BANKS], 1)
                    free(w)
                pe.wait_ge(bank_free[N(("ffn_in", l), 2 * NFF - 1) % BANKS], N(("ffn_in", l), 2 * NFF - 1) // BANKS + 1)
                to_residual(W(("ffn_out", l)), N(("ffn_out", l)), NFF // 2, lambda k: ffa[:, k, lo:], T2 - lo)

            layer_norm(0, 0, "m_out")
            ffn(0, 0)
            layer_norm(1, 0, ("ffn_out", 0))

            pe.wait_ge(h_ready, seen(h_ready))
            feature_major(W("a_dkv"), N("a_ckv"), KD, 2, lambda k: hT[:, k, :], T2)
            feature_major(W("a_dkv", 1), N("a_kr"), KD, 1, lambda k: hT[:, k, :], T2)
            feature_major(W("a_dq"), N("a_cq"), KD, 2, lambda k: hT[:, k, LAT:], T)
            feature_major(W("a_dq", 1), N("a_cq", 1), KD, 1, lambda k: hT[:, k, LAT:], T)
            sum_squares(N("a_kvn"), lambda k: cks[:, k, :], 2, T2, ones)
            sum_squares(N("a_qn"), lambda k: cks[:, k, 0:T], 3, T, ones)
            pe.wait_ge(ckn_ready, seen(ckn_ready))
            feature_major(W("a_ukv"), N("a_kn"), 2, AH, lambda k: ckv[:, k, :], T2)
            pe.wait_ge(slot_full[(W("a_ukv", 1)) % R], 16 * ((W("a_ukv", 1)) // R + 1))
            ws = slot(W("a_ukv", 1), 2)
            for t in range(4):
                for c in range(2):
                    n = N("a_v", 2 * t + c)
                    if n >= BANKS:
                        pe.wait_ge(bank_free[n % BANKS], n // BANKS)
                    for k in range(2):
                        ins = mm(ps(n), ckv[:, k, t * P:(t + 1) * P], ws[:, k, c * T2:(c + 1) * T2], start=(k == 0),
                                 stop=(k == 1))
                        if t == c == k == 0:
                            if used:
                                ins.then_inc(slot_free[used.pop() % R], 1)
                    ins.then_inc(bank_full[n % BANKS], 1)
            free(W("a_ukv", 1))
            pe.wait_ge(ckn_ready, seen(ckn_ready))
            for g in range(4):
                feature_major(W("a_uq", g), N("a_qnope", 2 * g), 3, 4, lambda k: cq[:, k, :], T)
            pe.wait_ge(bank_free[N("a_kr") % BANKS], N("a_kr") // BANKS + 1)
            for n in range(N("a_kn"), N(("aS", 0))):
                pe.wait_ge(bank_free[n % BANKS], n // BANKS + 1)
            for i in range(2 * AH + 4):
                if i < 2 * AH:
                    h, t = i // 2, i % 2
                    n = N(("aS", i))
                    if n >= BANKS:
                        pe.wait_ge(bank_free[n % BANKS], n // BANKS)
                    mm(ps(n), qn[:, h, t * P:(t + 1) * P], kn[:, h, :], start=True, stop=False)
                    mm(ps(n), qr[0:64, h, t * P:(t + 1) * P], krope[0:64, :], start=False, stop=True).then_inc(bank_full[n % BANKS], 1)
                if 0 <= i - 2 < 2 * AH:
                    j = i - 2
                    n = N(("aPT", j))
                    pe.wait_ge(ap_ready, seen(ap_ready))
                    if n >= BANKS:
                        pe.wait_ge(bank_free[n % BANKS], n // BANKS)
                    for t in range(4):
                        ins = nc.tensor.transpose(ps(n, t * P, (t + 1) * P), ap_[:, j % 3, t * P:(t + 1) * P], ident)
                    ins.then_inc(bank_full[n % BANKS], 1)
                if i >= 4 and i % 2 == 0 and (i - 4) // 2 < AH:
                    h = (i - 4) // 2
                    n = N(("aO", h))
                    if n >= BANKS:
                        pe.wait_ge(bank_free[n % BANKS], n // BANKS)
                    pe.wait_ge(bank_free[N(("aPT", 2 * h)) % BANKS], N(("aPT", 2 * h)) // BANKS + 1)
                    pe.wait_ge(bank_free[N(("aPT", 2 * h + 1)) % BANKS], N(("aPT", 2 * h + 1)) // BANKS + 1)
                    for t in range(4):
                        ins = mm(ps(n, 0, T), av[:, t, h * P:(h + 1) * P], apt[:, h % 2, t, :], start=(t == 0), stop=(t == 3))
                    ins.then_inc(bank_full[n % BANKS], 1)
            for h in range(AH):
                pe.wait_ge(bank_free[N(("aO", h)) % BANKS], N(("aO", h)) // BANKS + 1)
            to_residual(W("a_out"), N("a_out"), 4, lambda k: aoT[:, k, :], T)
            layer_norm(2, LAT, "a_out")
            ffn(1, LAT)
            layer_norm(3, LAT, ("ffn_out", 1))
            pe.wait_ge(ln_ready, seen(ln_ready, 4))
            for t in range(2):
                for c in range(2):
                    n = N("oT", 2 * t + c)
                    if n >= BANKS:
                        pe.wait_ge(bank_free[n % BANKS], n // BANKS)
                    for k in range(4):
                        ins = nc.tensor.transpose(ps(n, k * P, (k + 1) * P), xT[:, 4 * c + k, LAT + t * P:LAT + (t + 1) * P],
                                                  ident)
                    ins.then_inc(bank_full[n % BANKS], 1)

        @block.scalar
        def _(act_):
            seen = Count()
            own = Count()
            do = nc.scalar.activation
            act_.wait_ge(small_ready, 2)
            act_.wait_ge(dma_par, 16)

            def squares(dst, src):
                do(dst, src, ACT.Square).then_inc(sq_ready, 1)

            def rstd(n, cols, count):
                act_.wait_ge(bank_full[n % BANKS], n // BANKS + 1)
                do(stat[:, 1, 0:cols], ps(n, 0, cols), ACT.Ln, bias=eps[:, :], scale=1.0 / count).then_inc(bank_free[n % BANKS], 1)
                act_.wait_ge(bank_free[n % BANKS], n // BANKS + 1)
                do(stat[:, 0, 0:cols], stat[:, 1, 0:cols], ACT.Exp, scale=-0.5).then_inc(rstd_ready, 1)

            act_.wait_ge(bank_full[N("bias") % BANKS], N("bias") // BANKS + 1)
            do(relu[0:12, 0, :], bank[N("bias") % BANKS][0:12, :], ACT.Copy).then_inc(bank_free[N("bias") % BANKS], 1)
            for k in range(KD):
                act_.wait_ge(bank_full[N("xT", k) % BANKS], N("xT", k) // BANKS + 1)
                do(xT[:, k, :], ps(N("xT", k)), ACT.Copy).then_inc(bank_free[N("xT", k) % BANKS], 1)
            act_.wait_ge(bank_free[N("xT", KD - 1) % BANKS], N("xT", KD - 1) // BANKS + 1)
            do(cs[:, :], par_at("cond", 0, 16), ACT.Silu).then_inc(cs_ready, 1)
            for l in range(DEPTH):
                if l:
                    act_.wait_ge(bank_free[N(("down", l - 1), KD - 1) % BANKS], N(("down", l - 1), KD - 1) // BANKS + 1)
                squares(act[:, 0:KD, :], xT[:, :, LAT:])
                rstd(N(("rms1", l)), T, D)
                act_.wait_ge(lam_sum, seen(lam_sum))
                do(lam[:, 2:4], lam[:, 0:2], ACT.Exp).then_inc(lam_exp, 1)
                for g in range(8):
                    n = N(("proj", l), g)
                    act_.wait_ge(bank_full[n % BANKS], n // BANKS + 1)
                    do(qk[:, 2 * g:2 * g + 2, :].rearrange("p a b -> p (a b)"), ps(n), ACT.Copy).then_inc(bank_free[n % BANKS], 1)
                n = N(("proj", l), 8)
                act_.wait_ge(bank_full[n % BANKS], n // BANKS + 1)
                do(x2[0:64].rearrange("p a b -> p (a b)"), bank[n % BANKS][0:64, :], ACT.Copy)
                pv = bank[n % BANKS][64:128, :].rearrange("p (a b) -> p a b", a=2)
                do(x2[64:128, :, 0:255], pv[:, :, 1:256], ACT.Copy).then_inc(bank_free[n % BANKS], 1)
                for g in range(4):
                    n = N(("nat", l), g)
                    act_.wait_ge(bank_full[n % BANKS], n // BANKS + 1)
                    pv = ps(n).rearrange("p (a b) -> p a b", a=2)
                    (do(vn[:, g, :, :], pv, ACT.Copy) if g < 3 else do(vsw, pv[:, :, 0:140], ACT.Copy)).then_inc(bank_free[n % BANKS], 1)
                act_.wait_ge(bank_free[N(("nat", l), 3) % BANKS], N(("nat", l), 3) // BANKS + 1)
                do(lam[:, 16:40].rearrange("p (a b) -> p a b", a=2), vsw[:, :, 128:140], ACT.Exp, scale=-1.0
                   ).then_inc(gate_exp, 1)
                for i in range(4):
                    n = N(("hid", l), i)
                    act_.wait_ge(bank_full[n % BANKS], n // BANKS + 1)
                    do(hid[:, i, :], ps(n, 0, 16), ACT.Copy).then_inc(bank_free[n % BANKS], 1)
                for i in range(4):
                    act_.wait_ge(bank_free[N(("hid", l), i) % BANKS], N(("hid", l), i) // BANKS + 1)
                    do(hidg[:, i, :], hid[:, i, :], ACT.Gelu_apprx_tanh, bias=hid[:, i, 15:16]).then_inc(hid_ready, 1)
                n = N(("kc", l))
                act_.wait_ge(bank_full[n % BANKS], n // BANKS + 1)
                do(kcT, ps(n, 0, 16), ACT.Copy).then_inc(bank_free[n % BANKS], 1)
                n = N(("vc", l))
                act_.wait_ge(bank_full[n % BANKS], n // BANKS + 1)
                do(vc[0:16, :], bank[n % BANKS][0:16, 0:64], ACT.Copy).then_inc(bank_free[n % BANKS], 1)
                for i in range(NU + 3):
                    if i < NU:
                        u, s, t = UNITS[i], sbuf[:, i % 3, :], tbuf[:, i % 2, :]
                        act_.wait_ge(logits_ready, seen(logits_ready))
                        if u["kind"] == "sb":
                            do(t, s, ACT.Abs).then_inc(act_own, 1)
                            act_.wait_ge(act_own, own(act_own))
                            do(t, t, ACT.Exp, scale=-1.0).then_inc(act_own, 1)
                            act_.wait_ge(act_own, own(act_own))
                            do(t, t, ACT.Ln, bias=one[:, :]).then_inc(exp_ready, 1)
                        elif u["kind"] == "cmp":
                            do(s[:, 0:16], s[:, 0:16], ACT.Exp, bias=st[:, i, 0:1])
                            do(s[:, 16:32], s[:, 16:32], ACT.Exp, bias=st[:, i, 1:2]).then_inc(exp_ready, 1)
                        else:
                            do(s[:, 0:128], s[:, 0:128], ACT.Exp, bias=st[:, i, 0:1], accum_out=st[:, i, 2:3])
                            do(s[:, 128:384], s[:, 128:384], ACT.Exp, bias=st[:, i, 1:2],
                               accum_out=st[:, i, 3:4]).then_inc(exp_ready, 1)
                    if 0 <= i - 1 < NU and UNITS[i - 1]["kind"] == "sb":
                        s = sbuf[:, (i - 1) % 3, :]
                        act_.wait_ge(arg_ready, seen(arg_ready))
                        do(s, s, ACT.Exp).then_inc(sb_ready, 1)
                    if 0 <= i - 2 < NU:
                        j = i - 2
                        n = N(("PT", l, j))
                        act_.wait_ge(bank_full[n % BANKS], n // BANKS + 1)
                        if UNITS[j]["kind"] == "cmp":
                            do(ptb[0:16, j % 2, 0:256], bank[n % BANKS][0:16, 0:256], ACT.Copy).then_inc(bank_free[n % BANKS], 1)
                        else:
                            do(ptb[:, j % 2, :], ps(n, 0, 384), ACT.Copy).then_inc(bank_free[n % BANKS], 1)
                    if 0 <= i - 3 < NU and UNITS[i - 3]["last"]:
                        u, n = UNITS[i - 3], N(("O", l, i - 3))
                        act_.wait_ge(bank_full[n % BANKS], n // BANKS + 1)
                        half = slice(u["row"], u["row"] + 64)
                        do(mixed[half, u["chunk"], :], bank[n % BANKS][half, 0:T], ACT.Copy).then_inc(bank_free[n % BANKS], 1)
                act_.wait_ge(bank_free[N(("O", l, NU - 1)) % BANKS], N(("O", l, NU - 1)) // BANKS + 1)
                squares(relu[:, 0, :].rearrange("p (a b) -> p a b", a=2), mixed[:, 6:8, :])
                rstd(N(("dfn", l)), 512, HD)
                act_.wait_ge(bank_free[N(("out", l), KD - 1) % BANKS], N(("out", l), KD - 1) // BANKS + 1)
                squares(act[:, 0:KD, :], xT[:, :, LAT:])
                rstd(N(("rms2", l)), T, D)
                for g in range(16):
                    n = N(("up", l), g)
                    act_.wait_ge(bank_full[n % BANKS], n // BANKS + 1)
                    if g >= 2:
                        act_.wait_ge(act_ready, seen(act_ready))
                    do(relu[:, g % 2, :], ps(n), ACT.Relu).then_inc(bank_free[n % BANKS], 1)
                act_.wait_ge(act_ready, seen(act_ready, 2))
            act_.wait_ge(bank_free[N(("down", DEPTH - 1), KD - 1) % BANKS], N(("down", DEPTH - 1), KD - 1) // BANKS + 1)
            squares(act[:, 0:KD, :], xT[:, :, LAT:])
            rstd(N("rmsf"), T, D)

            for j in range(MK):
                n = N("m_up", j)
                act_.wait_ge(bank_full[n % BANKS], n // BANKS + 1)
                do(xm[:, j, :], ps(n), ACT.Copy).then_inc(bank_free[n % BANKS], 1)
                if j:
                    act_.wait_ge(conv_ready, seen(conv_ready))
                    do(xc[:, j - 1, :], mqk[:, (j - 1) % 4, :], ACT.Silu).then_inc(silu_ready, 1)
            act_.wait_ge(conv_ready, seen(conv_ready))
            do(xc[:, MK - 1, :], mqk[:, (MK - 1) % 4, :], ACT.Silu).then_inc(silu_ready, 1)
            n = N("m_gates")
            act_.wait_ge(bank_full[n % BANKS], n // BANKS + 1)
            do(grow[:, 0, :], ps(n), ACT.Identity, bias=par_at("b_gates")).then_inc(bank_free[n % BANKS], 1)
            act_.wait_ge(bank_free[n % BANKS], n // BANKS + 1)
            do(grow[64:128, 1, :], grow[64:128, 0, :], ACT.Abs).then_inc(act_own, 1)
            act_.wait_ge(act_own, own(act_own))
            do(grow[64:128, 1, :], grow[64:128, 1, :], ACT.Exp, scale=-1.0).then_inc(act_own, 1)
            act_.wait_ge(act_own, own(act_own))
            do(grow[64:128, 1, :], grow[64:128, 1, :], ACT.Ln, bias=one[64:128, :]).then_inc(lng_ready, 1)
            act_.wait_ge(rows_ready, seen(rows_ready))
            do(rows[0:64, 1, :], rows[0:64, 1, :], ACT.Exp, scale=-1.0).then_inc(floor_ready, 1)
            n = N("m_aT")
            act_.wait_ge(bank_full[n % BANKS], n // BANKS + 1)
            do(aT.rearrange("p a b -> p (a b)"), ps(n, 0, 256), ACT.Copy).then_inc(bank_free[n % BANKS], 1)
            for h in range(MH):
                for t in range(4):
                    n = N("m_v", 4 * h + t)
                    act_.wait_ge(bank_full[n % BANKS], n // BANKS + 1)
                    do(mv[:, t, h * T2:(h + 1) * T2], ps(n), ACT.Copy).then_inc(bank_free[n % BANKS], 1)
            for h in range(MH):
                for j in range(4):
                    n = N(("m_q", h), j)
                    act_.wait_ge(bank_full[n % BANKS], n // BANKS + 1)
                    (do(mqk[:, j, :], ps(n), ACT.Copy, scale=1.0 if j < 2 else 1.0 / 16)).then_inc(bank_free[n % BANKS], 1)
                for z, spans in enumerate((((0, 512), (640, 1280), (1408, 1536)), ((0, 128), (256, 1152), (1280, 1536)))):
                    act_.wait_ge(D_ready, seen(D_ready))
                    for lo, hi in spans:
                        ins = do(mP[:, z, lo:hi], mP[:, z, lo:hi], ACT.Exp, scale=-1.0)
                    ins.then_inc(E_ready, 1)
                for j in range(4):
                    n = N(("m_og", h), j)
                    act_.wait_ge(bank_full[n % BANKS], n // BANKS + 1)
                    do(og[:, j, :], ps(n), ACT.Sigmoid).then_inc(bank_free[n % BANKS], 1)
                act_.wait_ge(bank_free[N(("m_PV", h), 3) % BANKS], N(("m_PV", h), 3) // BANKS + 1)
                do(mqk.rearrange("p a b -> p (a b)"), hs[:, 4 * h:4 * h + 4, :].rearrange("p a b -> p (a b)"), ACT.Square
                   ).then_inc(sq_ready, 1)
                rstd(N(("m_rms", h)), T2, T2)

            def layer_norm(i, lo):
                act_.wait_ge(bank_free[N(("mean", i)) % BANKS], N(("mean", i)) // BANKS + 1)
                do(sq2[:, :, lo:], xT[:, :, lo:], ACT.Square).then_inc(sq_ready, 1)
                rstd(N(("var", i)), T2 - lo, D)

            def ffn(l, lo):
                for j in range(NFF):
                    act_.wait_ge(conv_ready, seen(conv_ready))
                    c = ctmp[:, j % 4, lo:]
                    do(c, c, ACT.Silu).then_inc(bank_free[N(("ffn_in", l), 2 * j) % BANKS], 1)

            layer_norm(0, 0)
            ffn(0, 0)
            layer_norm(1, 0)

            for j in range(2):
                n = N("a_ckv", j)
                act_.wait_ge(bank_full[n % BANKS], n // BANKS + 1)
                do(ckv[:, j, :], ps(n), ACT.Copy).then_inc(bank_free[n % BANKS], 1)
            n = N("a_cq")
            act_.wait_ge(bank_full[n % BANKS], n // BANKS + 1)
            do(cq[:, 0:2, :].rearrange("p a b -> p (a b)"), ps(n), ACT.Copy).then_inc(bank_free[n % BANKS], 1)
            n = N("a_cq", 1)
            act_.wait_ge(bank_full[n % BANKS], n // BANKS + 1)
            do(cq[:, 2, :], ps(n, 0, T), ACT.Copy).then_inc(bank_free[n % BANKS], 1)
            act_.wait_ge(bank_free[n % BANKS], n // BANKS + 1)
            do(cks[:, 0:2, :], ckv, ACT.Square).then_inc(sq_ready, 1)
            rstd(N("a_kvn"), T2, T2 // 2)
            do(cks[:, :, 0:T], cq, ACT.Square).then_inc(sq_ready, 1)
            act_.wait_ge(ckn_ready, seen(ckn_ready))
            rstd(N("a_qn"), T, 384)
            for h in range(AH):
                n = N("a_kn", h)
                act_.wait_ge(bank_full[n % BANKS], n // BANKS + 1)
                do(kn[:, h, :], ps(n), ACT.Copy).then_inc(bank_free[n % BANKS], 1)
            for t in range(4):
                for c in range(2):
                    n = N("a_v", 2 * t + c)
                    act_.wait_ge(bank_full[n % BANKS], n // BANKS + 1)
                    do(av[:, t, c * T2:(c + 1) * T2], ps(n), ACT.Copy).then_inc(bank_free[n % BANKS], 1)
            for g in range(4):
                n = N("a_qnope", g)
                act_.wait_ge(bank_full[n % BANKS], n // BANKS + 1)
                do(qn[:, 2 * g:2 * g + 2, :].rearrange("p a b -> p (a b)"), ps(n), ACT.Copy).then_inc(bank_free[n % BANKS], 1)
            for i in range(2 * AH + 4):
                if i < 2 * AH:
                    n = N(("aS", i))
                    act_.wait_ge(amax_ready, seen(amax_ready))
                    do(ap_[:, i % 3, :], ps(n), ACT.Exp, bias=ast[:, i, 1:2], scale=A_SCALE,
                               accum_out=ast[:, i, 2:3]).then_inc(bank_free[n % BANKS], 1)
                if 0 <= i - 2 < 2 * AH:
                    j = i - 2
                    n = N(("aPT", j))
                    act_.wait_ge(bank_full[n % BANKS], n // BANKS + 1)
                    do(apt[:, (j // 2) % 2, :, (j % 2) * P:(j % 2 + 1) * P], ps(n).rearrange("p (a b) -> p a b", a=4),
                               ACT.Copy).then_inc(bank_free[n % BANKS], 1)
                if i >= 4 and i % 2 == 0 and (i - 4) // 2 < AH:
                    h = (i - 4) // 2
                    n = N(("aO", h))
                    act_.wait_ge(bank_full[n % BANKS], n // BANKS + 1)
                    do(aoT[:, h, :], ps(n, 0, T), ACT.Copy).then_inc(bank_free[n % BANKS], 1)
            layer_norm(2, LAT)
            ffn(1, LAT)
            layer_norm(3, LAT)
            for t in range(2):
                for c in range(2):
                    n = N("oT", 2 * t + c)
                    act_.wait_ge(bank_full[n % BANKS], n // BANKS + 1)
                    ins = do(osb[:, t, c * T2:(c + 1) * T2], ps(n), ACT.Copy)
            ins.then_inc(out_copied, 1)

        @block.vector
        def _(dve):
            seen = Count()
            own = Count()
            v = nc.vector
            stt = v.scalar_tensor_tensor

            def normed(dst, gain, chunks, cols=LAT):
                dve.wait_ge(rstd_ready, seen(rstd_ready))
                for k in range(chunks):
                    ins = stt(dst(k), xT[:, k, cols:], par_at(gain, k), stat[:, 0, 0:T2 - cols], ALU.mult, ALU.mult)
                ins.then_inc(h_ready, 1)
                dve.wait_ge(h_ready, own(h_ready))

            v.memset(eps[:, :], EPS).then_inc(small_ready, 1)
            v.memset(one[:, :], 1.0).then_inc(small_ready, 1)
            v.memset(cbias, NEG).then_inc(dve_own, 1)
            dve.wait_ge(dve_own, own(dve_own))
            dve.wait_ge(dma_par, 16)
            dve.wait_ge(dma_con, 16)
            for l in range(DEPTH):
                lam_init = 0.8 - 0.6 * math.exp(-0.3 * l)
                dl = par_at(("dlam", l), 0, 128).rearrange("p (a b c) -> p a b c", a=2, b=2)
                prod = lamp.rearrange("p (a c) -> p a c", a=2)
                v.tensor_tensor(prod, dl[:, :, 0, :], dl[:, :, 1, :], ALU.mult).then_inc(dve_own, 1)
                dve.wait_ge(dve_own, own(dve_own))
                v.tensor_reduce(lam[:, 0:2], prod, AX, ALU.add).then_inc(lam_sum, 1)
                normed(lambda k: hT[:, k, LAT:], ("g_attn", l), KD)
                dve.wait_ge(lam_exp, seen(lam_exp))
                v.tensor_tensor(lam[:, 4:5], lam[:, 3:4], lam[:, 2:3], ALU.subtract).then_inc(dve_own, 1)
                dve.wait_ge(dve_own, own(dve_own))
                v.tensor_scalar(lam[:, 5:6], lam[:, 4:5], -lam_init, None, ALU.add).then_inc(dve_own, 1)
                dve.wait_ge(dve_own, own(dve_own))
                v.tensor_scalar(lam[:, 6:7], par_at(("subln", l)), 1.0 - lam_init, None, ALU.mult).then_inc(dve_own, 1)
                dve.wait_ge(dve_own, own(dve_own))
                dve.wait_ge(bank_free[N(("proj", l), 8) % BANKS], N(("proj", l), 8) // BANKS + 1)
                for b in range(2):
                    xv = x2[:, b, :].rearrange("p (c j e) -> p e j c", j=8, e=2)
                    v.tensor_copy(x3[:, b, 0:8, 0:CMP_N], xv[:, 0, :, 0:15])
                    v.tensor_copy(x3[:, b, 8:16, 0:CMP_N], xv[:, 0, :, 1:16])
                    ins = v.tensor_copy(x3[:, b, :, 15], par_at(("pos", l), 16 * b, 16))
                ins.then_inc(x3_ready, 1)
                dve.wait_ge(gate_exp, seen(gate_exp))
                v.tensor_scalar(lam[:, 16:40], lam[:, 16:40], 1.0, None, ALU.add).then_inc(dve_own, 1)
                dve.wait_ge(dve_own, own(dve_own))
                v.reciprocal(lam[:, 16:40], lam[:, 16:40]).then_inc(dve_own, 1)
                dve.wait_ge(dve_own, own(dve_own))
                gates = lam[:, 16:40].rearrange("p (a b) -> p a b", a=2)
                if l == 0:
                    dve.wait_ge(dma_bias, 32)
                    v.tensor_copy(bias[:, :, 0:128], hankel[:, :, 0:128][:, :, ::-1])
                    v.tensor_copy(bias[:, :, 128:384], hankel[:, :, ::-1])
                    for q in range(2):
                        ins = v.tensor_copy(cbias[:, :, 16 * q:16 * q + CMP_N], tz[:, :, P * q:P * q + 225:16][:, :, ::-1])
                    ins.then_inc(dve_own, 1)
                    dve.wait_ge(dve_own, own(dve_own))
                for i in range(NU + 1):
                    if i < NU:
                        u, s, n = UNITS[i], sbuf[:, i % 3, :], N(("S", l, i))
                    if 1 <= i < 25:
                        n = N(("ada", l, i - 1))
                        dve.wait_ge(bank_full[n % BANKS], n // BANKS + 1)
                        for g in range(2):
                            piece = 2 * (i - 1) + g
                            plus = 1.0 if 8 <= piece < 16 or 32 <= piece < 40 else 0.0
                            ins = v.tensor_scalar(mod[:, l, 2 * piece:2 * piece + 2], ps(n, 2 * g, 2 * g + 2),
                                                  par_at(("ada_b", l), piece), plus, ALU.add, ALU.add)
                        ins.then_inc(bank_free[n % BANKS], 1)
                    if i < NU:
                        n = N(("S", l, i))
                        scale = u["kk"] ** -0.5
                        dve.wait_ge(bank_full[n % BANKS], n // BANKS + 1)
                        if u["kind"] == "sb":
                            stt(s, ps(n, 0, 384), scale, con_at("strict", 384), ALU.mult, ALU.add).then_inc(bank_free[n % BANKS], 1)
                            dve.wait_ge(bank_free[n % BANKS], n // BANKS + 1)
                            v.tensor_scalar(tbuf[:, 2 + i % 2, :], s, 0.0, None, ALU.max).then_inc(logits_ready, 1)
                        elif u["kind"] == "cmp":
                            stt(s[:, 0:32], ps(n, 0, 32), scale, cbias[:, u["h"], :], ALU.mult, ALU.add).then_inc(bank_free[n % BANKS], 1)
                            dve.wait_ge(bank_free[n % BANKS], n // BANKS + 1)
                            v.tensor_reduce(st[:, i, 0:2], s[:, 0:32].rearrange("p (a b) -> p a b", a=2), AX, ALU.max,
                                            negate=True).then_inc(logits_ready, 1)
                        else:
                            stt(s, ps(n, 0, 384), scale, bias[:, u["bias"], :], ALU.mult, ALU.add).then_inc(bank_free[n % BANKS], 1)
                            dve.wait_ge(bank_free[n % BANKS], n // BANKS + 1)
                            v.tensor_reduce(st[:, i, 0:1], s[:, 0:128], AX, ALU.max, negate=True)
                            v.tensor_reduce(st[:, i, 1:2], s[:, 128:384], AX, ALU.max, negate=True
                                            ).then_inc(logits_ready, 1)
                    if i >= 1:
                        j = i - 1
                        u, s = UNITS[j], sbuf[:, j % 3, :]
                        dve.wait_ge(exp_ready, seen(exp_ready))
                        if u["kind"] == "sb":
                            t, m = tbuf[:, j % 2, :], tbuf[:, 2 + j % 2, :]
                            for lo, hi in ((0, 128), (128, 384)):
                                ins = v.tensor_tensor_scan(t[:, lo:hi][:, ::-1], m[:, lo:hi][:, ::-1],
                                                           t[:, lo:hi][:, ::-1], 0.0, ALU.add, ALU.add)
                            ins.then_inc(dve_own, 1)
                            dve.wait_ge(dve_own, own(dve_own))
                            v.tensor_tensor(s, s, t, ALU.subtract).then_inc(arg_ready, 1)
                            continue
                        w = 128
                        if u["kind"] == "cmp":
                            w = 16
                            v.tensor_tensor(s[:, 0:32], s[:, 0:32], con_at("cmask", 32), ALU.mult).then_inc(dve_own, 1)
                            dve.wait_ge(dve_own, own(dve_own))
                            v.tensor_reduce(st[:, j, 2:4], s[:, 0:32].rearrange("p (a b) -> p a b", a=2), AX,
                                                     ALU.add).then_inc(dve_own, 1)
                            dve.wait_ge(dve_own, own(dve_own))
                            v.tensor_scalar(st[:, j, 2:4], st[:, j, 2:4], 1e-30, None, ALU.max).then_inc(dve_own, 1)
                            dve.wait_ge(dve_own, own(dve_own))
                        v.reciprocal(st[:, j, 4:6], st[:, j, 2:4]).then_inc(dve_own, 1)
                        dve.wait_ge(dve_own, own(dve_own))
                        if "gate" in u:
                            v.tensor_tensor(st[:, j, 4:6], st[:, j, 4:6], gates[:, :, u["gate"]], ALU.mult).then_inc(dve_own, 1)
                            dve.wait_ge(dve_own, own(dve_own))
                        if u.get("c"):
                            v.tensor_scalar(st[:, j, 4:6], st[:, j, 4:6], lam[:, 5:6], None, ALU.mult).then_inc(dve_own, 1)
                            dve.wait_ge(dve_own, own(dve_own))
                        end = 32 if u["kind"] == "cmp" else 384
                        v.tensor_scalar(s[:, 0:w], s[:, 0:w], st[:, j, 4:5], None, ALU.mult)
                        v.tensor_scalar(s[:, w:end], s[:, w:end], st[:, j, 5:6], None, ALU.mult).then_inc(p_ready, 1)
                dve.wait_ge(rstd_ready, seen(rstd_ready))
                m = mixed[:, 6:8, :]
                stt(m, m, lam[:, 6:7], stat[:, 0, :].rearrange("p (a b) -> p a b", a=2), ALU.mult, ALU.mult
                    ).then_inc(dfn_ready, 1)

                def residual(name):
                    for g in range(KD):
                        n = N((name, l), g)
                        dve.wait_ge(bank_full[n % BANKS], n // BANKS + 1)
                        v.tensor_tensor(xT[:, g, LAT:], xT[:, g, LAT:], ps(n, 0, T), ALU.add).then_inc(bank_free[n % BANKS], 1)

                residual("out")
                normed(lambda k: hT[:, k, LAT:], ("g_mlp", l), KD)
                for g in range(16):
                    dve.wait_ge(bank_free[N(("up", l), g) % BANKS], N(("up", l), g) // BANKS + 1)
                    v.tensor_tensor(act[:, 2 * g:2 * g + 2, :].rearrange("p a b -> p (a b)"), relu[:, g % 2, :],
                                    relu[:, g % 2, :], ALU.mult).then_inc(act_ready, 1)
                residual("down")
            normed(lambda k: xT[:, k, LAT:], "g_final", KD)

            def mod_at(l, part, k, seg):
                c = 2 * (KD * part + k) + 1 - seg
                return mod[:, l, c:c + 1]

            def modulate(l, part, segs=(0, 1)):
                for k in range(KD):
                    for seg in segs:
                        t = slice(seg * T, seg * T + T)
                        ins = v.tensor_scalar(hT[:, k, t], xT[:, k, t], mod_at(l, part + 1, k, seg), mod_at(l, part, k, seg),
                                              ALU.mult, ALU.add)
                ins.then_inc(h_ready, 1)
                dve.wait_ge(h_ready, own(h_ready))
                for k in range(KD):
                    ins = v.tensor_scalar(xT[:, k, segs[0] * T:], xT[:, k, segs[0] * T:], ALPHA, None, ALU.mult)
                ins.then_inc(dve_own, 1)
                dve.wait_ge(dve_own, own(dve_own))

            def conv(dst, src, w, b, segs, lo=0):
                v.tensor_scalar(dst, src, w[:, 1:2], b, ALU.mult, ALU.add).then_inc(dve_own, 1)
                dve.wait_ge(dve_own, own(dve_own))
                d3, s3 = (a.rearrange("p (a b) -> p a b", a=segs) for a in (dst, src))
                stt(d3[:, :, 1:T], s3[:, :, 0:T - 1], w[:, 0:1], d3[:, :, 1:T], ALU.mult, ALU.add).then_inc(dve_own, 1)
                dve.wait_ge(dve_own, own(dve_own))
                return stt(d3[:, :, 0:T - 1], s3[:, :, 1:T], w[:, 2:3], d3[:, :, 0:T - 1], ALU.mult, ALU.add)

            modulate(0, 0)
            for j in range(MK):
                dve.wait_ge(bank_free[N("m_up", j) % BANKS], N("m_up", j) // BANKS + 1)
                if j >= 4:
                    dve.wait_ge(silu_ready, seen(silu_ready))
                conv(mqk[:, j % 4, :], xm[:, j, :], par_at("mconv_w", 3 * j, 3), par_at("mconv_b", j), 2
                     ).then_inc(conv_ready, 1)
            dve.wait_ge(silu_ready, seen(silu_ready, 4))
            dve.wait_ge(bank_free[N("m_gates") % BANKS], N("m_gates") // BANKS + 1)
            v.tensor_scalar(grow[64:128, 2, :], grow[64:128, 0, :], 0.0, None, ALU.min).then_inc(dve_own, 1)
            dve.wait_ge(dve_own, own(dve_own))
            dve.wait_ge(lng_ready, seen(lng_ready))

            def both_ways(dst, a, b, base, op0, op1):
                f = slice(base, base + 32)
                g = slice(base + 32, base + 64)
                v.tensor_tensor_scan(dst[f, :], a[f, :], b[f, :], 0.0, op0, op1)
                v.tensor_tensor_scan(dst[g, 0:T][:, ::-1], a[g, 0:T][:, ::-1], b[g, 0:T][:, ::-1], 0.0, op0, op1).then_inc(dve_own, 1)
                dve.wait_ge(dve_own, own(dve_own))
                v.tensor_tensor_scan(dst[g, T:T2][:, ::-1], a[g, T:T2][:, ::-1], b[g, T:T2][:, ::-1], dst[g, 0:1],
                                              op0, op1).then_inc(dve_own, 1)
                dve.wait_ge(dve_own, own(dve_own))

            both_ways(grow[:, 3, :], grow[:, 2, :], grow[:, 1, :], 64, ALU.add, ALU.subtract)
            v.tensor_copy(grow[0:64, 4, :], grow[64:128, 3, :]).then_inc(dve_own, 1)
            dve.wait_ge(dve_own, own(dve_own))
            v.tensor_tensor(grow[0:64, 5, :], grow[0:64, 0, :], grow[0:64, 4, :], ALU.subtract).then_inc(dve_own, 1)
            dve.wait_ge(dve_own, own(dve_own))
            both_ways(rows[:, 0, :], grow[:, 5, :], grow[:, 5, :], 0, ALU.max, ALU.max)
            v.tensor_tensor(rows[0:64, 1, :], grow[0:64, 4, :], rows[0:64, 0, :], ALU.add).then_inc(rows_ready, 1)
            dve.wait_ge(floor_ready, seen(floor_ready))
            dve.wait_ge(bank_free[N("m_aT") % BANKS], N("m_aT") // BANKS + 1)
            v.memset(mP[:, 1, 128:256], 0.0)
            v.memset(mP[:, 1, 1152:1280], 0.0).then_inc(dve_own, 1)
            dve.wait_ge(dve_own, own(dve_own))
            spans = (((0, 512), (128, 512), (256, 512), (384, 512)), ((0, 512), (0, 512), (256, 384), (256, 512)))
            for h in range(MH):
                v.memset(mP[:, 0, 512:640], 0.0)
                v.memset(mP[:, 0, 1280:1408], 0.0).then_inc(dve_own, 1)
                dve.wait_ge(dve_own, own(dve_own))
                for z in range(2):
                    n = N(("m_max", h), z)
                    dve.wait_ge(bank_full[n % BANKS], n // BANKS + 1)
                    r = 32 * z + h
                    for s_ in range(4):
                        parts = [spans[z][s_]] if (z, s_) != (1, 0) else [(0, 128), (256, 512)]
                        for lo, hi in parts:
                            ins = v.tensor_scalar(mP[:, z, OFF[s_] + lo - T_AT[s_]:OFF[s_] + hi - T_AT[s_]], ps(n, lo, hi),
                                                  aT[:, s_, r:r + 1], 0.0, ALU.subtract, ALU.max)
                    ins.then_inc(bank_free[n % BANKS], 1)
                    dve.wait_ge(bank_free[n % BANKS], n // BANKS + 1)
                    for s_ in range(4):
                        d = OFF[s_] + s_ * P - T_AT[s_]
                        ins = v.tensor_tensor(mP[:, z, d:d + P], mP[:, z, d:d + P], con_at("tri", 256)[:, z * P:(z + 1) * P],
                                              ALU.max)
                    ins.then_inc(D_ready, 1)
                for z in range(2):
                    dve.wait_ge(E_ready, seen(E_ready))
                    for s_ in range(4):
                        n = N(("m_QK", h), s_)
                        if z == 0:
                            dve.wait_ge(bank_full[n % BANKS], n // BANKS + 1)
                        p_ = mP[:, z, OFF[s_]:OFF[s_] + T2 - T_AT[s_]]
                        ins = v.tensor_tensor(p_, p_, ps(n, 0, T2 - T_AT[s_]), ALU.mult)
                        if z == 1:
                            ins.then_inc(bank_free[n % BANKS], 1)
                dve.wait_ge(bank_free[n % BANKS], n // BANKS + 1)
                n = N(("m_den", h))
                dve.wait_ge(bank_full[n % BANKS], n // BANKS + 1)
                dn = bank[n % BANKS][0:64, :]
                stt(rows[0:64, 2, :], dn, -1.0, rows[0:64, 1, :], ALU.mult, ALU.max).then_inc(dve_own, 1)
                dve.wait_ge(dve_own, own(dve_own))
                v.tensor_tensor(rows[0:64, 2, :], dn, rows[0:64, 2, :], ALU.max).then_inc(bank_free[n % BANKS], 1)
                dve.wait_ge(bank_free[n % BANKS], n // BANKS + 1)
                v.reciprocal(rows[0:64, 2, :], rows[0:64, 2, :]).then_inc(rden_ready, 1)
                for z in range(2):
                    n = N(("m_rec", h), z)
                    dve.wait_ge(bank_full[n % BANKS], n // BANKS + 1)
                    for s_ in range(4):
                        p_ = mP[:, z, OFF[s_]:OFF[s_] + T2 - T_AT[s_]]
                        ins = v.tensor_tensor(p_, p_, ps(n, T_AT[s_], T2), ALU.mult)
                    ins.then_inc(bank_free[n % BANKS], 1)
                dve.wait_ge(bank_free[n % BANKS], n // BANKS + 1)
                v.tensor_tensor(mP[:, 0, :], mP[:, 0, :], mP[:, 1, :], ALU.add).then_inc(W_ready, 1)
                for e in range(4):
                    n = N(("m_PV", h), e)
                    dve.wait_ge(bank_full[n % BANKS], n // BANKS + 1)
                    dve.wait_ge(bank_free[N(("m_og", h), e) % BANKS], N(("m_og", h), e) // BANKS + 1)
                    v.tensor_tensor(hs[:, 4 * h + e, :], ps(n), og[:, e, :], ALU.mult).then_inc(bank_free[n % BANKS], 1)
                dve.wait_ge(rstd_ready, seen(rstd_ready))
                for e in range(4):
                    k = 4 * h + e
                    ins = stt(hs[:, k, :], hs[:, k, :], par_at("m_norm", k), stat[:, 0, :], ALU.mult, ALU.mult)
                ins.then_inc(hs_ready, 1)

            def residual2(name, l, part, segs):
                for g in range(KD):
                    n = N(name, g)
                    dve.wait_ge(bank_full[n % BANKS], n // BANKS + 1)
                    for seg in segs:
                        t = slice(seg * T, seg * T + T)
                        ins = stt(xT[:, g, t], ps(n, (seg - segs[0]) * T, (seg - segs[0] + 1) * T), mod_at(l, part, g, seg),
                                  xT[:, g, t], ALU.mult, ALU.add)
                    ins.then_inc(bank_free[n % BANKS], 1)
                dve.wait_ge(bank_free[n % BANKS], n // BANKS + 1)

            def layer_norm(i, l, s_, lo):
                n = N(("mean", i))
                dve.wait_ge(bank_full[n % BANKS], n // BANKS + 1)
                for k in range(KD):
                    ins = stt(xT[:, k, lo:], ps(n, 0, T2 - lo), -1.0 / D, xT[:, k, lo:], ALU.mult, ALU.add)
                ins.then_inc(bank_free[n % BANKS], 1)
                dve.wait_ge(bank_free[n % BANKS], n // BANKS + 1)
                dve.wait_ge(rstd_ready, seen(rstd_ready))
                for k in range(KD):
                    ins = stt(xT[:, k, lo:], xT[:, k, lo:], par_at(("ln_g", l, s_), k), stat[:, 0, 0:T2 - lo], ALU.mult, ALU.mult)
                ins.then_inc(dve_own, 1)
                dve.wait_ge(dve_own, own(dve_own))
                for k in range(KD):
                    ins = v.tensor_scalar(xT[:, k, lo:], xT[:, k, lo:], par_at(("ln_b", l, s_), k), None, ALU.add)
                ins.then_inc(ln_ready, 1)
                dve.wait_ge(ln_ready, own(ln_ready))

            def ffn(l, segs):
                lo, cols = segs[0] * T, len(segs) * T
                for j in range(NFF + 1):
                    if j < NFF:
                        n = N(("ffn_in", l), 2 * j)
                        dve.wait_ge(bank_full[n % BANKS], n // BANKS + 1)
                        w = par_at(("fconv_w", l), 3 * j, 3)
                        conv(ctmp[:, j % 4, lo:], ps(n, 0, cols), w, par_at(("fconv_b", l), j), len(segs)
                             ).then_inc(conv_ready, 1)
                    if j:
                        i = j - 1
                        n = N(("ffn_in", l), 2 * i)
                        dve.wait_ge(bank_full[(n + 1) % BANKS], (n + 1) // BANKS + 1)
                        dve.wait_ge(bank_free[n % BANKS], n // BANKS + 1)
                        v.tensor_tensor(ffa[:, i, lo:], ctmp[:, i % 4, lo:], ps(n + 1, 0, cols), ALU.mult).then_inc(bank_free[(n + 1) % BANKS], 1)

            residual2("m_out", 0, 2, (0, 1))
            layer_norm(0, 0, 0, 0)
            modulate(0, 3)
            ffn(0, (0, 1))
            residual2(("ffn_out", 0), 0, 5, (0, 1))
            layer_norm(1, 0, 1, 0)

            modulate(1, 0)
            n = N("a_kr")
            dve.wait_ge(bank_full[n % BANKS], n // BANKS + 1)
            rope = con_at("rope", 256)

            def rotate(dst, n, lo):
                v.tensor_tensor(rt[0:64, 0, :], bank[n % BANKS][0:64, lo:lo + T], rope[0:64, :], ALU.mult)
                v.tensor_tensor(rt[0:64, 1, :], bank[n % BANKS][64:128, lo:lo + T], rope[64:128, :], ALU.mult).then_inc(dve_own, 1)
                dve.wait_ge(dve_own, own(dve_own))
                return v.tensor_tensor(dst, rt[0:64, 0, :], rt[0:64, 1, :], ALU.add)

            v.tensor_copy(krope[0:64, 0:T], bank[n % BANKS][0:64, 0:T])
            rotate(krope[0:64, T:T2], n, T).then_inc(bank_free[n % BANKS], 1)
            dve.wait_ge(bank_free[n % BANKS], n // BANKS + 1)
            dve.wait_ge(rstd_ready, seen(rstd_ready))
            for k in range(2):
                ins = stt(ckv[:, k, :], ckv[:, k, :], par_at("kv_norm", k), stat[:, 0, :], ALU.mult, ALU.mult)
            ins.then_inc(ckn_ready, 1)
            dve.wait_ge(ckn_ready, own(ckn_ready))
            dve.wait_ge(rstd_ready, seen(rstd_ready))
            for k in range(3):
                ins = stt(cq[:, k, :], cq[:, k, :], par_at("q_norm", k), stat[:, 0, 0:T], ALU.mult, ALU.mult)
            ins.then_inc(ckn_ready, 1)
            dve.wait_ge(ckn_ready, own(ckn_ready))
            for h in range(AH):
                n = N("a_qrope", h // 2)
                if h % 2 == 0:
                    dve.wait_ge(bank_full[n % BANKS], n // BANKS + 1)
                ins = rotate(qr[0:64, h, :], n, (h % 2) * T)
                if h % 2:
                    ins.then_inc(bank_free[n % BANKS], 1)
                    dve.wait_ge(bank_free[n % BANKS], n // BANKS + 1)
                else:
                    ins.then_inc(dve_own, 1)
                    dve.wait_ge(dve_own, own(dve_own))
            for i in range(2 * AH + 1):
                if i < 2 * AH:
                    n = N(("aS", i))
                    dve.wait_ge(bank_full[n % BANKS], n // BANKS + 1)
                    v.tensor_reduce(ast[:, i, 0:1], ps(n), AX, ALU.max, negate=True).then_inc(dve_own, 1)
                    dve.wait_ge(dve_own, own(dve_own))
                    v.tensor_scalar(ast[:, i, 1:2], ast[:, i, 0:1], A_SCALE, None, ALU.mult).then_inc(amax_ready, 1)
                if i:
                    j = i - 1
                    dve.wait_ge(bank_free[N(("aS", j)) % BANKS], N(("aS", j)) // BANKS + 1)
                    v.reciprocal(ast[:, j, 3:4], ast[:, j, 2:3]).then_inc(dve_own, 1)
                    dve.wait_ge(dve_own, own(dve_own))
                    v.tensor_scalar(ap_[:, j % 3, :], ap_[:, j % 3, :], ast[:, j, 3:4], None, ALU.mult).then_inc(ap_ready, 1)
            residual2("a_out", 1, 2, (1,))
            layer_norm(2, 1, 0, LAT)
            modulate(1, 3, (1,))
            ffn(1, (1,))
            residual2(("ffn_out", 1), 1, 5, (1,))
            layer_norm(3, 1, 1, LAT)


def pack_constants():
    p = np.arange(P)[:, None]
    c = np.zeros((P, CON.n), np.float32)

    def put(name, a):
        c[:, CON(name):CON(name) + a.shape[1]] = a

    put("ident", np.eye(P))
    put("ones", np.ones((P, P)))
    put("halves", np.kron(np.eye(2), np.ones((HD, HD))))
    keys = np.arange(T)[None, :]
    put("strict", np.where(np.concatenate([keys[:, :P] < p, keys < p + P], 1), 0.0, NEG))
    ends = 16 * np.arange(16)[None, :] + 31
    put("cmask", np.concatenate([(ends <= p + P * q) & (np.arange(16) < CMP_N) for q in range(2)], 1))
    keys = np.arange(P)[None, :]
    put("tri", np.concatenate([np.where(keys >= p, 0.0, -NEG), np.where(keys <= p, 0.0, -NEG)], 1))
    pick = np.zeros((P, 127))
    pick[:, 63] = 1
    put("pick", pick)
    t = np.arange(T)
    inv = np.float32(10000.0) ** (-np.arange(16, dtype=np.float32) / np.float32(16))
    ang = [(c.astype(np.float32)[None, :] * inv[:, None]).astype(np.float32) for c in (t // 64, t % 64)]
    cos = [np.cos(a) for a in ang for _ in range(2)]
    sin = [sign * np.sin(a) for a in ang for sign in (-1, 1)]
    put("rope", np.concatenate(cos + sin, 0))
    j = np.arange(512) - (T - 1)
    near = np.maximum(j, 1).astype(np.float32)
    far = 16 + (np.log(near / np.float32(16)) / np.float32(math.log(8)) * 16).astype(np.int32)
    bucket = np.where(j < 0, 32, np.where(j < 16, j, np.minimum(far, 31)))
    onehot = (np.arange(33)[:, None] == bucket[None, :]).astype(np.float32)
    return c, onehot


def pack_params(x):
    a = np.zeros((P, PAR.n), np.float32)

    def put(name, v):
        v = np.asarray(v)
        a[:v.shape[0], PAR(name):PAR(name) + v.shape[1]] = v

    def cols(v):
        return np.asarray(v).reshape(-1, P).T

    for l in range(DEPTH):
        put(("g_attn", l), cols(x["norm_attn"][l]))
        put(("g_mlp", l), cols(x["norm_mlp"][l]))
        put(("subln", l), np.tile(x["diff_subln"][l], 2)[:, None])
        pos = [np.asarray(x[k][l]).reshape(16, P).T for k in ("cmp_pos_k", "cmp_pos_v")]
        put(("pos", l), np.concatenate(pos, 1))
        k2 = np.asarray(x["cmp_k_w2"][l]).reshape(2, P, HD)
        put(("w2k", l), np.concatenate([k2[0], k2[0], k2[1], k2[1]], 1))
        v2 = np.asarray(x["cmp_v_w2"][l]).reshape(2, P, HD)
        put(("w2v", l), np.concatenate([v2[0], v2[1]], 1))
        put(("dlam", l), np.broadcast_to(np.asarray(x["diff_lambda"][l]).reshape(1, 128), (P, 128)))
    put("g_final", cols(x["final_norm"]))
    table = np.concatenate([np.asarray(x["rel_bias"]), np.full((1, 12), NEG, np.float32)], 0)
    put("table", table)
    for l in range(DEPTH):
        put(("ada_b", l), cols(x["ada_b_2"][l]))
        for i in range(2):
            put(("ln_g", l, i), cols(x["ln_g_2"][l][i]))
            put(("ln_b", l, i), cols(x["ln_b_2"][l][i]))
        put(("fconv_w", l), np.asarray(x["ffn_conv_w_2"][l]).reshape(3, NFF, P).transpose(2, 1, 0).reshape(P, -1))
        put(("fconv_b", l), cols(x["ffn_conv_b_2"][l]))
    conds = np.stack([cols(x["c_2"][0]), cols(x["c_ctx_2"])], 2)
    put("cond", conds.reshape(P, 16))
    put("mconv_w", np.asarray(x["m_conv_w_2"][0]).reshape(3, MK, P).transpose(2, 1, 0).reshape(P, -1))
    put("mconv_b", cols(x["m_conv_b_2"][0]))
    bg = np.zeros((P, 1), np.float32)
    for z in range(2):
        for g in range(2):
            bg[64 * g + 32 * z:64 * g + 32 * z + MH, 0] = np.asarray(x["m_b_gates_2"])[0, z, g * MH:(g + 1) * MH]
    put("b_gates", bg)
    put("m_norm", cols(x["m_norm_g_2"][0]))
    put("q_norm", cols(x["a_q_norm_2"][0]))
    put("kv_norm", cols(x["a_kv_norm_2"][0]))
    return a


def pack_stream(x):
    s = np.zeros((W.n, P, SLOT), np.float32)

    def put(w, a):
        k = a.shape[0] // P
        full = np.zeros((k, P, SLOT // k), np.float32)
        full[:, :, :a.shape[1]] = a.reshape(k, P, a.shape[1])
        s[w, :, :k * (SLOT // k)] = full.transpose(1, 0, 2).reshape(P, -1)

    for l in range(DEPTH):
        w = np.asarray(x["w_in"][l])

        def c(lo, n):
            return w[:, lo:lo + n]

        kc, vc, ks, vs, kw, vw = (c(1792 + 64 * i, 64) for i in range(6))
        df = 2188
        for g, a in enumerate((c(0, 256), c(256, 256), c(768, 256), c(1024, 256), c(1536, 256), c(df, 256),
                               c(df + 256, 256), np.concatenate([ks, ks, kw, kw], 1),
                               np.concatenate([kc, kc, vc, vc], 1))):
            put(W(("proj", l), g), a)
        for g, a in enumerate((c(512, 256), c(1280, 256), c(df + 512, 256),
                               np.concatenate([vs, vw, c(2176, 12)], 1))):
            put(W(("nat", l), g), a)
        for i, k in enumerate(("cmp_k_w1", "cmp_v_w1")):
            for h in range(2):
                put(W(("cmp", l), 2 * i + h), np.asarray(x[k][l])[:, P * h:P * h + P])
        for name, key in (("out", "w_out"), ("down", "w_down")):
            m = np.asarray(x[key][l])
            for i in range(m.shape[0] // T):
                put(W((name, l), i), m[T * i:T * (i + 1)])
        for g in range(16):
            put(W(("up", l), g), np.asarray(x["w_up"][l])[:, T * g:T * (g + 1)])

    def rows_of(w, m, per):
        for i in range(m.shape[0] // (per * P)):
            put(w + i, m[per * P * i:per * P * (i + 1)])

    for l in range(DEPTH):
        a = np.asarray(x["ada_w_2"][l])
        for i in range(24):
            put(W(("ada", l), i), a[:, T * i:T * (i + 1)])
        f = np.asarray(x["ffn_w_in_2"][l])
        for j in range(NFF):
            put(W(("ffn_in", l), j), np.concatenate([f[:, P * j:P * j + P], f[:, P * (NFF + j):P * (NFF + j + 1)]], 1))
        rows_of(W(("ffn_out", l)), np.asarray(x["ffn_w_out_2"][l]), 2)
    a = np.asarray(x["m_w_up_2"][0])
    for g in range(8):
        put(W("m_up", g), a[:, T * g:T * (g + 1)])
    gates = np.zeros((MK * P, P), np.float32)
    for z in range(2):
        for g in range(2):
            gates[:, 64 * g + 32 * z:64 * g + 32 * z + MH] = np.asarray(x["m_w_gates_2"])[0, z, :, g * MH:(g + 1) * MH]
    put(W("m_gates"), gates)
    wv, wqk, wog = (np.asarray(x[k][0]) for k in ("m_w_v_2", "m_w_qk_2", "m_w_og_2"))
    for h in range(MH):
        rows_of(W("m_v", 4 * h), wv[:, T2 * h:T2 * (h + 1)], 4)
        for j in range(2):
            rows_of(W(("m_qk", h), 2 * j), wqk[:, D * j + T * h:D * j + T * (h + 1)], KD)
            put(W(("m_og", h), j), wog[:, T2 * h + T * j:T2 * h + T * (j + 1)])
    rows_of(W("m_out"), np.asarray(x["m_w_out_2"][0]), 2)
    swap = np.concatenate([np.arange(16, 32), np.arange(16), np.arange(48, 64), np.arange(32, 48)])
    a = np.asarray(x["a_w_dkv_2"][0])
    put(W("a_dkv"), a[:, :T])
    put(W("a_dkv", 1), np.concatenate([a[:, T:], a[:, T:][:, swap]], 1))
    a = np.asarray(x["a_w_dq_2"][0])
    put(W("a_dq"), a[:, :T])
    put(W("a_dq", 1), a[:, T:])
    a = np.asarray(x["a_w_ukv_2"][0]).reshape(2 * P, AH, 2, P)
    for i in range(2):
        put(W("a_ukv", i), a[:, :, i].reshape(2 * P, D))
    a = np.asarray(x["a_w_uq_2"][0]).reshape(3 * P, AH, 192)
    for g in range(2):
        put(W("a_uq", g), a[:, 4 * g:4 * g + 4, :P].reshape(3 * P, 4 * P))
        r = a[:, 4 * g:4 * g + 4, P:]
        put(W("a_uq", 2 + g), np.concatenate([r, r[:, :, swap]], 2).reshape(3 * P, 4 * P))
    rows_of(W("a_out"), np.asarray(x["a_w_out_2"][0]), 2)
    return s


def kernel(**inputs):
    import concourse.bacc as bacc
    from concourse.bass_utils import run_bass_kernel_spmd

    nc = bacc.Bacc("TRN2", target_bir_lowering=False, num_devices=1)
    consts, onehot = pack_constants()
    arrays = {
        "in_tokens": np.concatenate([np.asarray(inputs["ctx_2"])[0], np.asarray(inputs["x"])[0]], 0),
        "in_stream": pack_stream(inputs),
        "in_params": pack_params(inputs),
        "in_consts": consts,
        "in_onehot": onehot,
    }
    args = [nc.dram_tensor(name, a.shape, F32, kind="ExternalInput").ap() for name, a in arrays.items()]
    args.append(nc.dram_tensor("out_0", (1, T, D), F32, kind="ExternalOutput").ap())
    args.append(nc.dram_tensor("bias_vectors", (12, 512), F32, kind="Internal").ap())
    build(nc, *args)
    r = run_bass_kernel_spmd(nc, [arrays], core_ids=[0])
    return r.results[0]["out_0"]
```

```python
import math
from contextlib import ExitStack

import numpy as np
import concourse.bass as bass
from concourse import mybir

P = 128
F32 = mybir.dt.float32
ALU = mybir.AluOpType
ACT = mybir.ActivationFunctionType
AX = mybir.AxisListType.X

D = 1024
KD = D // P
T = 256
T2 = 2 * T
LAT = T
DEPTH = 2
EPS = 1e-6
NEG = -1e30
HD = 64
CMP_N = 15
SLOT = 2048
R = 2
BANKS = 8
ALPHA = (2 * DEPTH) ** 0.25
NFF = 22
MH = 4
MK = 16
AH = 8
A_SCALE = 192 ** -0.5
OFF = (0, 512, 1024, 1280)
T_AT = (0, 0, T, T)


class Plan:

    def __init__(self):
        self.at, self.n = {}, 0

    def add(self, name, count=1):
        self.at[name] = self.n
        self.n += count

    def __call__(self, name, i=0):
        return self.at[name] + i


def units():
    out = []
    for h in range(4):
        out.append(dict(kind="sb", h=h, q=h // 2, k=2 + h // 2, r=64 * (h % 2), kk=64, v=("vn", 0), first=True,
                        last=True, chunk=h // 2, row=64 * (h % 2)))
    for h in range(4):
        out.append(dict(kind="mb", h=h, q=4 + h // 2, k=6 + h // 2, r=64 * (h % 2), kk=64, v=("vn", 1), bias=h,
                        first=True, last=True, chunk=2 + h // 2, row=64 * (h % 2)))
    for h in range(4):
        for b, kind in enumerate(("cmp", "slc", "win")):
            out.append(dict(kind=kind, h=h, q=8 + h // 2, k=13 + b, r=64 * (h % 2), kk=64, v=(kind, 0), bias=4 + h,
                            first=b == 0, last=b == 2, chunk=4 + h // 2, row=64 * (h % 2), gate=4 * b + h))
    for h in range(4):
        for c in range(2):
            out.append(dict(kind="df", h=h, q=10 + h // 2, k=12 + h // 2, r=64 * (h % 2) + 32 * c, kk=32, v=("vn", 2),
                            bias=8 + h, first=c == 0, last=c == 1, chunk=6 + h // 2, row=64 * (h % 2), c=c))
    return out


UNITS = units()
NU = len(UNITS)


FR = mybir.dt.float32r


def params1_layout():
    p = Plan()
    for l in range(DEPTH):
        p.add(("pos", l), 32)
        p.add(("w2k", l), 256)
        p.add(("w2v", l), 128)
        p.add(("dlam", l), 128)
    p.add("table", 12)
    p.add("strict", 384)
    p.add("cmask", 32)
    p.add("halves", 128)
    return p


def params_layout():
    p = Plan()
    for l in range(DEPTH):
        p.add(("g_attn", l), KD)
        p.add(("g_mlp", l), KD)
        p.add(("subln", l), 1)
        p.add(("ada_b", l), 48)
        for s in range(2):
            p.add(("ln_g", l, s), KD)
            p.add(("ln_b", l, s), KD)
        p.add(("fconv_w", l), 3 * NFF)
        p.add(("fconv_b", l), NFF)
    p.add("g_final", KD)
    p.add("cond", 16)
    p.add("mconv_w", 48)
    p.add("mconv_b", 16)
    p.add("b_gates", 1)
    p.add("m_norm", 16)
    p.add("q_norm", 3)
    p.add("kv_norm", 2)
    return p


def consts_layout():
    p = Plan()
    p.add("ident", 128)
    p.add("ones", 128)
    p.add("rope", 256)
    p.add("tri", 256)
    p.add("pick", 127)
    return p


PAR = params_layout()
PAR1 = params1_layout()
CON = consts_layout()


class Group:

    def __init__(self, name, tickets, K, T_, src, natural=False):
        self.name, self.tickets, self.K, self.T, self.src, self.natural = name, tickets, K, T_, src, natural
        across = tickets // (T_ // P) * 4 if natural else tickets
        self.kc = next(c for c in (8, 4, 2) if c * across <= SLOT // P)
        self.slots = -(-K // self.kc)


class Stream:

    def __init__(self):
        self.w, self.g, self.split, self.q = {}, {}, [], 0
        self.n, self.chunks, self.raised = 0, [], 0

    def direct(self, name, count=1):
        self.w[name] = self.n
        self.n += count

    def group(self, *a, **kw):
        g = Group(*a, **kw)
        self.g[g.name] = g
        g.w0, g.s0, g.q0 = self.n, len(self.split), self.q
        self.w[g.name] = self.n
        self.n += g.slots
        self.q += g.K
        for j in range(g.slots):
            self.split.append((g.w0 + j, g.q0 + min(g.K, (j + 1) * g.kc) - 1))
        for k in range(g.K):
            self.raised += k < g.K - 1
            self.chunks.append((g, k, self.raised))


def stream_plan():
    w = Stream()
    for l in range(DEPTH):
        for i in range(3):
            w.group(("proj", l, i), (8, 8, 2)[i], KD, T, "h")
        w.group(("nat", l), 4, KD, T, "h", natural=True)
        w.direct(("cmp", l), 4)
        w.direct(("ada", l), 24)
        w.group(("out", l), 8, KD, T, "mixed")
        for i in range(4):
            w.group(("up", l, i), 8, KD, T, "h")
        w.group(("down", l), 8, 32, T, "act")
    for i in range(4):
        w.group(("m_up", i), 4, KD, T2, "h")
    w.direct("m_gates")
    for h in range(MH):
        w.group(("m_v", h), 4, MK, T2, "xm", natural=True)
    for h in range(MH):
        w.group(("m_qk", h), 4, MK, T2, "xc")
        w.group(("m_og", h), 4, KD, T2, "h")
    w.group("m_out", 8, MK, T2, "hs")
    for i in range(NFF // 2):
        w.group(("ffn_in", 0, i), 4, KD, T2, "h")
    w.group(("ffn_out", 0), 8, NFF, T2, "ffa")
    w.group("a_dkv", 3, KD, T2, "h")
    w.group("a_dq", 3, KD, T, "h")
    w.group("a_ukv", AH, 2, T2, "ckv")
    w.group("a_v", 8, 2, T2, "ckv", natural=True)
    for i in range(2):
        w.group(("a_uq", i), 8, 3, T, "cq")
    w.group("a_out", 8, AH, T, "aoT")
    for i in range(6):
        w.group(("ffn_in", 1, i), 8 if i < 5 else 4, KD, T, "h")
    w.group(("ffn_out", 1), 8, NFF, T, "ffa")
    w.direct("padding", -w.n % R)
    return w


def ticket_plan():
    n = Plan()
    n.add("bias")
    n.add("xT", KD)
    for l in range(DEPTH):
        n.add(("rms1", l))
        for i in range(3):
            n.add(("proj", l, i), (8, 8, 2)[i])
        n.add(("nat", l), 4)
        n.add(("hid", l), 4)
        n.add(("kc", l))
        n.add(("vc", l))
        for i in range(NU + 3):
            if i < NU:
                n.add(("S", l, i))
            if i < 24:
                n.add(("ada", l, i))
            if 0 <= i - 2 < NU:
                n.add(("PT", l, i - 2))
            if 0 <= i - 3 < NU and UNITS[i - 3]["first"]:
                n.add(("O", l, i - 3))
            elif 0 <= i - 3 < NU:
                n.at[("O", l, i - 3)] = n.at[("O", l, i - 4)]
        n.add(("dfn", l))
        n.add(("out", l), 8)
        n.add(("rms2", l))
        for i in range(4):
            n.add(("up", l, i), 8)
        n.add(("down", l), 8)
    n.add("rmsf")
    for i in range(4):
        n.add(("m_up", i), 4)
    n.add("m_gates")
    n.add("m_aT")
    for h in range(MH):
        n.add(("m_v", h), 4)
    for h in range(MH):
        n.add(("m_max", h), 2)
        n.add(("m_qk", h), 4)
        n.add(("m_QK", h), 4)
        n.add(("m_og", h), 4)
        n.add(("m_den", h))
        n.add(("m_rec", h), 2)
        n.add(("m_PV", h), 4)
        n.add(("m_rms", h))
    n.add("m_out", 8)
    n.add(("mean", 0))
    n.add(("var", 0))
    for i in range(NFF // 2):
        n.add(("ffn_in", 0, i), 4)
    n.add(("ffn_out", 0), 8)
    n.add(("mean", 1))
    n.add(("var", 1))
    n.add("a_dkv", 3)
    n.add("a_dq", 3)
    n.add("a_kvn")
    n.add("a_qn")
    n.add("a_ukv", AH)
    n.add("a_v", 8)
    for i in range(2):
        n.add(("a_uq", i), 8)
    for i in range(2 * AH + 4):
        if i < 2 * AH:
            n.add(("aS", i))
        if 0 <= i - 2 < 2 * AH:
            n.add(("aPT", i - 2))
        if i >= 4 and i % 2 == 0 and (i - 4) // 2 < AH:
            n.add(("aO", (i - 4) // 2))
    n.add("a_out", 8)
    n.add(("mean", 2))
    n.add(("var", 2))
    for i in range(6):
        n.add(("ffn_in", 1, i), 8 if i < 5 else 4)
    n.add(("ffn_out", 1), 8)
    n.add(("mean", 3))
    n.add(("var", 3))
    n.add("oT", 4)
    return n


ST = stream_plan()
N = ticket_plan()


def W(name, i=0):
    return ST.w[name] + i


def G(*name):
    return ST.g[name if len(name) > 1 else name[0]]


class Count:

    def __init__(self):
        self.n = {}

    def __call__(self, sem, more=1):
        self.n[id(sem)] = self.n.get(id(sem), 0) + more
        return self.n[id(sem)]


def build(nc, tokens, stream, params, params1, consts, onehot, out, scratch):
    with ExitStack() as ctx:
        def sb(name, shape):
            return ctx.enter_context(nc.sbuf_tensor(name, shape, F32))

        def sem(name):
            return ctx.enter_context(nc.semaphore(name))

        bank = [ctx.enter_context(nc.psum_tensor(f"bank{i}", [P, 512], F32)) for i in range(BANKS)]
        ring = sb("ring", [P, R, SLOT])
        ws = ctx.enter_context(nc.sbuf_tensor("ws", [P, 2, 2, SLOT], FR))
        xs = ctx.enter_context(nc.sbuf_tensor("xs", [P, 2, 2, T2], FR))
        slot_full = [sem(f"slot_full{i}") for i in range(R)]
        w_high = sem("weights_high_ready")
        slot_done = sem("slot_done")
        x_high = sem("input_high_ready")
        x_done = sem("input_split")
        chunk_done = sem("chunk_multiplied")
        bank_full = [sem(f"bank_full{i}") for i in range(BANKS)]
        bank_free = [sem(f"bank_free{i}") for i in range(BANKS)]

        xT = sb("xT", [P, KD, T2])
        hT = sb("hT", [P, KD, T2])
        par = sb("par", [P, PAR.n])
        con = sb("con", [P, CON.n])
        eps = sb("eps", [P, 1])
        one = sb("one", [P, 1])
        stat = sb("stat", [P, 2, T2])
        A1 = 31840
        arena = sb("arena", [P, A1])

        def region(off, shape):
            n = int(np.prod(shape))
            ap = arena[:, off:off + n]
            if len(shape) == 2:
                ap = ap.rearrange("p (a b) -> p a b", a=shape[0])
            if len(shape) == 3:
                ap = ap.rearrange("p (a b c) -> p a b c", a=shape[0], b=shape[1])
            return ap

        def par_at(name, i=0, n=1):
            return par[:, PAR(name, i):PAR(name, i) + n]

        def con_at(name, n):
            return con[:, CON(name):CON(name) + n]

        ident = con_at("ident", 128)
        ones = con_at("ones", 128)

        o = Plan()
        for name, n in (("qk", 16 * T), ("x2", 2 * T), ("x3", 512), ("vn", 6 * T), ("vsw", 280), ("mixed", KD * T),
                        ("act", 32 * T), ("bias", 12 * 384), ("cbias", 128), ("hid", 64), ("hidg", 64), ("lamp", 64), ("kc", 32), ("vc", 64),
                        ("s", 3 * 384), ("t", 4 * 384), ("pt", 2 * 384), ("st", 8 * NU), ("lam", 64),
                        ("relu", 2 * 512), ("par1", PAR1.n)):
            o.add(name, n)
        qk = region(o("qk"), (16, T))
        x2 = region(o("x2"), (2, T))
        x3 = region(o("x3"), (2, 16, 16))
        vn = region(o("vn"), (3, 2, T))
        vsw = region(o("vsw"), (2, 140))
        mixed = region(o("mixed"), (KD, T))
        act = region(o("act"), (32, T))
        bias = region(o("bias"), (12, 384))
        cbias = region(o("cbias"), (4, 32))
        hid = region(o("hid"), (4, 16))
        hidg = region(o("hidg"), (4, 16))
        lamp = region(o("lamp"), (64,))
        kcT = region(o("kc"), (16,))
        vc = region(o("vc"), (64,))
        sbuf = region(o("s"), (3, 384))
        tbuf = region(o("t"), (4, 384))
        ptb = region(o("pt"), (2, 384))
        st = region(o("st"), (NU, 8))
        lam = region(o("lam"), (64,))
        xnat = region(o("act") + 4096, (4, D))
        hankel = region(o("act") + 4096, (12, T))
        tz = region(o("mixed"), (4 * 353,)).rearrange("p (a b) -> p a b", a=4)
        relu = region(o("relu"), (2, 512))
        par1 = region(o("par1"), (PAR1.n,))
        assert o.n <= A1, o.n

        def par1_at(name, i=0, n=1):
            return par1[:, PAR1(name, i):PAR1(name, i) + n]

        halves = par1_at("halves", 0, 128)

        mod = sb("mod", [P, DEPTH, 96])
        cs = sb("cs", [P, 16])
        scrap = sb("scrap", [P, DEPTH])
        o = Plan()
        for name, n in (("xm", MK * T2), ("xc", MK * T2), ("v", MK * T2), ("qk", 4 * T2), ("P", 6 * T2),
                        ("rows", 3 * T2), ("aT", 4 * 64)):
            o.add(name, n)
        assert o.n <= A1, o.n
        xm = region(o("xm"), (MK, T2))
        hs = xm
        xc = region(o("xc"), (MK, T2))
        mv = region(o("v"), (4, MH * T2))
        mqk = region(o("qk"), (4, T2))
        og = mqk
        mP = region(o("P"), (2, 3 * T2))
        grow = region(o("P"), (6, T2))
        rows = region(o("rows"), (3, T2))
        aT = region(o("aT"), (4, 64))
        sq2 = region(o("xc"), (KD, T2))
        ctmp = region(o("xm"), (4, T2))
        ffa = region(o("xc") + KD * T2, (NFF, T2))
        o = Plan()
        for name, n in (("ckv", 2 * T2), ("cq", 3 * T), ("kr", T2), ("rt", 2 * T), ("kn", AH * T2), ("v", 4 * D), ("qn", AH * T),
                        ("qr", AH * T), ("oT", AH * T), ("ap", 3 * T2), ("apt", 2 * 4 * T), ("ast", 16 * 4),
                        ("cks", 3 * T2), ("osb", 2 * D)):
            o.add(name, n)
        assert o.n <= A1, o.n
        ckv = region(o("ckv"), (2, T2))
        cq = region(o("cq"), (3, T))
        krope = region(o("kr"), (T2,))
        rt = region(o("rt"), (2, T))
        kn = region(o("kn"), (AH, T2))
        av = region(o("v"), (4, D))
        qn = region(o("qn"), (AH, T))
        qr = region(o("qr"), (AH, T))
        aoT = region(o("oT"), (AH, T))
        ap_ = region(o("ap"), (3, T2))
        apt = region(o("apt"), (2, 4, T))
        ast = region(o("ast"), (16, 4))
        cks = region(o("cks"), (3, T2))
        osb = region(o("osb"), (2, D))

        cs_ready = sem("condition_ready")
        mod_ready = sem("modulation_ready")
        conv_ready = sem("conv_ready")
        silu_ready = sem("silu_ready")
        lng_ready = sem("log_gate_terms_ready")
        rows_ready = sem("gate_rows_ready")
        floor_ready = sem("denominator_floor_ready")
        D_ready = sem("exponents_ready")
        E_ready = sem("decays_ready")
        rden_ready = sem("reciprocal_denominators_ready")
        W_ready = sem("mlstm_weights_ready")
        hs_ready = sem("mixer_output_ready")
        ln_ready = sem("layer_norm_ready")
        ffa_ready = sem("feed_forward_inner_ready")
        ckn_ready = sem("latents_normed")
        amax_ready = sem("max_ready")
        aexp_ready = sem("attention_exp_ready")
        ap_ready = sem("attention_weights_ready")
        dma_x, dma_con, dma_par, dma_oh = sem("dma_x"), sem("dma_con"), sem("dma_par"), sem("dma_onehot")
        dma_bv, dma_bias, dma_out = sem("dma_bias_vector"), sem("dma_bias"), sem("dma_out")
        dve_own, act_own = sem("dve_own"), sem("act_own")
        small_ready = sem("small_constants_ready")
        cbias_ready = sem("compressed_bias_ready")
        sq_ready = sem("squares_ready")
        rstd_ready = sem("rstd_ready")
        h_ready = sem("h_ready")
        x3_ready = sem("x3_ready")
        hid_ready = sem("hidden_ready")
        logits_ready = sem("logits_ready")
        exp_ready = sem("exp_ready")
        arg_ready = sem("log_weights_ready")
        sb_ready = sem("stick_weights_ready")
        p_ready = sem("softmax_weights_ready")
        dfn_ready = sem("diff_normed")
        act_ready = sem("activations_ready")
        gate_exp = sem("gate_exp_ready")
        lam_sum = sem("lambda_sums_ready")
        lam_exp = sem("lambda_exp_ready")
        out_copied = sem("out_copied")

        def ps(n, lo=0, hi=512):
            return bank[n % BANKS][:, lo:hi]

        SRC = {"mixed": mixed, "act": act, "xm": xm, "xc": xc, "hs": hs, "ckv": ckv, "cq": cq, "aoT": aoT}

        def source(g, k):
            if g.src in ("h", "ffa"):
                return (hT if g.src == "h" else ffa)[:, k, T2 - g.T:]
            return SRC[g.src][:, k, :]

        def chunk_end(q):
            g, k, raised = ST.chunks[q]
            if k < g.K - 1:
                return chunk_done, raised
            n = N(g.name) + g.tickets - 1
            return bank_full[n % BANKS], n // BANKS + 1

        def follows(s_):
            return s_ + 1 < len(ST.split) and ST.split[s_ + 1][0] == ST.split[s_][0] + 1

        block = ctx.enter_context(nc.Block())

        @block.sync
        def _(sp):
            sp.dma_start(con[:, :], consts).then_inc(dma_con, 16)
            sp.dma_start(par[:, :], params).then_inc(dma_par, 16)
            sp.dma_start(par1, params1).then_inc(dma_par, 16)
            sp.dma_start(act.rearrange("p a b -> p (a b)")[0:33, 0:512], onehot).then_inc(dma_oh, 16)
            sp.dma_start(xnat, tokens.rearrange("(a p) d -> p a d", p=P)).then_inc(dma_x, 16)
            for i in range(R):
                sp.dma_start(ring[:, i, :], stream[i]).then_inc(slot_full[i], 16)
            sp.wait_ge(bank_free[N("bias") % BANKS], N("bias") // BANKS + 1)
            sp.dma_start(scratch, relu[0:12, 0, :]).then_inc(dma_bv, 16)
            sp.wait_ge(dma_bv, 16)
            for k in range(KD):
                sp.wait_ge(bank_free[N("xT", k) % BANKS], N("xT", k) // BANKS + 1)
            hnd = scratch.tensor
            sp.dma_start(hankel, bass.AP(tensor=hnd, offset=128, ap=[[1, P], [512, 12], [1, T]])).then_inc(dma_bias, 16)
            sp.dma_start(tz, bass.AP(tensor=hnd, offset=4 * 512, ap=[[1, P], [512, 4], [1, 353]])).then_inc(dma_bias, 16)
            with sp.Fori(1, ST.n // R) as turn:
                for i in range(R):
                    sp.wait_ge(slot_done, turn * R + (i - R + 1))
                    sp.dma_start(ring[:, i, :], stream[turn * R + i]).then_inc(slot_full[i], 16)
            sp.wait_ge(out_copied, 1)
            sp.dma_start(out.rearrange("b (a p) d -> p (b a) d", p=P), osb).then_inc(dma_out, 16)
            sp.wait_ge(dma_out, 16)

        @block.tensor
        def _(pe):
            seen = Count()
            mm = nc.tensor.matmul

            def slot(w, kc):
                n = SLOT // kc
                return ring[:, w % R, 0:kc * n].rearrange("p (k n) -> p k n", k=kc)

            def linear(g):
                N0 = N(g.name)
                for k in range(g.K):
                    w, j, q = g.w0 + k // g.kc, k % g.kc, g.q0 + k
                    if j == 0:
                        pe.wait_ge(slot_done, w + 1)
                    pe.wait_ge(x_done, q + 1)
                    cols = SLOT // g.kc
                    a = [ws[:, (g.s0 + k // g.kc) % 2, i, j * cols:(j + 1) * cols] for i in range(2)]
                    x = [xs[:, q % 2, i, 0:g.T] for i in range(2)]
                    for p in range(g.tickets):
                        n = N0 + p
                        if k == 0:
                            if n >= BANKS:
                                pe.wait_ge(bank_free[n % BANKS], n // BANKS)
                        for i, (wi, xi) in enumerate(((0, 0), (0, 1), (1, 0))):
                            first, last = k == i == 0, k == g.K - 1 and i == 2
                            if not g.natural:
                                ins = mm(ps(n, 0, g.T), a[wi][:, p * P:(p + 1) * P], x[xi], start=first, stop=last)
                            else:
                                nh = g.tickets // (g.T // P)
                                width = 396 if nh == 2 and g.T == T and p % 2 else 512
                                ins = mm(ps(n, 0, width), x[xi][:, (p // nh) * P:(p // nh + 1) * P],
                                         a[wi][:, (p % nh) * 512:(p % nh) * 512 + width], start=first, stop=last)
                        if k == g.K - 1:
                            ins.then_inc(bank_full[n % BANKS], 1)
                        elif p == g.tickets - 1:
                            ins.then_inc(chunk_done, 1)

            def sum_squares(n, src, chunks, cols, stationary):
                pe.wait_ge(sq_ready, seen(sq_ready))
                if n >= BANKS:
                    pe.wait_ge(bank_free[n % BANKS], n // BANKS)
                for k in range(chunks):
                    ins = mm(ps(n, 0, cols), stationary, src(k), start=(k == 0), stop=(k == chunks - 1))
                ins.then_inc(bank_full[n % BANKS], 1)

            pe.wait_ge(dma_con, 16)
            pe.wait_ge(dma_par, 32)
            pe.wait_ge(dma_oh, 16)
            oh = act.rearrange("p a b -> p (a b)")[0:33, 0:512]
            n = N("bias")
            if n >= BANKS:
                pe.wait_ge(bank_free[n % BANKS], n // BANKS)
            mm(bank[n % BANKS][0:12, :], par1[0:33, PAR1("table"):PAR1("table") + 12], oh, start=True, stop=True).then_inc(bank_full[n % BANKS], 1)
            pe.wait_ge(dma_x, 16)
            for k in range(KD):
                n = N("xT", k)
                if n >= BANKS:
                    pe.wait_ge(bank_free[n % BANKS], n // BANKS)
                for t in range(4):
                    ins = nc.tensor.transpose(ps(n, t * P, (t + 1) * P), xnat[:, t, k * P:(k + 1) * P], ident)
                ins.then_inc(bank_full[n % BANKS], 1)

            for l in range(DEPTH):
                sum_squares(N(("rms1", l)), lambda k: act[:, k, :], KD, T, ones)
                for i in range(3):
                    linear(G("proj", l, i))
                linear(G("nat", l))
                pe.wait_ge(x3_ready, seen(x3_ready))
                for i in range(4):
                    w, n = W(("cmp", l), i), N(("hid", l), i)
                    pe.wait_ge(slot_full[w % R], 16 * (w // R + 1))
                    wd = slot(w, 16)
                    if n >= BANKS:
                        pe.wait_ge(bank_free[n % BANKS], n // BANKS)
                    for j in range(16):
                        ins = mm(ps(n, 0, 16), wd[:, j, :], x3[:, i // 2, j, :], start=(j == 0), stop=(j == 15))
                    ins.then_inc(bank_full[n % BANKS], 1)
                pe.wait_ge(hid_ready, seen(hid_ready, 4))
                n = N(("kc", l))
                if n >= BANKS:
                    pe.wait_ge(bank_free[n % BANKS], n // BANKS)
                for j in range(2):
                    ins = mm(ps(n, 0, 16), par1_at(("w2k", l), 128 * j, 128), hidg[:, j, :],
                             start=(j == 0), stop=(j == 1))
                ins.then_inc(bank_full[n % BANKS], 1)
                n = N(("vc", l))
                if n >= BANKS:
                    pe.wait_ge(bank_free[n % BANKS], n // BANKS)
                for j in range(2):
                    ins = mm(bank[n % BANKS][0:16, 0:64], hidg[:, 2 + j, :],
                             par1_at(("w2v", l), 64 * j, 64), start=(j == 0), stop=(j == 1))
                ins.then_inc(bank_full[n % BANKS], 1)
                for n in range(N(("vc", l)) - BANKS + 1, N(("vc", l)) + 1):
                    pe.wait_ge(bank_free[n % BANKS], n // BANKS + 1)
                for i in range(NU + 3):
                    if i < NU:
                        u, n = UNITS[i], N(("S", l, i))
                        lo, hi = u["r"], u["r"] + u["kk"]
                        if n >= BANKS:
                            pe.wait_ge(bank_free[n % BANKS], n // BANKS)
                        if u["kind"] == "cmp":
                            mm(ps(n, 0, 16), qk[lo:hi, u["q"], 0:128], kcT[lo:hi, :], start=True, stop=True)
                            ins = mm(ps(n, 16, 32), qk[lo:hi, u["q"], 128:256], kcT[lo:hi, :], start=True, stop=True)
                        else:
                            ins = mm(ps(n, 0, 128), qk[lo:hi, u["q"], 0:128], qk[lo:hi, u["k"], 0:128], start=True, stop=True)
                            ins = mm(ps(n, 128, 384), qk[lo:hi, u["q"], 128:256], qk[lo:hi, u["k"], :],
                                     start=True, stop=True)
                        ins.then_inc(bank_full[n % BANKS], 1)
                    if i < 24:
                        w, n = W(("ada", l), i), N(("ada", l, i))
                        if l == i == 0:
                            pe.wait_ge(cs_ready, seen(cs_ready))
                        pe.wait_ge(slot_full[w % R], 16 * (w // R + 1))
                        wd = slot(w, KD)
                        if n >= BANKS:
                            pe.wait_ge(bank_free[n % BANKS], n // BANKS)
                        for g in range(2):
                            for k in range(KD):
                                ins = mm(ps(n, 2 * g, 2 * g + 2), wd[:, k, g * P:(g + 1) * P], cs[:, 2 * k:2 * k + 2],
                                         start=(k == 0), stop=(k == KD - 1))
                        ins.then_inc(bank_full[n % BANKS], 1)
                    if 0 <= i - 2 < NU:
                        j = i - 2
                        u, n = UNITS[j], N(("PT", l, j))
                        pe.wait_ge(sb_ready if u["kind"] == "sb" else p_ready, seen(sb_ready if u["kind"] == "sb" else p_ready))
                        if n >= BANKS:
                            pe.wait_ge(bank_free[n % BANKS], n // BANKS)
                        s = sbuf[:, j % 3, :]
                        if u["kind"] == "cmp":
                            for t in range(2):
                                ins = nc.tensor.transpose(bank[n % BANKS][0:16, t * P:(t + 1) * P],
                                                          s[:, 16 * t:16 * t + 16], ident)
                        else:
                            for t in range(3):
                                ins = nc.tensor.transpose(ps(n, t * P, (t + 1) * P), s[:, t * P:(t + 1) * P], ident)
                        ins.then_inc(bank_full[n % BANKS], 1)
                    if 0 <= i - 3 < NU:
                        j = i - 3
                        u, n = UNITS[j], N(("O", l, j))
                        if u["first"]:
                            if n >= BANKS:
                                pe.wait_ge(bank_free[n % BANKS], n // BANKS)
                        pe.wait_ge(bank_free[N(("PT", l, j)) % BANKS], N(("PT", l, j)) // BANKS + 1)
                        pt = ptb[:, j % 2, :]
                        ob = bank[n % BANKS][u["row"]:u["row"] + 64, :]
                        if u["kind"] == "cmp":
                            ins = mm(ob[:, 0:256], vc[0:16, :], pt[0:16, 0:256], start=u["first"], stop=u["last"])
                        else:
                            if u["v"][0] == "vn":
                                v = [vn[:, u["v"][1], t, 64 * u["h"]:64 * u["h"] + 64] for t in range(2)]
                            else:
                                v0 = 0 if u["kind"] == "slc" else 64
                                v = [vsw[:, t, v0:v0 + 64] for t in range(2)]
                            mm(ob[:, 0:256], v[0], pt[:, 0:256], start=u["first"], stop=False)
                            ins = mm(ob[:, 128:256], v[1], pt[:, 256:384], start=False, stop=u["last"])
                        if u["last"]:
                            ins.then_inc(bank_full[n % BANKS], 1)
                n = N(("dfn", l))
                pe.wait_ge(sq_ready, seen(sq_ready))
                if n >= BANKS:
                    pe.wait_ge(bank_free[n % BANKS], n // BANKS)
                mm(ps(n), halves, relu[:, 0, :], start=True, stop=True).then_inc(bank_full[n % BANKS], 1)
                linear(G("out", l))
                sum_squares(N(("rms2", l)), lambda k: act[:, k, :], KD, T, ones)
                for i in range(4):
                    linear(G("up", l, i))
                linear(G("down", l))
            sum_squares(N("rmsf"), lambda k: act[:, k, :], KD, T, ones)

            for i in range(4):
                linear(G("m_up", i))
            pe.wait_ge(silu_ready, seen(silu_ready, MK))
            n = N("m_gates")
            pe.wait_ge(slot_full[(W("m_gates")) % R], 16 * ((W("m_gates")) // R + 1))
            wd = slot(W("m_gates"), MK)
            if n >= BANKS:
                pe.wait_ge(bank_free[n % BANKS], n // BANKS)
            for k in range(MK):
                ins = mm(ps(n), wd[:, k, :], xc[:, k, :], start=(k == 0), stop=(k == MK - 1))
            ins.then_inc(bank_full[n % BANKS], 1)
            pe.wait_ge(rows_ready, seen(rows_ready))
            n = N("m_aT")
            if n >= BANKS:
                pe.wait_ge(bank_free[n % BANKS], n // BANKS)
            for t in range(4):
                ins = nc.tensor.transpose(ps(n, 64 * t, 64 * t + 64), grow[0:64, 5, t * P:(t + 1) * P], ident[0:64, 0:64])
            ins.then_inc(bank_full[n % BANKS], 1)
            for h in range(MH):
                linear(G("m_v", h))
            pe.wait_ge(bank_free[N("m_aT") % BANKS], N("m_aT") // BANKS + 1)
            for h in range(MH):
                for z in range(2):
                    n = N(("m_max", h), z)
                    if n >= BANKS:
                        pe.wait_ge(bank_free[n % BANKS], n // BANKS)
                    r = 32 * z + h
                    mm(ps(n), ident[0:64, r:r + 1].to_broadcast([64, P]), rows[0:64, 0, :], start=True, stop=True).then_inc(bank_full[n % BANKS], 1)
                linear(G("m_qk", h))
                for n in range(N(("m_qk", h)), N(("m_qk", h)) + 4):
                    pe.wait_ge(bank_free[n % BANKS], n // BANKS + 1)
                for st_ in range(4):
                    n = N(("m_QK", h), st_)
                    if n >= BANKS:
                        pe.wait_ge(bank_free[n % BANKS], n // BANKS)
                    for c in range(2):
                        ins = mm(ps(n, 0, T2 - T_AT[st_]), mqk[:, 2 + c, st_ * P:(st_ + 1) * P], mqk[:, c, T_AT[st_]:],
                                 start=(c == 0), stop=(c == 1))
                    ins.then_inc(bank_full[n % BANKS], 1)
                linear(G("m_og", h))
                pe.wait_ge(bank_free[N(("m_QK", h), 3) % BANKS], N(("m_QK", h), 3) // BANKS + 1)
                n = N(("m_den", h))
                if n >= BANKS:
                    pe.wait_ge(bank_free[n % BANKS], n // BANKS)
                for z in range(2):
                    r = 32 * z + h
                    for st_ in range(4):
                        ins = mm(bank[n % BANKS][0:64, T_AT[st_]:T2], con[:, CON("pick") + 63 - r:CON("pick") + 127 - r],
                                 mP[:, z, OFF[st_]:OFF[st_] + T2 - T_AT[st_]], start=(z + st_ == 0), stop=(z == 1 and st_ == 3))
                ins.then_inc(bank_full[n % BANKS], 1)
                pe.wait_ge(rden_ready, seen(rden_ready))
                for z in range(2):
                    n = N(("m_rec", h), z)
                    if n >= BANKS:
                        pe.wait_ge(bank_free[n % BANKS], n // BANKS)
                    r = 32 * z + h
                    mm(ps(n), ident[0:64, r:r + 1].to_broadcast([64, P]), rows[0:64, 2, :], start=True, stop=True).then_inc(bank_full[n % BANKS], 1)
                pe.wait_ge(W_ready, seen(W_ready))
                for e in range(4):
                    n = N(("m_PV", h), e)
                    if n >= BANKS:
                        pe.wait_ge(bank_free[n % BANKS], n // BANKS)
                    for st_ in range(4):
                        ins = mm(ps(n, T_AT[st_], T2), mv[:, st_, h * T2 + e * P:h * T2 + (e + 1) * P],
                                 mP[:, 0, OFF[st_]:OFF[st_] + T2 - T_AT[st_]], start=(st_ == 0), stop=(st_ == 3))
                    ins.then_inc(bank_full[n % BANKS], 1)
                sum_squares(N(("m_rms", h)), lambda k: mqk[:, k, :], 4, T2, ones)
            linear(G("m_out"))

            def layer_norm(i, lo, name):
                pe.wait_ge(bank_free[N(name, KD - 1) % BANKS], N(name, KD - 1) // BANKS + 1)
                n = N(("mean", i))
                if n >= BANKS:
                    pe.wait_ge(bank_free[n % BANKS], n // BANKS)
                for k in range(KD):
                    ins = mm(ps(n, 0, T2 - lo), ones, xT[:, k, lo:], start=(k == 0), stop=(k == KD - 1))
                ins.then_inc(bank_full[n % BANKS], 1)
                sum_squares(N(("var", i)), lambda k: sq2[:, k, lo:], KD, T2 - lo, ones)

            def ffn(l):
                for i in range((NFF // 2, 6)[l]):
                    linear(G("ffn_in", l, i))
                linear(G("ffn_out", l))

            layer_norm(0, 0, "m_out")
            ffn(0)
            layer_norm(1, 0, ("ffn_out", 0))

            linear(G("a_dkv"))
            linear(G("a_dq"))
            sum_squares(N("a_kvn"), lambda k: cks[:, k, :], 2, T2, ones)
            sum_squares(N("a_qn"), lambda k: cks[:, k, 0:T], 3, T, ones)
            linear(G("a_ukv"))
            linear(G("a_v"))
            for i in range(2):
                linear(G("a_uq", i))
            pe.wait_ge(bank_free[N("a_dkv", 2) % BANKS], N("a_dkv", 2) // BANKS + 1)
            for n in range(N("a_v"), N(("aS", 0))):
                pe.wait_ge(bank_free[n % BANKS], n // BANKS + 1)
            for i in range(2 * AH + 4):
                if i < 2 * AH:
                    h, t = i // 2, i % 2
                    n = N(("aS", i))
                    if n >= BANKS:
                        pe.wait_ge(bank_free[n % BANKS], n // BANKS)
                    mm(ps(n), qn[:, h, t * P:(t + 1) * P], kn[:, h, :], start=True, stop=False)
                    mm(ps(n), qr[0:64, h, t * P:(t + 1) * P], krope[0:64, :], start=False, stop=True).then_inc(bank_full[n % BANKS], 1)
                if 0 <= i - 2 < 2 * AH:
                    j = i - 2
                    n = N(("aPT", j))
                    pe.wait_ge(ap_ready, seen(ap_ready))
                    if n >= BANKS:
                        pe.wait_ge(bank_free[n % BANKS], n // BANKS)
                    for t in range(4):
                        ins = nc.tensor.transpose(ps(n, t * P, (t + 1) * P), ap_[:, j % 3, t * P:(t + 1) * P], ident)
                    ins.then_inc(bank_full[n % BANKS], 1)
                if i >= 4 and i % 2 == 0 and (i - 4) // 2 < AH:
                    h = (i - 4) // 2
                    n = N(("aO", h))
                    if n >= BANKS:
                        pe.wait_ge(bank_free[n % BANKS], n // BANKS)
                    pe.wait_ge(bank_free[N(("aPT", 2 * h)) % BANKS], N(("aPT", 2 * h)) // BANKS + 1)
                    pe.wait_ge(bank_free[N(("aPT", 2 * h + 1)) % BANKS], N(("aPT", 2 * h + 1)) // BANKS + 1)
                    for t in range(4):
                        ins = mm(ps(n, 0, T), av[:, t, h * P:(h + 1) * P], apt[:, h % 2, t, :], start=(t == 0), stop=(t == 3))
                    ins.then_inc(bank_full[n % BANKS], 1)
            linear(G("a_out"))
            layer_norm(2, LAT, "a_out")
            ffn(1)
            layer_norm(3, LAT, ("ffn_out", 1))
            pe.wait_ge(ln_ready, seen(ln_ready, 4))
            for t in range(2):
                for c in range(2):
                    n = N("oT", 2 * t + c)
                    if n >= BANKS:
                        pe.wait_ge(bank_free[n % BANKS], n // BANKS)
                    for k in range(4):
                        ins = nc.tensor.transpose(ps(n, k * P, (k + 1) * P), xT[:, 4 * c + k, LAT + t * P:LAT + (t + 1) * P],
                                                  ident)
                    ins.then_inc(bank_full[n % BANKS], 1)

        @block.scalar
        def _(act_):
            seen = Count()
            own = Count()
            do = nc.scalar.activation
            act_.wait_ge(small_ready, 2)
            act_.wait_ge(dma_par, 32)

            fed = {"w": 0, "q": 0}

            def weights_to(s_):
                while fed["w"] <= s_:
                    i = fed["w"]
                    w = ST.split[i][0]
                    act_.wait_ge(slot_full[w % R], 16 * (w // R + 1))
                    if i >= 2:
                        act_.wait_ge(*chunk_end(ST.split[i - 2][1]))
                    do(ws[:, i % 2, 0, :], ring[:, w % R, :], ACT.Copy).then_inc(w_high, 1)
                    fed["w"] += 1

            def feed_to(q_):
                while fed["q"] <= q_:
                    q = fed["q"]
                    g, k, _ = ST.chunks[q]
                    s_ = g.s0 + k // g.kc
                    weights_to(s_)
                    if q >= 2:
                        act_.wait_ge(*chunk_end(q - 2))
                    do(xs[:, q % 2, 0, 0:g.T], source(g, k), ACT.Copy).then_inc(x_high, 1)
                    fed["q"] += 1
                    if (k % g.kc == 1 or k == g.K - 1) and follows(s_):
                        weights_to(s_ + 1)

            def feed(g, more=0):
                feed_to(g.q0 + g.K - 1 + more)

            def squares(dst, src):
                do(dst, src, ACT.Square).then_inc(sq_ready, 1)

            def rstd(n, cols, count):
                act_.wait_ge(bank_full[n % BANKS], n // BANKS + 1)
                do(stat[:, 1, 0:cols], ps(n, 0, cols), ACT.Ln, bias=eps[:, :], scale=1.0 / count).then_inc(bank_free[n % BANKS], 1)
                act_.wait_ge(bank_free[n % BANKS], n // BANKS + 1)
                do(stat[:, 0, 0:cols], stat[:, 1, 0:cols], ACT.Exp, scale=-0.5).then_inc(rstd_ready, 1)

            act_.wait_ge(bank_full[N("bias") % BANKS], N("bias") // BANKS + 1)
            do(relu[0:12, 0, :], bank[N("bias") % BANKS][0:12, :], ACT.Copy).then_inc(bank_free[N("bias") % BANKS], 1)
            for k in range(KD):
                act_.wait_ge(bank_full[N("xT", k) % BANKS], N("xT", k) // BANKS + 1)
                do(xT[:, k, :], ps(N("xT", k)), ACT.Copy).then_inc(bank_free[N("xT", k) % BANKS], 1)
            act_.wait_ge(bank_free[N("xT", KD - 1) % BANKS], N("xT", KD - 1) // BANKS + 1)
            do(cs[:, :], par_at("cond", 0, 16), ACT.Silu).then_inc(cs_ready, 1)
            for l in range(DEPTH):
                if l:
                    act_.wait_ge(bank_free[N(("down", l - 1), KD - 1) % BANKS], N(("down", l - 1), KD - 1) // BANKS + 1)
                squares(act[:, 0:KD, :], xT[:, :, LAT:])
                rstd(N(("rms1", l)), T, D)
                act_.wait_ge(lam_sum, seen(lam_sum))
                do(lam[:, 2:4], lam[:, 0:2], ACT.Exp).then_inc(lam_exp, 1)
                act_.wait_ge(h_ready, 2 * l + 1)
                for i in range(3):
                    g = G("proj", l, i)
                    feed(g, 1)
                    for p in range(g.tickets):
                        n = N(g.name) + p
                        act_.wait_ge(bank_full[n % BANKS], n // BANKS + 1)
                        piece = 8 * i + p
                        if piece < 16:
                            do(qk[:, piece, :], ps(n, 0, T), ACT.Copy).then_inc(bank_free[n % BANKS], 1)
                        else:
                            do(x2[0:64, piece - 16, :], bank[n % BANKS][0:64, 0:T], ACT.Copy)
                            do(x2[64:128, piece - 16, 0:T - 1], bank[n % BANKS][64:128, 1:T], ACT.Copy).then_inc(bank_free[n % BANKS], 1)
                feed(G("nat", l))
                for t in range(2):
                    n = N(("nat", l), 2 * t)
                    act_.wait_ge(bank_full[n % BANKS], n // BANKS + 1)
                    do(vn[:, 0:2, t, :], ps(n).rearrange("p (a b) -> p a b", a=2), ACT.Copy).then_inc(bank_free[n % BANKS], 1)
                    n += 1
                    act_.wait_ge(bank_full[n % BANKS], n // BANKS + 1)
                    do(vn[:, 2, t, :], ps(n, 0, T), ACT.Copy)
                    do(vsw[:, t, :], ps(n, T, T + 140), ACT.Copy).then_inc(bank_free[n % BANKS], 1)
                act_.wait_ge(bank_free[N(("nat", l), 1) % BANKS], N(("nat", l), 1) // BANKS + 1)
                act_.wait_ge(bank_free[N(("nat", l), 3) % BANKS], N(("nat", l), 3) // BANKS + 1)
                do(lam[:, 16:40].rearrange("p (a b) -> p a b", a=2), vsw[:, :, 128:140], ACT.Exp, scale=-1.0
                   ).then_inc(gate_exp, 1)
                for i in range(4):
                    act_.wait_ge(bank_free[N(("hid", l), i) % BANKS], N(("hid", l), i) // BANKS + 1)
                    do(hidg[:, i, :], hid[:, i, :], ACT.Gelu_apprx_tanh, bias=hid[:, i, 15:16]).then_inc(hid_ready, 1)
                n = N(("kc", l))
                act_.wait_ge(bank_full[n % BANKS], n // BANKS + 1)
                do(kcT, ps(n, 0, 16), ACT.Copy).then_inc(bank_free[n % BANKS], 1)
                n = N(("vc", l))
                act_.wait_ge(bank_full[n % BANKS], n // BANKS + 1)
                do(vc[0:16, :], bank[n % BANKS][0:16, 0:64], ACT.Copy).then_inc(bank_free[n % BANKS], 1)
                for i in range(NU + 3):
                    if i < NU:
                        u, s, t = UNITS[i], sbuf[:, i % 3, :], tbuf[:, i % 2, :]
                        act_.wait_ge(logits_ready, seen(logits_ready))
                        if u["kind"] == "sb":
                            do(t, s, ACT.Abs).then_inc(act_own, 1)
                            act_.wait_ge(act_own, own(act_own))
                            do(t, t, ACT.Exp, scale=-1.0).then_inc(act_own, 1)
                            act_.wait_ge(act_own, own(act_own))
                            do(t, t, ACT.Ln, bias=one[:, :]).then_inc(exp_ready, 1)
                        elif u["kind"] == "cmp":
                            do(s[:, 0:16], s[:, 0:16], ACT.Exp, bias=st[:, i, 0:1])
                            do(s[:, 16:32], s[:, 16:32], ACT.Exp, bias=st[:, i, 1:2]).then_inc(exp_ready, 1)
                        else:
                            do(s[:, 0:128], s[:, 0:128], ACT.Exp, bias=st[:, i, 0:1], accum_out=st[:, i, 2:3])
                            do(s[:, 128:384], s[:, 128:384], ACT.Exp, bias=st[:, i, 1:2],
                               accum_out=st[:, i, 3:4]).then_inc(exp_ready, 1)
                    if 0 <= i - 1 < NU and UNITS[i - 1]["kind"] == "sb":
                        s = sbuf[:, (i - 1) % 3, :]
                        act_.wait_ge(arg_ready, seen(arg_ready))
                        do(s, s, ACT.Exp).then_inc(sb_ready, 1)
                    if 0 <= i - 2 < NU:
                        j = i - 2
                        n = N(("PT", l, j))
                        act_.wait_ge(bank_full[n % BANKS], n // BANKS + 1)
                        if UNITS[j]["kind"] == "cmp":
                            do(ptb[0:16, j % 2, 0:256], bank[n % BANKS][0:16, 0:256], ACT.Copy).then_inc(bank_free[n % BANKS], 1)
                        else:
                            do(ptb[:, j % 2, :], ps(n, 0, 384), ACT.Copy).then_inc(bank_free[n % BANKS], 1)
                    if 0 <= i - 3 < NU and UNITS[i - 3]["last"]:
                        u, n = UNITS[i - 3], N(("O", l, i - 3))
                        act_.wait_ge(bank_full[n % BANKS], n // BANKS + 1)
                        half = slice(u["row"], u["row"] + 64)
                        do(mixed[half, u["chunk"], :], bank[n % BANKS][half, 0:T], ACT.Copy).then_inc(bank_free[n % BANKS], 1)
                act_.wait_ge(bank_free[N(("O", l, NU - 1)) % BANKS], N(("O", l, NU - 1)) // BANKS + 1)
                squares(relu[:, 0, :].rearrange("p (a b) -> p a b", a=2), mixed[:, 6:8, :])
                rstd(N(("dfn", l)), 512, HD)
                act_.wait_ge(dfn_ready, l + 1)
                feed(G("out", l))
                act_.wait_ge(bank_free[N(("out", l), KD - 1) % BANKS], N(("out", l), KD - 1) // BANKS + 1)
                squares(act[:, 0:KD, :], xT[:, :, LAT:])
                rstd(N(("rms2", l)), T, D)
                act_.wait_ge(h_ready, 2 * l + 2)
                for i in range(4):
                    g = G("up", l, i)
                    feed(g, int(i < 3))
                    for p in range(8):
                        n = N(g.name) + p
                        act_.wait_ge(bank_full[n % BANKS], n // BANKS + 1)
                        if 8 * i + p >= 4:
                            act_.wait_ge(act_ready, seen(act_ready))
                        do(relu[:, (p % 4) // 2, (p % 2) * T:(p % 2 + 1) * T], ps(n, 0, T), ACT.Relu).then_inc(bank_free[n % BANKS], 1)
                act_.wait_ge(act_ready, seen(act_ready, 4))
                feed(G("down", l))
            act_.wait_ge(bank_free[N(("down", DEPTH - 1), KD - 1) % BANKS], N(("down", DEPTH - 1), KD - 1) // BANKS + 1)
            squares(act[:, 0:KD, :], xT[:, :, LAT:])
            rstd(N("rmsf"), T, D)

            act_.wait_ge(h_ready, 2 * DEPTH + 2)
            for i in range(4):
                feed(G("m_up", i), int(i < 3))
                for p in range(4):
                    j = 4 * i + p
                    n = N(("m_up", i), p)
                    act_.wait_ge(bank_full[n % BANKS], n // BANKS + 1)
                    do(xm[:, j, :], ps(n), ACT.Copy).then_inc(bank_free[n % BANKS], 1)
                    if j:
                        act_.wait_ge(conv_ready, seen(conv_ready))
                        do(xc[:, j - 1, :], mqk[:, (j - 1) % 4, :], ACT.Silu).then_inc(silu_ready, 1)
                    if p == 1 and i < 3:
                        feed(G("m_up", i), 2)
            act_.wait_ge(conv_ready, seen(conv_ready))
            do(xc[:, MK - 1, :], mqk[:, (MK - 1) % 4, :], ACT.Silu).then_inc(silu_ready, 1)
            act_.wait_ge(bank_free[N("m_gates") % BANKS], N("m_gates") // BANKS + 1)
            do(grow[64:128, 1, :], grow[64:128, 0, :], ACT.Abs).then_inc(act_own, 1)
            act_.wait_ge(act_own, own(act_own))
            do(grow[64:128, 1, :], grow[64:128, 1, :], ACT.Exp, scale=-1.0).then_inc(act_own, 1)
            act_.wait_ge(act_own, own(act_own))
            do(grow[64:128, 1, :], grow[64:128, 1, :], ACT.Ln, bias=one[64:128, :]).then_inc(lng_ready, 1)
            act_.wait_ge(rows_ready, seen(rows_ready))
            do(rows[0:64, 1, :], rows[0:64, 1, :], ACT.Exp, scale=-1.0).then_inc(floor_ready, 1)
            n = N("m_aT")
            act_.wait_ge(bank_full[n % BANKS], n // BANKS + 1)
            do(aT.rearrange("p a b -> p (a b)"), ps(n, 0, 256), ACT.Copy).then_inc(bank_free[n % BANKS], 1)
            for h in range(MH):
                feed(G("m_v", h), 1)
                for t in range(4):
                    n = N(("m_v", h), t)
                    act_.wait_ge(bank_full[n % BANKS], n // BANKS + 1)
                    do(mv[:, t, h * T2:(h + 1) * T2], ps(n), ACT.Copy).then_inc(bank_free[n % BANKS], 1)
                    if t == 1:
                        feed(G("m_v", h), 2)
            for h in range(MH):
                g = G("m_qk", h)
                for z, spans in enumerate((((0, 512), (640, 1280), (1408, 1536)), ((0, 128), (256, 1152), (1280, 1536)))):
                    feed_to(g.q0 + 5 + 5 * z)
                    act_.wait_ge(D_ready, seen(D_ready))
                    for lo, hi in spans:
                        ins = do(mP[:, z, lo:hi], mP[:, z, lo:hi], ACT.Exp, scale=-1.0)
                    ins.then_inc(E_ready, 1)
                feed(g, 2)
                for j in range(4):
                    n = N(("m_qk", h), j)
                    act_.wait_ge(bank_full[n % BANKS], n // BANKS + 1)
                    (do(mqk[:, j, :], ps(n), ACT.Copy, scale=1.0 if j < 2 else 1.0 / 16)).then_inc(bank_free[n % BANKS], 1)
                feed(G("m_og", h), int(h < 3))
                for j in range(4):
                    n = N(("m_og", h), j)
                    act_.wait_ge(bank_full[n % BANKS], n // BANKS + 1)
                    do(og[:, j, :], ps(n), ACT.Sigmoid).then_inc(bank_free[n % BANKS], 1)
                act_.wait_ge(bank_free[N(("m_PV", h), 3) % BANKS], N(("m_PV", h), 3) // BANKS + 1)
                do(mqk.rearrange("p a b -> p (a b)"), hs[:, 4 * h:4 * h + 4, :].rearrange("p a b -> p (a b)"), ACT.Square
                   ).then_inc(sq_ready, 1)
                rstd(N(("m_rms", h)), T2, T2)
            act_.wait_ge(hs_ready, MH)
            feed(G("m_out"))

            def layer_norm(i, lo):
                act_.wait_ge(bank_free[N(("mean", i)) % BANKS], N(("mean", i)) // BANKS + 1)
                do(sq2[:, :, lo:], xT[:, :, lo:], ACT.Square).then_inc(sq_ready, 1)
                rstd(N(("var", i)), T2 - lo, D)

            def ffn(l, lo):
                groups, per = ((NFF // 2, 2), (6, 4))[l]
                act_.wait_ge(h_ready, (2 * DEPTH + 3, 2 * DEPTH + 5)[l])
                for i in range(groups):
                    g = G("ffn_in", l, i)
                    more = int(i < groups - 1)
                    feed(g, more)
                    for p in range(g.tickets // 2):
                        act_.wait_ge(conv_ready, seen(conv_ready))
                        c = ctmp[:, (per * i + p) % 4, lo:]
                        do(c, c, ACT.Silu).then_inc(bank_free[(N(g.name) + 2 * p) % BANKS], 1)
                        if p == 0 and l == 0:
                            feed(g, 2 * more)
                act_.wait_ge(ffa_ready, l + 1)
                feed(G("ffn_out", l))

            layer_norm(0, 0)
            ffn(0, 0)
            layer_norm(1, 0)

            act_.wait_ge(h_ready, 2 * DEPTH + 4)
            feed(G("a_dkv"), 2)
            for j in range(2):
                n = N("a_dkv", j)
                act_.wait_ge(bank_full[n % BANKS], n // BANKS + 1)
                do(ckv[:, j, :], ps(n), ACT.Copy).then_inc(bank_free[n % BANKS], 1)
            act_.wait_ge(bank_free[n % BANKS], n // BANKS + 1)
            do(cks[:, 0:2, :], ckv, ACT.Square).then_inc(sq_ready, 1)
            feed(G("a_dq"))
            for j in range(3):
                n = N("a_dq", j)
                act_.wait_ge(bank_full[n % BANKS], n // BANKS + 1)
                do(cq[:, j, :], ps(n, 0, T), ACT.Copy).then_inc(bank_free[n % BANKS], 1)
            act_.wait_ge(bank_free[n % BANKS], n // BANKS + 1)
            rstd(N("a_kvn"), T2, T2 // 2)
            do(cks[:, :, 0:T], cq, ACT.Square).then_inc(sq_ready, 1)
            act_.wait_ge(ckn_ready, 1)
            rstd(N("a_qn"), T, 384)
            feed(G("a_ukv"), 1)
            for h in range(AH):
                n = N("a_ukv", h)
                act_.wait_ge(bank_full[n % BANKS], n // BANKS + 1)
                do(kn[:, h, :], ps(n), ACT.Copy).then_inc(bank_free[n % BANKS], 1)
            act_.wait_ge(ckn_ready, 2)
            feed(G("a_v"), 1)
            for t in range(4):
                for c in range(2):
                    n = N("a_v", 2 * t + c)
                    act_.wait_ge(bank_full[n % BANKS], n // BANKS + 1)
                    do(av[:, t, c * T2:(c + 1) * T2], ps(n), ACT.Copy).then_inc(bank_free[n % BANKS], 1)
            feed(G("a_uq", 0), 1)
            for h in range(AH):
                n = N(("a_uq", 0), h)
                act_.wait_ge(bank_full[n % BANKS], n // BANKS + 1)
                do(qn[:, h, :], ps(n, 0, T), ACT.Copy).then_inc(bank_free[n % BANKS], 1)
            feed(G("a_uq", 1))
            for i in range(2 * AH + 4):
                if i < 2 * AH:
                    n = N(("aS", i))
                    act_.wait_ge(amax_ready, seen(amax_ready))
                    do(ap_[:, i % 3, :], ps(n), ACT.Exp, bias=ast[:, i, 1:2], scale=A_SCALE,
                               accum_out=ast[:, i, 2:3]).then_inc(bank_free[n % BANKS], 1)
                if 0 <= i - 2 < 2 * AH:
                    j = i - 2
                    n = N(("aPT", j))
                    act_.wait_ge(bank_full[n % BANKS], n // BANKS + 1)
                    do(apt[:, (j // 2) % 2, :, (j % 2) * P:(j % 2 + 1) * P], ps(n).rearrange("p (a b) -> p a b", a=4),
                               ACT.Copy).then_inc(bank_free[n % BANKS], 1)
                if i >= 4 and i % 2 == 0 and (i - 4) // 2 < AH:
                    h = (i - 4) // 2
                    n = N(("aO", h))
                    act_.wait_ge(bank_full[n % BANKS], n // BANKS + 1)
                    do(aoT[:, h, :], ps(n, 0, T), ACT.Copy).then_inc(bank_free[n % BANKS], 1)
            act_.wait_ge(bank_free[N(("aO", AH - 1)) % BANKS], N(("aO", AH - 1)) // BANKS + 1)
            feed(G("a_out"))
            layer_norm(2, LAT)
            ffn(1, LAT)
            layer_norm(3, LAT)
            for t in range(2):
                for c in range(2):
                    n = N("oT", 2 * t + c)
                    act_.wait_ge(bank_full[n % BANKS], n // BANKS + 1)
                    ins = do(osb[:, t, c * T2:(c + 1) * T2], ps(n), ACT.Copy)
            ins.then_inc(out_copied, 1)

        @block.vector
        def _(dve):
            seen = Count()
            own = Count()
            v = nc.vector
            stt = v.scalar_tensor_tensor

            fed = {"w": 0, "q": 0}

            def weights_to(s_):
                while fed["w"] <= s_:
                    i = fed["w"]
                    w = ST.split[i][0]
                    dve.wait_ge(w_high, i + 1)
                    v.tensor_tensor(ws[:, i % 2, 1, :], ring[:, w % R, :], ws[:, i % 2, 0, :].bitcast(F32), ALU.subtract
                                    ).then_inc(slot_done, 1)
                    fed["w"] += 1

            def feed_to(q_):
                while fed["q"] <= q_:
                    q = fed["q"]
                    g, k, _ = ST.chunks[q]
                    s_ = g.s0 + k // g.kc
                    weights_to(s_)
                    dve.wait_ge(x_high, q + 1)
                    v.tensor_tensor(xs[:, q % 2, 1, 0:g.T], source(g, k), xs[:, q % 2, 0, 0:g.T].bitcast(F32),
                                    ALU.subtract).then_inc(x_done, 1)
                    fed["q"] += 1
                    if (k % g.kc == 1 or k == g.K - 1) and follows(s_):
                        weights_to(s_ + 1)

            def feed(g, more=0):
                feed_to(g.q0 + g.K - 1 + more)

            def normed(dst, gain, chunks, cols=LAT):
                dve.wait_ge(rstd_ready, seen(rstd_ready))
                for k in range(chunks):
                    ins = stt(dst(k), xT[:, k, cols:], par_at(gain, k), stat[:, 0, 0:T2 - cols], ALU.mult, ALU.mult)
                ins.then_inc(h_ready, 1)
                dve.wait_ge(h_ready, own(h_ready))

            v.memset(eps[:, :], EPS).then_inc(small_ready, 1)
            v.memset(one[:, :], 1.0).then_inc(small_ready, 1)
            v.memset(cbias, NEG).then_inc(dve_own, 1)
            dve.wait_ge(dve_own, own(dve_own))
            dve.wait_ge(dma_par, 32)
            dve.wait_ge(dma_con, 16)
            for l in range(DEPTH):
                lam_init = 0.8 - 0.6 * math.exp(-0.3 * l)
                dl = par1_at(("dlam", l), 0, 128).rearrange("p (a b c) -> p a b c", a=2, b=2)
                prod = lamp.rearrange("p (a c) -> p a c", a=2)
                v.tensor_tensor(prod, dl[:, :, 0, :], dl[:, :, 1, :], ALU.mult).then_inc(dve_own, 1)
                dve.wait_ge(dve_own, own(dve_own))
                v.tensor_reduce(lam[:, 0:2], prod, AX, ALU.add).then_inc(lam_sum, 1)
                normed(lambda k: hT[:, k, LAT:], ("g_attn", l), KD)
                dve.wait_ge(lam_exp, seen(lam_exp))
                v.tensor_tensor(lam[:, 4:5], lam[:, 3:4], lam[:, 2:3], ALU.subtract).then_inc(dve_own, 1)
                dve.wait_ge(dve_own, own(dve_own))
                v.tensor_scalar(lam[:, 5:6], lam[:, 4:5], -lam_init, None, ALU.add).then_inc(dve_own, 1)
                dve.wait_ge(dve_own, own(dve_own))
                v.tensor_scalar(lam[:, 6:7], par_at(("subln", l)), 1.0 - lam_init, None, ALU.mult).then_inc(dve_own, 1)
                dve.wait_ge(dve_own, own(dve_own))
                for i in range(3):
                    feed(G("proj", l, i), 1)
                dve.wait_ge(bank_free[N(("proj", l, 2)) % BANKS], N(("proj", l, 2)) // BANKS + 1)
                dve.wait_ge(bank_free[N(("proj", l, 2), 1) % BANKS], N(("proj", l, 2), 1) // BANKS + 1)
                for b in range(2):
                    xv = x2[:, b, :].rearrange("p (c j e) -> p e j c", j=8, e=2)
                    v.tensor_copy(x3[:, b, 0:8, 0:CMP_N], xv[:, 0, :, 0:15])
                    v.tensor_copy(x3[:, b, 8:16, 0:CMP_N], xv[:, 0, :, 1:16])
                    ins = v.tensor_copy(x3[:, b, :, 15], par1_at(("pos", l), 16 * b, 16))
                ins.then_inc(x3_ready, 1)
                feed(G("nat", l))
                for i in range(4):
                    n = N(("hid", l), i)
                    dve.wait_ge(bank_full[n % BANKS], n // BANKS + 1)
                    v.tensor_copy(hid[:, i, 0:8], ps(n, 0, 8)).then_inc(slot_done, 1)
                    v.tensor_copy(hid[:, i, 8:16], ps(n, 8, 16)).then_inc(bank_free[n % BANKS], 1)
                dve.wait_ge(gate_exp, seen(gate_exp))
                v.tensor_scalar(lam[:, 16:40], lam[:, 16:40], 1.0, None, ALU.add).then_inc(dve_own, 1)
                dve.wait_ge(dve_own, own(dve_own))
                v.reciprocal(lam[:, 16:40], lam[:, 16:40]).then_inc(dve_own, 1)
                dve.wait_ge(dve_own, own(dve_own))
                gates = lam[:, 16:40].rearrange("p (a b) -> p a b", a=2)
                if l == 0:
                    dve.wait_ge(dma_bias, 32)
                    v.tensor_copy(bias[:, :, 0:128], hankel[:, :, 0:128][:, :, ::-1])
                    v.tensor_copy(bias[:, :, 128:384], hankel[:, :, ::-1])
                    for q in range(2):
                        ins = v.tensor_copy(cbias[:, :, 16 * q:16 * q + CMP_N], tz[:, :, P * q:P * q + 225:16][:, :, ::-1])
                    ins.then_inc(dve_own, 1)
                    dve.wait_ge(dve_own, own(dve_own))
                for i in range(NU + 1):
                    if i < NU:
                        u, s, n = UNITS[i], sbuf[:, i % 3, :], N(("S", l, i))
                    if 1 <= i < 25:
                        n = N(("ada", l, i - 1))
                        dve.wait_ge(bank_full[n % BANKS], n // BANKS + 1)
                        for g in range(2):
                            piece = 2 * (i - 1) + g
                            plus = 1.0 if 8 <= piece < 16 or 32 <= piece < 40 else 0.0
                            ins = v.tensor_scalar(mod[:, l, 2 * piece:2 * piece + 2], ps(n, 2 * g, 2 * g + 2),
                                                  par_at(("ada_b", l), piece), plus, ALU.add, ALU.add)
                            if g == 0:
                                ins.then_inc(slot_done, 1)
                        ins.then_inc(bank_free[n % BANKS], 1)
                    if i < NU:
                        n = N(("S", l, i))
                        scale = u["kk"] ** -0.5
                        dve.wait_ge(bank_full[n % BANKS], n // BANKS + 1)
                        if u["kind"] == "sb":
                            stt(s, ps(n, 0, 384), scale, par1_at("strict", 0, 384), ALU.mult, ALU.add).then_inc(bank_free[n % BANKS], 1)
                            dve.wait_ge(bank_free[n % BANKS], n // BANKS + 1)
                            v.tensor_scalar(tbuf[:, 2 + i % 2, :], s, 0.0, None, ALU.max).then_inc(logits_ready, 1)
                        elif u["kind"] == "cmp":
                            stt(s[:, 0:32], ps(n, 0, 32), scale, cbias[:, u["h"], :], ALU.mult, ALU.add).then_inc(bank_free[n % BANKS], 1)
                            dve.wait_ge(bank_free[n % BANKS], n // BANKS + 1)
                            v.tensor_reduce(st[:, i, 0:2], s[:, 0:32].rearrange("p (a b) -> p a b", a=2), AX, ALU.max,
                                            negate=True).then_inc(logits_ready, 1)
                        else:
                            stt(s, ps(n, 0, 384), scale, bias[:, u["bias"], :], ALU.mult, ALU.add).then_inc(bank_free[n % BANKS], 1)
                            dve.wait_ge(bank_free[n % BANKS], n // BANKS + 1)
                            v.tensor_reduce(st[:, i, 0:1], s[:, 0:128], AX, ALU.max, negate=True)
                            v.tensor_reduce(st[:, i, 1:2], s[:, 128:384], AX, ALU.max, negate=True
                                            ).then_inc(logits_ready, 1)
                    if i >= 1:
                        j = i - 1
                        u, s = UNITS[j], sbuf[:, j % 3, :]
                        dve.wait_ge(exp_ready, seen(exp_ready))
                        if u["kind"] == "sb":
                            t, m = tbuf[:, j % 2, :], tbuf[:, 2 + j % 2, :]
                            for lo, hi in ((0, 128), (128, 384)):
                                ins = v.tensor_tensor_scan(t[:, lo:hi][:, ::-1], m[:, lo:hi][:, ::-1],
                                                           t[:, lo:hi][:, ::-1], 0.0, ALU.add, ALU.add)
                            ins.then_inc(dve_own, 1)
                            dve.wait_ge(dve_own, own(dve_own))
                            v.tensor_tensor(s, s, t, ALU.subtract).then_inc(arg_ready, 1)
                            continue
                        w = 128
                        if u["kind"] == "cmp":
                            w = 16
                            v.tensor_tensor(s[:, 0:32], s[:, 0:32], par1_at("cmask", 0, 32), ALU.mult).then_inc(dve_own, 1)
                            dve.wait_ge(dve_own, own(dve_own))
                            v.tensor_reduce(st[:, j, 2:4], s[:, 0:32].rearrange("p (a b) -> p a b", a=2), AX,
                                                     ALU.add).then_inc(dve_own, 1)
                            dve.wait_ge(dve_own, own(dve_own))
                            v.tensor_scalar(st[:, j, 2:4], st[:, j, 2:4], 1e-30, None, ALU.max).then_inc(dve_own, 1)
                            dve.wait_ge(dve_own, own(dve_own))
                        v.reciprocal(st[:, j, 4:6], st[:, j, 2:4]).then_inc(dve_own, 1)
                        dve.wait_ge(dve_own, own(dve_own))
                        if "gate" in u:
                            v.tensor_tensor(st[:, j, 4:6], st[:, j, 4:6], gates[:, :, u["gate"]], ALU.mult).then_inc(dve_own, 1)
                            dve.wait_ge(dve_own, own(dve_own))
                        if u.get("c"):
                            v.tensor_scalar(st[:, j, 4:6], st[:, j, 4:6], lam[:, 5:6], None, ALU.mult).then_inc(dve_own, 1)
                            dve.wait_ge(dve_own, own(dve_own))
                        end = 32 if u["kind"] == "cmp" else 384
                        v.tensor_scalar(s[:, 0:w], s[:, 0:w], st[:, j, 4:5], None, ALU.mult)
                        v.tensor_scalar(s[:, w:end], s[:, w:end], st[:, j, 5:6], None, ALU.mult).then_inc(p_ready, 1)
                dve.wait_ge(rstd_ready, seen(rstd_ready))
                m = mixed[:, 6:8, :]
                stt(m, m, lam[:, 6:7], stat[:, 0, :].rearrange("p (a b) -> p a b", a=2), ALU.mult, ALU.mult).then_inc(dfn_ready, 1)
                dve.wait_ge(dfn_ready, own(dfn_ready))
                for n in range(N(("O", l, NU - 1)) - BANKS + 1, N(("O", l, NU - 1)) + 1):
                    dve.wait_ge(bank_free[n % BANKS], n // BANKS + 1)
                feed(G("out", l))

                def residual(name):
                    for g in range(KD):
                        n = N((name, l), g)
                        dve.wait_ge(bank_full[n % BANKS], n // BANKS + 1)
                        v.tensor_tensor(xT[:, g, LAT:], xT[:, g, LAT:], ps(n, 0, T), ALU.add).then_inc(bank_free[n % BANKS], 1)

                residual("out")
                normed(lambda k: hT[:, k, LAT:], ("g_mlp", l), KD)
                for i in range(4):
                    g = G("up", l, i)
                    feed(g, int(i < 3))
                    for p in range(8):
                        dve.wait_ge(bank_free[(N(g.name) + p) % BANKS], (N(g.name) + p) // BANKS + 1)
                        r = relu[:, (p % 4) // 2, (p % 2) * T:(p % 2 + 1) * T]
                        ins = v.tensor_tensor(act[:, 8 * i + p, :], r, r, ALU.mult)
                        if i == 3 and p == 7:
                            ins.then_inc(act_ready, 1)
                            dve.wait_ge(act_ready, own(act_ready))
                        else:
                            own(act_ready)
                            ins.then_inc(act_ready, 1)
                feed(G("down", l))
                residual("down")
            normed(lambda k: xT[:, k, LAT:], "g_final", KD)

            def mod_at(l, part, k, seg):
                c = 2 * (KD * part + k) + 1 - seg
                return mod[:, l, c:c + 1]

            def modulate(l, part, segs=(0, 1)):
                for k in range(KD):
                    for seg in segs:
                        t = slice(seg * T, seg * T + T)
                        ins = v.tensor_scalar(hT[:, k, t], xT[:, k, t], mod_at(l, part + 1, k, seg), mod_at(l, part, k, seg),
                                              ALU.mult, ALU.add)
                ins.then_inc(h_ready, 1)
                dve.wait_ge(h_ready, own(h_ready))
                for k in range(KD):
                    ins = v.tensor_scalar(xT[:, k, segs[0] * T:], xT[:, k, segs[0] * T:], ALPHA, None, ALU.mult)
                ins.then_inc(dve_own, 1)
                dve.wait_ge(dve_own, own(dve_own))

            def conv(dst, src, w, b, segs, lo=0):
                v.tensor_scalar(dst, src, w[:, 1:2], b, ALU.mult, ALU.add).then_inc(dve_own, 1)
                dve.wait_ge(dve_own, own(dve_own))
                d3, s3 = (a.rearrange("p (a b) -> p a b", a=segs) for a in (dst, src))
                stt(d3[:, :, 1:T], s3[:, :, 0:T - 1], w[:, 0:1], d3[:, :, 1:T], ALU.mult, ALU.add).then_inc(dve_own, 1)
                dve.wait_ge(dve_own, own(dve_own))
                return stt(d3[:, :, 0:T - 1], s3[:, :, 1:T], w[:, 2:3], d3[:, :, 0:T - 1], ALU.mult, ALU.add)

            modulate(0, 0)
            for i in range(4):
                feed(G("m_up", i), int(i < 3))
                for p in range(4):
                    j = 4 * i + p
                    dve.wait_ge(bank_free[N(("m_up", i), p) % BANKS], N(("m_up", i), p) // BANKS + 1)
                    if j >= 4:
                        dve.wait_ge(silu_ready, seen(silu_ready))
                    conv(mqk[:, j % 4, :], xm[:, j, :], par_at("mconv_w", 3 * j, 3), par_at("mconv_b", j), 2
                         ).then_inc(conv_ready, 1)
                    if p == 1 and i < 3:
                        feed(G("m_up", i), 2)
            dve.wait_ge(silu_ready, seen(silu_ready, 4))
            n = N("m_gates")
            dve.wait_ge(bank_full[n % BANKS], n // BANKS + 1)
            v.tensor_scalar(grow[0:64, 0, :], bank[n % BANKS][0:64, :], par_at("b_gates")[0:64, :], None, ALU.add
                            ).then_inc(slot_done, 1)
            v.tensor_scalar(grow[64:128, 0, :], bank[n % BANKS][64:128, :], par_at("b_gates")[64:128, :], None,
                                    ALU.add).then_inc(bank_free[n % BANKS], 1)
            dve.wait_ge(bank_free[n % BANKS], n // BANKS + 1)
            v.tensor_scalar(grow[64:128, 2, :], grow[64:128, 0, :], 0.0, None, ALU.min).then_inc(dve_own, 1)
            dve.wait_ge(dve_own, own(dve_own))
            dve.wait_ge(lng_ready, seen(lng_ready))

            def both_ways(dst, a, b, base, op0, op1):
                f = slice(base, base + 32)
                g = slice(base + 32, base + 64)
                v.tensor_tensor_scan(dst[f, :], a[f, :], b[f, :], 0.0, op0, op1)
                v.tensor_tensor_scan(dst[g, 0:T][:, ::-1], a[g, 0:T][:, ::-1], b[g, 0:T][:, ::-1], 0.0, op0, op1).then_inc(dve_own, 1)
                dve.wait_ge(dve_own, own(dve_own))
                v.tensor_tensor_scan(dst[g, T:T2][:, ::-1], a[g, T:T2][:, ::-1], b[g, T:T2][:, ::-1], dst[g, 0:1],
                                              op0, op1).then_inc(dve_own, 1)
                dve.wait_ge(dve_own, own(dve_own))

            both_ways(grow[:, 3, :], grow[:, 2, :], grow[:, 1, :], 64, ALU.add, ALU.subtract)
            v.tensor_copy(grow[0:64, 4, :], grow[64:128, 3, :]).then_inc(dve_own, 1)
            dve.wait_ge(dve_own, own(dve_own))
            v.tensor_tensor(grow[0:64, 5, :], grow[0:64, 0, :], grow[0:64, 4, :], ALU.subtract).then_inc(dve_own, 1)
            dve.wait_ge(dve_own, own(dve_own))
            both_ways(rows[:, 0, :], grow[:, 5, :], grow[:, 5, :], 0, ALU.max, ALU.max)
            v.tensor_tensor(rows[0:64, 1, :], grow[0:64, 4, :], rows[0:64, 0, :], ALU.add).then_inc(rows_ready, 1)
            dve.wait_ge(floor_ready, seen(floor_ready))
            dve.wait_ge(bank_free[N("m_aT") % BANKS], N("m_aT") // BANKS + 1)
            v.memset(mP[:, 1, 128:256], 0.0)
            v.memset(mP[:, 1, 1152:1280], 0.0).then_inc(dve_own, 1)
            dve.wait_ge(dve_own, own(dve_own))
            for h in range(MH):
                feed(G("m_v", h), 2)
            spans = (((0, 512), (128, 512), (256, 512), (384, 512)), ((0, 512), (0, 512), (256, 384), (256, 512)))
            for h in range(MH):
                g = G("m_qk", h)
                feed_to(g.q0 + 1)
                v.memset(mP[:, 0, 512:640], 0.0)
                v.memset(mP[:, 0, 1280:1408], 0.0).then_inc(dve_own, 1)
                dve.wait_ge(dve_own, own(dve_own))
                for z in range(2):
                    feed_to(g.q0 + 3 + 5 * z)
                    n = N(("m_max", h), z)
                    dve.wait_ge(bank_full[n % BANKS], n // BANKS + 1)
                    r = 32 * z + h
                    for s_ in range(4):
                        parts = [spans[z][s_]] if (z, s_) != (1, 0) else [(0, 128), (256, 512)]
                        for lo, hi in parts:
                            ins = v.tensor_scalar(mP[:, z, OFF[s_] + lo - T_AT[s_]:OFF[s_] + hi - T_AT[s_]], ps(n, lo, hi),
                                                  aT[:, s_, r:r + 1], 0.0, ALU.subtract, ALU.max)
                    ins.then_inc(bank_free[n % BANKS], 1)
                    dve.wait_ge(bank_free[n % BANKS], n // BANKS + 1)
                    for s_ in range(4):
                        d = OFF[s_] + s_ * P - T_AT[s_]
                        ins = v.tensor_tensor(mP[:, z, d:d + P], mP[:, z, d:d + P], con_at("tri", 256)[:, z * P:(z + 1) * P],
                                              ALU.max)
                    ins.then_inc(D_ready, 1)
                feed(g, 2)
                for z in range(2):
                    dve.wait_ge(E_ready, seen(E_ready))
                    for s_ in range(4):
                        n = N(("m_QK", h), s_)
                        if z == 0:
                            dve.wait_ge(bank_full[n % BANKS], n // BANKS + 1)
                        p_ = mP[:, z, OFF[s_]:OFF[s_] + T2 - T_AT[s_]]
                        ins = v.tensor_tensor(p_, p_, ps(n, 0, T2 - T_AT[s_]), ALU.mult)
                        if z == 1:
                            ins.then_inc(bank_free[n % BANKS], 1)
                dve.wait_ge(bank_free[n % BANKS], n // BANKS + 1)
                feed(G("m_og", h), int(h < 3))
                n = N(("m_den", h))
                dve.wait_ge(bank_full[n % BANKS], n // BANKS + 1)
                dn = bank[n % BANKS][0:64, :]
                stt(rows[0:64, 2, :], dn, -1.0, rows[0:64, 1, :], ALU.mult, ALU.max).then_inc(dve_own, 1)
                dve.wait_ge(dve_own, own(dve_own))
                v.tensor_tensor(rows[0:64, 2, :], dn, rows[0:64, 2, :], ALU.max).then_inc(bank_free[n % BANKS], 1)
                dve.wait_ge(bank_free[n % BANKS], n // BANKS + 1)
                v.reciprocal(rows[0:64, 2, :], rows[0:64, 2, :]).then_inc(rden_ready, 1)
                for z in range(2):
                    n = N(("m_rec", h), z)
                    dve.wait_ge(bank_full[n % BANKS], n // BANKS + 1)
                    for s_ in range(4):
                        p_ = mP[:, z, OFF[s_]:OFF[s_] + T2 - T_AT[s_]]
                        ins = v.tensor_tensor(p_, p_, ps(n, T_AT[s_], T2), ALU.mult)
                    ins.then_inc(bank_free[n % BANKS], 1)
                dve.wait_ge(bank_free[n % BANKS], n // BANKS + 1)
                v.tensor_tensor(mP[:, 0, :], mP[:, 0, :], mP[:, 1, :], ALU.add).then_inc(W_ready, 1)
                for e in range(4):
                    n = N(("m_PV", h), e)
                    dve.wait_ge(bank_full[n % BANKS], n // BANKS + 1)
                    dve.wait_ge(bank_free[N(("m_og", h), e) % BANKS], N(("m_og", h), e) // BANKS + 1)
                    v.tensor_tensor(hs[:, 4 * h + e, :], ps(n), og[:, e, :], ALU.mult).then_inc(bank_free[n % BANKS], 1)
                dve.wait_ge(rstd_ready, seen(rstd_ready))
                for e in range(4):
                    k = 4 * h + e
                    ins = stt(hs[:, k, :], hs[:, k, :], par_at("m_norm", k), stat[:, 0, :], ALU.mult, ALU.mult)
                ins.then_inc(hs_ready, 1)
                dve.wait_ge(hs_ready, own(hs_ready))

            def residual2(name, l, part, segs):
                feed(G(*name) if isinstance(name, tuple) else G(name))
                for g in range(KD):
                    n = N(name, g)
                    dve.wait_ge(bank_full[n % BANKS], n // BANKS + 1)
                    for seg in segs:
                        t = slice(seg * T, seg * T + T)
                        ins = stt(xT[:, g, t], ps(n, (seg - segs[0]) * T, (seg - segs[0] + 1) * T), mod_at(l, part, g, seg),
                                  xT[:, g, t], ALU.mult, ALU.add)
                    ins.then_inc(bank_free[n % BANKS], 1)
                dve.wait_ge(bank_free[n % BANKS], n // BANKS + 1)

            def layer_norm(i, l, s_, lo):
                n = N(("mean", i))
                dve.wait_ge(bank_full[n % BANKS], n // BANKS + 1)
                for k in range(KD):
                    ins = stt(xT[:, k, lo:], ps(n, 0, T2 - lo), -1.0 / D, xT[:, k, lo:], ALU.mult, ALU.add)
                ins.then_inc(bank_free[n % BANKS], 1)
                dve.wait_ge(bank_free[n % BANKS], n // BANKS + 1)
                dve.wait_ge(rstd_ready, seen(rstd_ready))
                for k in range(KD):
                    ins = stt(xT[:, k, lo:], xT[:, k, lo:], par_at(("ln_g", l, s_), k), stat[:, 0, 0:T2 - lo], ALU.mult, ALU.mult)
                ins.then_inc(dve_own, 1)
                dve.wait_ge(dve_own, own(dve_own))
                for k in range(KD):
                    ins = v.tensor_scalar(xT[:, k, lo:], xT[:, k, lo:], par_at(("ln_b", l, s_), k), None, ALU.add)
                ins.then_inc(ln_ready, 1)
                dve.wait_ge(ln_ready, own(ln_ready))

            def ffn(l, segs):
                lo, cols = segs[0] * T, len(segs) * T
                groups = (NFF // 2, 6)[l]
                for i in range(groups):
                    g = G("ffn_in", l, i)
                    more = int(i < groups - 1)
                    feed(g, more)
                    pairs = g.tickets // 2
                    for p in range(pairs + 1):
                        if p < pairs:
                            n = N(g.name) + 2 * p
                            j = (2, 4)[l] * i + p
                            dve.wait_ge(bank_full[n % BANKS], n // BANKS + 1)
                            conv(ctmp[:, j % 4, lo:], ps(n, 0, cols), par_at(("fconv_w", l), 3 * j, 3),
                                 par_at(("fconv_b", l), j), len(segs)).then_inc(conv_ready, 1)
                            if p == 0 and l == 0:
                                feed(g, 2 * more)
                        if p:
                            n = N(g.name) + 2 * (p - 1)
                            j = (2, 4)[l] * i + p - 1
                            dve.wait_ge(bank_free[n % BANKS], n // BANKS + 1)
                            dve.wait_ge(bank_full[(n + 1) % BANKS], (n + 1) // BANKS + 1)
                            v.tensor_tensor(ffa[:, j, lo:], ctmp[:, j % 4, lo:], ps(n + 1, 0, cols), ALU.mult).then_inc(bank_free[(n + 1) % BANKS], 1)
                dve.wait_ge(bank_free[(n + 1) % BANKS], (n + 1) // BANKS + 1)
                v.tensor_copy(scrap[:, l:l + 1], eps[:, :]).then_inc(ffa_ready, 1)
                dve.wait_ge(ffa_ready, own(ffa_ready))

            residual2("m_out", 0, 2, (0, 1))
            layer_norm(0, 0, 0, 0)
            modulate(0, 3)
            ffn(0, (0, 1))
            residual2(("ffn_out", 0), 0, 5, (0, 1))
            layer_norm(1, 0, 1, 0)

            modulate(1, 0)
            feed(G("a_dkv"), 2)
            n = N("a_dkv", 2)
            dve.wait_ge(bank_full[n % BANKS], n // BANKS + 1)
            rope = con_at("rope", 256)

            def rotate(dst, n, lo):
                v.tensor_tensor(rt[0:64, 0, :], bank[n % BANKS][0:64, lo:lo + T], rope[0:64, :], ALU.mult)
                v.tensor_tensor(rt[0:64, 1, :], bank[n % BANKS][64:128, lo:lo + T], rope[64:128, :], ALU.mult).then_inc(dve_own, 1)
                dve.wait_ge(dve_own, own(dve_own))
                return v.tensor_tensor(dst, rt[0:64, 0, :], rt[0:64, 1, :], ALU.add)

            v.tensor_copy(krope[0:64, 0:T], bank[n % BANKS][0:64, 0:T])
            rotate(krope[0:64, T:T2], n, T).then_inc(bank_free[n % BANKS], 1)
            dve.wait_ge(bank_free[n % BANKS], n // BANKS + 1)
            feed(G("a_dq"))
            dve.wait_ge(rstd_ready, seen(rstd_ready))
            for k in range(2):
                ins = stt(ckv[:, k, :], ckv[:, k, :], par_at("kv_norm", k), stat[:, 0, :], ALU.mult, ALU.mult)
            ins.then_inc(ckn_ready, 1)
            dve.wait_ge(ckn_ready, own(ckn_ready))
            dve.wait_ge(rstd_ready, seen(rstd_ready))
            for k in range(3):
                ins = stt(cq[:, k, :], cq[:, k, :], par_at("q_norm", k), stat[:, 0, 0:T], ALU.mult, ALU.mult)
            ins.then_inc(ckn_ready, 1)
            dve.wait_ge(ckn_ready, own(ckn_ready))
            feed(G("a_ukv"), 1)
            feed(G("a_v"), 1)
            feed(G("a_uq", 0), 1)
            feed(G("a_uq", 1))
            for h in range(AH):
                n = N(("a_uq", 1), h)
                dve.wait_ge(bank_full[n % BANKS], n // BANKS + 1)
                rotate(qr[0:64, h, :], n, 0).then_inc(bank_free[n % BANKS], 1)
                dve.wait_ge(bank_free[n % BANKS], n // BANKS + 1)
            for i in range(2 * AH + 1):
                if i < 2 * AH:
                    n = N(("aS", i))
                    dve.wait_ge(bank_full[n % BANKS], n // BANKS + 1)
                    v.tensor_reduce(ast[:, i, 0:1], ps(n), AX, ALU.max, negate=True).then_inc(dve_own, 1)
                    dve.wait_ge(dve_own, own(dve_own))
                    v.tensor_scalar(ast[:, i, 1:2], ast[:, i, 0:1], A_SCALE, None, ALU.mult).then_inc(amax_ready, 1)
                if i:
                    j = i - 1
                    dve.wait_ge(bank_free[N(("aS", j)) % BANKS], N(("aS", j)) // BANKS + 1)
                    v.reciprocal(ast[:, j, 3:4], ast[:, j, 2:3]).then_inc(dve_own, 1)
                    dve.wait_ge(dve_own, own(dve_own))
                    v.tensor_scalar(ap_[:, j % 3, :], ap_[:, j % 3, :], ast[:, j, 3:4], None, ALU.mult).then_inc(ap_ready, 1)
            residual2("a_out", 1, 2, (1,))
            layer_norm(2, 1, 0, LAT)
            modulate(1, 3, (1,))
            ffn(1, (1,))
            residual2(("ffn_out", 1), 1, 5, (1,))
            layer_norm(3, 1, 1, LAT)


def pack_constants():
    p = np.arange(P)[:, None]
    c = np.zeros((P, CON.n), np.float32)

    def put(name, a):
        c[:, CON(name):CON(name) + a.shape[1]] = a

    put("ident", np.eye(P))
    put("ones", np.ones((P, P)))
    keys = np.arange(T)[None, :]
    strict = np.where(np.concatenate([keys[:, :P] < p, keys < p + P], 1), 0.0, NEG)
    ends = 16 * np.arange(16)[None, :] + 31
    cmask = np.concatenate([(ends <= p + P * q) & (np.arange(16) < CMP_N) for q in range(2)], 1)
    keys = np.arange(P)[None, :]
    put("tri", np.concatenate([np.where(keys >= p, 0.0, -NEG), np.where(keys <= p, 0.0, -NEG)], 1))
    pick = np.zeros((P, 127))
    pick[:, 63] = 1
    put("pick", pick)
    t = np.arange(T)
    inv = np.float32(10000.0) ** (-np.arange(16, dtype=np.float32) / np.float32(16))
    ang = [(c.astype(np.float32)[None, :] * inv[:, None]).astype(np.float32) for c in (t // 64, t % 64)]
    cos = [np.cos(a) for a in ang for _ in range(2)]
    sin = [sign * np.sin(a) for a in ang for sign in (-1, 1)]
    put("rope", np.concatenate(cos + sin, 0))
    j = np.arange(512) - (T - 1)
    near = np.maximum(j, 1).astype(np.float32)
    far = 16 + (np.log(near / np.float32(16)) / np.float32(math.log(8)) * 16).astype(np.int32)
    bucket = np.where(j < 0, 32, np.where(j < 16, j, np.minimum(far, 31)))
    onehot = (np.arange(33)[:, None] == bucket[None, :]).astype(np.float32)
    return c, onehot, strict, cmask


def cols(v):
    return np.asarray(v).reshape(-1, P).T


def pack_params1(x, strict, cmask):
    a = np.zeros((P, PAR1.n), np.float32)

    def put(name, v):
        v = np.asarray(v)
        a[:v.shape[0], PAR1(name):PAR1(name) + v.shape[1]] = v

    for l in range(DEPTH):
        pos = [np.asarray(x[k][l]).reshape(16, P).T for k in ("cmp_pos_k", "cmp_pos_v")]
        put(("pos", l), np.concatenate(pos, 1))
        k2 = np.asarray(x["cmp_k_w2"][l]).reshape(2, P, HD)
        put(("w2k", l), np.concatenate([k2[0], k2[0], k2[1], k2[1]], 1))
        v2 = np.asarray(x["cmp_v_w2"][l]).reshape(2, P, HD)
        put(("w2v", l), np.concatenate([v2[0], v2[1]], 1))
        put(("dlam", l), np.broadcast_to(np.asarray(x["diff_lambda"][l]).reshape(1, 128), (P, 128)))
    put("table", np.concatenate([np.asarray(x["rel_bias"]), np.full((1, 12), NEG, np.float32)], 0))
    put("strict", strict)
    put("cmask", cmask)
    put("halves", np.kron(np.eye(2), np.ones((HD, HD))))
    return a


def pack_params(x):
    a = np.zeros((P, PAR.n), np.float32)

    def put(name, v):
        v = np.asarray(v)
        a[:v.shape[0], PAR(name):PAR(name) + v.shape[1]] = v

    for l in range(DEPTH):
        put(("g_attn", l), cols(x["norm_attn"][l]))
        put(("g_mlp", l), cols(x["norm_mlp"][l]))
        put(("subln", l), np.tile(x["diff_subln"][l], 2)[:, None])
    put("g_final", cols(x["final_norm"]))
    for l in range(DEPTH):
        put(("ada_b", l), cols(x["ada_b_2"][l]))
        for i in range(2):
            put(("ln_g", l, i), cols(x["ln_g_2"][l][i]))
            put(("ln_b", l, i), cols(x["ln_b_2"][l][i]))
        put(("fconv_w", l), np.asarray(x["ffn_conv_w_2"][l]).reshape(3, NFF, P).transpose(2, 1, 0).reshape(P, -1))
        put(("fconv_b", l), cols(x["ffn_conv_b_2"][l]))
    conds = np.stack([cols(x["c_2"][0]), cols(x["c_ctx_2"])], 2)
    put("cond", conds.reshape(P, 16))
    put("mconv_w", np.asarray(x["m_conv_w_2"][0]).reshape(3, MK, P).transpose(2, 1, 0).reshape(P, -1))
    put("mconv_b", cols(x["m_conv_b_2"][0]))
    bg = np.zeros((P, 1), np.float32)
    for z in range(2):
        for g in range(2):
            bg[64 * g + 32 * z:64 * g + 32 * z + MH, 0] = np.asarray(x["m_b_gates_2"])[0, z, g * MH:(g + 1) * MH]
    put("b_gates", bg)
    put("m_norm", cols(x["m_norm_g_2"][0]))
    put("q_norm", cols(x["a_q_norm_2"][0]))
    put("kv_norm", cols(x["a_kv_norm_2"][0]))
    return a


def pack_stream(x):
    s = np.zeros((ST.n, P, SLOT), np.float32)

    def put(w, a, kc=None):
        k = a.shape[0] // P
        full = np.zeros((kc or k, P, SLOT // (kc or k)), np.float32)
        full[:k, :, :a.shape[1]] = a.reshape(k, P, a.shape[1])
        s[w] = full.transpose(1, 0, 2).reshape(P, SLOT)

    def group(name, *parts):
        g = ST.g[name]
        m = np.concatenate(parts, 1)
        for j in range(g.slots):
            rows = m[j * g.kc * P:(j + 1) * g.kc * P]
            put(g.w0 + j, rows, g.kc)

    for l in range(DEPTH):
        w = np.asarray(x["w_in"][l])

        def c(lo, n):
            return w[:, lo:lo + n]

        kc, vc, ks, vs, kw, vw = (c(1792 + 64 * i, 64) for i in range(6))
        df = 2188
        group(("proj", l, 0), c(0, 512), c(768, 512))
        group(("proj", l, 1), c(1536, 256), c(df, 512), ks, ks, kw, kw)
        group(("proj", l, 2), kc, kc, vc, vc)
        group(("nat", l), c(512, 256), c(1280, 256), c(df + 512, 256), vs, vw, c(2176, 12))
        for i, k in enumerate(("cmp_k_w1", "cmp_v_w1")):
            for h in range(2):
                put(W(("cmp", l), 2 * i + h), np.asarray(x[k][l])[:, P * h:P * h + P])
        a = np.asarray(x["ada_w_2"][l])
        for i in range(24):
            put(W(("ada", l), i), a[:, T * i:T * (i + 1)])
        group(("out", l), np.asarray(x["w_out"][l]))
        for i in range(4):
            group(("up", l, i), np.asarray(x["w_up"][l])[:, D * i:D * (i + 1)])
        group(("down", l), np.asarray(x["w_down"][l]))
        f = np.asarray(x["ffn_w_in_2"][l])
        pairs = [f[:, P * (j + NFF * i):P * (j + NFF * i + 1)] for j in range(NFF) for i in range(2)]
        per = (4, 8)[l]
        for i in range(-(-2 * NFF // per)):
            group(("ffn_in", l, i), *pairs[per * i:per * (i + 1)])
        group(("ffn_out", l), np.asarray(x["ffn_w_out_2"][l]))
    a = np.asarray(x["m_w_up_2"][0])
    for i in range(4):
        group(("m_up", i), a[:, T2 * i:T2 * (i + 1)])
    gates = np.zeros((MK * P, P), np.float32)
    for z in range(2):
        for g in range(2):
            gates[:, 64 * g + 32 * z:64 * g + 32 * z + MH] = np.asarray(x["m_w_gates_2"])[0, z, :, g * MH:(g + 1) * MH]
    put(W("m_gates"), gates)
    wv, wqk, wog = (np.asarray(x[k][0]) for k in ("m_w_v_2", "m_w_qk_2", "m_w_og_2"))
    for h in range(MH):
        group(("m_v", h), wv[:, T2 * h:T2 * (h + 1)])
        group(("m_qk", h), wqk[:, T * h:T * (h + 1)], wqk[:, D + T * h:D + T * (h + 1)])
        group(("m_og", h), wog[:, T2 * h:T2 * (h + 1)])
    group("m_out", np.asarray(x["m_w_out_2"][0]))
    swap = np.concatenate([np.arange(16, 32), np.arange(16), np.arange(48, 64), np.arange(32, 48)])
    a = np.asarray(x["a_w_dkv_2"][0])
    group("a_dkv", a, a[:, T:][:, swap])
    group("a_dq", np.asarray(x["a_w_dq_2"][0]))
    a = np.asarray(x["a_w_ukv_2"][0]).reshape(2 * P, AH, 2, P)
    for i, name in enumerate(("a_ukv", "a_v")):
        group(name, a[:, :, i].reshape(2 * P, D))
    a = np.asarray(x["a_w_uq_2"][0]).reshape(3 * P, AH, 192)
    group(("a_uq", 0), a[:, :, :P].reshape(3 * P, D))
    r = a[:, :, P:]
    group(("a_uq", 1), np.concatenate([r, r[:, :, swap]], 2).reshape(3 * P, D))
    group("a_out", np.asarray(x["a_w_out_2"][0]))
    return s


def kernel(**inputs):
    import concourse.bacc as bacc
    from concourse.bass_utils import run_bass_kernel_spmd

    nc = bacc.Bacc("TRN2", target_bir_lowering=False, num_devices=1, dynamic_dma_scratch_size=1024)
    consts, onehot, strict, cmask = pack_constants()
    arrays = {
        "in_tokens": np.concatenate([np.asarray(inputs["ctx_2"])[0], np.asarray(inputs["x"])[0]], 0),
        "in_stream": pack_stream(inputs),
        "in_params": pack_params(inputs),
        "in_params1": pack_params1(inputs, strict, cmask),
        "in_consts": consts,
        "in_onehot": onehot,
    }
    args = [nc.dram_tensor(name, a.shape, F32, kind="ExternalInput").ap() for name, a in arrays.items()]
    args.append(nc.dram_tensor("out_0", (1, T, D), F32, kind="ExternalOutput").ap())
    args.append(nc.dram_tensor("bias_vectors", (12, 512), F32, kind="Internal").ap())
    build(nc, *args)
    r = run_bass_kernel_spmd(nc, [arrays], core_ids=[0])
    return r.results[0]["out_0"]
```

```python
import math
from contextlib import ExitStack

import numpy as np
import concourse.bass as bass
from concourse import mybir

P = 128
F32 = mybir.dt.float32
ALU = mybir.AluOpType
ACT = mybir.ActivationFunctionType
AX = mybir.AxisListType.X

D = 1024
KD = D // P
T = 256
T2 = 2 * T
LAT = T
DEPTH = 2
EPS = 1e-6
NEG = -1e30
HD = 64
CMP_N = 15
SLOT = 2048
R = 2
BANKS = 8
SIDE = 4
CMP_W = 4
ADA_W = 24
SIDE_W = CMP_W + ADA_W
ALPHA = (2 * DEPTH) ** 0.25
NFF = 22
MIXER = 61 * 512 + 256
MH = 4
MK = 16
AH = 8
A_SCALE = 192 ** -0.5
OFF = (0, 512, 1024, 1280)
T_AT = (0, 0, T, T)


class Plan:

    def __init__(self):
        self.at, self.n = {}, 0

    def add(self, name, count=1):
        self.at[name] = self.n
        self.n += count

    def __call__(self, name, i=0):
        return self.at[name] + i


def units():
    out = []
    for h in range(4):
        out.append(dict(kind="sb", h=h, q=h // 2, k=2 + h // 2, r=64 * (h % 2), kk=64, v=("vn", 0), first=True,
                        last=True, chunk=h // 2, row=64 * (h % 2)))
    for h in range(4):
        out.append(dict(kind="mb", h=h, q=4 + h // 2, k=6 + h // 2, r=64 * (h % 2), kk=64, v=("vn", 1), bias=h,
                        first=True, last=True, chunk=2 + h // 2, row=64 * (h % 2)))
    for h in range(4):
        for b, kind in enumerate(("cmp", "slc", "win")):
            out.append(dict(kind=kind, h=h, q=8 + h // 2, k=13 + b, r=64 * (h % 2), kk=64, v=(kind, 0), bias=4 + h,
                            first=b == 0, last=b == 2, chunk=4 + h // 2, row=64 * (h % 2), gate=4 * b + h))
    for h in range(4):
        for c in range(2):
            out.append(dict(kind="df", h=h, q=10 + h // 2, k=12 + h // 2, r=64 * (h % 2) + 32 * c, kk=32, v=("vn", 2),
                            bias=8 + h, first=c == 0, last=c == 1, chunk=6 + h // 2, row=64 * (h % 2), c=c))
    return out


UNITS = units()
NU = len(UNITS)


FR = mybir.dt.float32r


def params1_layout():
    p = Plan()
    for l in range(DEPTH):
        p.add(("pos", l), 32)
        p.add(("ada_b", l), 96)
        p.add(("w2k", l), 256)
        p.add(("w2v", l), 128)
        p.add(("dlam", l), 128)
    p.add("table", 12)
    p.add("strict", 384)
    p.add("cmask", 32)
    p.add("halves", 128)
    return p


def params_layout():
    p = Plan()
    for l in range(DEPTH):
        p.add(("g_attn", l), KD)
        p.add(("g_mlp", l), KD)
        p.add(("subln", l), 1)
        for s in range(2):
            p.add(("ln_g", l, s), KD)
            p.add(("ln_b", l, s), KD)
        p.add(("fconv_w", l), 3 * NFF)
        p.add(("fconv_b", l), NFF)
    p.add("g_final", KD)
    p.add("cond", 16)
    p.add("mconv_w", 48)
    p.add("mconv_b", 16)
    p.add("b_gates", 1)
    p.add("m_norm", 16)
    p.add("q_norm", 3)
    p.add("kv_norm", 2)
    return p


def consts_layout():
    p = Plan()
    p.add("ident", 128)
    p.add("ones", 128)
    p.add("rope", 256)
    p.add("tri", 256)
    p.add("pick", 127)
    return p


PAR = params_layout()
PAR1 = params1_layout()
CON = consts_layout()


class Group:

    def __init__(self, name, tickets, K, T_, src, natural=False, fresh=None):
        self.fresh = fresh
        self.name, self.tickets, self.K, self.T, self.src, self.natural = name, tickets, K, T_, src, natural
        across = tickets // (T_ // P) * 4 if natural else tickets
        self.kc = next(c for c in (8, 4, 2) if c * across <= SLOT // P)
        self.slots = -(-K // self.kc)


class Stream:

    def __init__(self):
        self.w, self.g, self.split, self.q = {}, {}, [], 0
        self.n, self.chunks, self.raised = 0, [], 0
        self.cell, self.held = 0, [None] * 4

    def direct(self, name, count=1):
        self.w[name] = self.n
        self.n += count

    def group(self, *a, **kw):
        g = Group(*a, **kw)
        self.g[g.name] = g
        g.w0, g.s0, g.q0 = self.n, len(self.split), self.q
        self.w[g.name] = self.n
        self.n += g.slots
        self.q += g.K
        for j in range(g.slots):
            self.split.append((g.w0 + j, g.q0 + min(g.K, (j + 1) * g.kc) - 1))
        for k in range(g.K):
            self.raised += k < g.K - 1
            cells = g.T // T
            self.cell = -(-self.cell // cells) * cells % 4
            mine = range(self.cell, self.cell + cells)
            before = max((self.held[c] for c in mine if self.held[c] is not None), default=None)
            for c in mine:
                self.held[c] = g.q0 + k
            self.chunks.append((g, k, self.raised, self.cell, before))
            self.cell = (self.cell + cells) % 4


def stream_plan():
    w = Stream()
    for l in range(DEPTH):
        for i in range(3):
            w.group(("proj", l, i), (8, 8, 2)[i], KD, T, "h", fresh=None if i else 2 * l)
        w.group(("nat", l), 4, KD, T, "h", natural=True)
        w.group(("out", l), 8, KD, T, "mixed")
        for i in range(4):
            w.group(("up", l, i), 8, KD, T, "h", fresh=None if i else 2 * l + 1)
        w.group(("down", l), 8, 32, T, "act")
    for i in range(4):
        w.group(("m_up", i), 4, KD, T2, "h", fresh=None if i else 4)
    w.direct("m_gates")
    for h in range(MH):
        w.group(("m_v", h), 4, MK, T2, "xm", natural=True)
    for h in range(MH):
        w.group(("m_qk", h), 4, MK, T2, "xc")
        w.group(("m_og", h), 4, KD, T2, "h")
    w.group("m_out", 8, MK, T2, "hs")
    for i in range(NFF // 2):
        w.group(("ffn_in", 0, i), 4, KD, T2, "h", fresh=None if i else 5)
    w.group(("ffn_out", 0), 8, NFF, T2, "ffa")
    w.group("a_dkv", 3, KD, T2, "h", fresh=6)
    w.group("a_dq", 3, KD, T, "h")
    w.group("a_ukv", AH, 2, T2, "ckv")
    w.group("a_v", 8, 2, T2, "ckv", natural=True)
    for i in range(2):
        w.group(("a_uq", i), 8, 3, T, "cq")
    w.group("a_out", 8, AH, T, "aoT")
    for i in range(6):
        w.group(("ffn_in", 1, i), 8 if i < 5 else 4, KD, T, "h", fresh=None if i else 7)
    w.group(("ffn_out", 1), 8, NFF, T, "ffa")
    return w


def ticket_plan():
    n = Plan()
    n.add("bias")
    n.add("xT", KD)
    for l in range(DEPTH):
        n.add(("rms1", l))
        for i in range(3):
            n.add(("proj", l, i), (8, 8, 2)[i])
        n.add(("nat", l), 4)
        n.add(("hid", l), 4)
        n.add(("hidT", l))
        n.add(("kc", l))
        n.add(("vc", l))
        for i in range(NU + 3):
            if i < NU:
                n.add(("S", l, i))
            if i <= ADA_W:
                n.add(("ada", l, i))
            if 0 <= i - 2 < NU:
                n.add(("PT", l, i - 2))
            if 0 <= i - 3 < NU and UNITS[i - 3]["first"]:
                n.add(("O", l, i - 3))
            elif 0 <= i - 3 < NU:
                n.at[("O", l, i - 3)] = n.at[("O", l, i - 4)]
        n.add(("dfn", l))
        n.add(("out", l), 8)
        n.add(("rms2", l))
        for i in range(4):
            n.add(("up", l, i), 8)
        n.add(("down", l), 8)
    n.add("rmsf")
    for i in range(4):
        n.add(("m_up", i), 4)
    n.add("m_gates")
    n.add("m_aT")
    for h in range(MH):
        n.add(("m_v", h), 4)
    for h in range(MH):
        n.add(("m_max", h), 2)
        n.add(("m_qk", h), 4)
        n.add(("m_QK", h), 4)
        n.add(("m_og", h), 4)
        n.add(("m_den", h))
        n.add(("m_rec", h), 2)
        n.add(("m_PV", h), 4)
        n.add(("m_rms", h))
    n.add("m_out", 8)
    n.add(("mean", 0))
    n.add(("var", 0))
    for i in range(NFF // 2):
        n.add(("ffn_in", 0, i), 4)
    n.add(("ffn_out", 0), 8)
    n.add(("mean", 1))
    n.add(("var", 1))
    n.add("a_dkv", 3)
    n.add("a_dq", 3)
    n.add("a_kvn")
    n.add("a_qn")
    n.add("a_ukv", AH)
    n.add("a_v", 8)
    for i in range(2):
        n.add(("a_uq", i), 8)
    for i in range(2 * AH + 4):
        if i < 2 * AH:
            n.add(("aS", i))
        if 0 <= i - 2 < 2 * AH:
            n.add(("aPT", i - 2))
        if i >= 4 and i % 2 == 0 and (i - 4) // 2 < AH:
            n.add(("aO", (i - 4) // 2))
    n.add("a_out", 8)
    n.add(("mean", 2))
    n.add(("var", 2))
    for i in range(6):
        n.add(("ffn_in", 1, i), 8 if i < 5 else 4)
    n.add(("ffn_out", 1), 8)
    n.add(("mean", 3))
    n.add(("var", 3))
    n.add("oT", 4)
    return n


ST = stream_plan()
N = ticket_plan()


def W(name, i=0):
    return ST.w[name] + i


def G(*name):
    return ST.g[name if len(name) > 1 else name[0]]


class Count:

    def __init__(self):
        self.n = {}

    def __call__(self, sem, more=1):
        self.n[id(sem)] = self.n.get(id(sem), 0) + more
        return self.n[id(sem)]


def build(nc, tokens, stream, side, params, params1, consts, onehot, out, scratch):
    with ExitStack() as ctx:
        def sb(name, shape):
            return ctx.enter_context(nc.sbuf_tensor(name, shape, F32))

        def sem(name):
            return ctx.enter_context(nc.semaphore(name))

        bank = [ctx.enter_context(nc.psum_tensor(f"bank{i}", [P, 512], F32)) for i in range(BANKS)]
        ring = sb("ring", [P, R, SLOT])
        ws = ctx.enter_context(nc.sbuf_tensor("ws", [P, 2, 2, SLOT], FR))
        xs = ctx.enter_context(nc.sbuf_tensor("xs", [P, 2, 4 * T], FR))
        slot_full = [sem(f"slot_full{i}") for i in range(R)]
        side_full = [sem(f"side_full{i}") for i in range(SIDE)]
        w_high = sem("weights_high_ready")
        slot_done = sem("slot_done")
        x_high = sem("input_high_ready")
        x_done = sem("input_split")
        chunk_done = sem("chunk_multiplied")
        bank_full = [sem(f"bank_full{i}") for i in range(BANKS)]
        bank_free = [sem(f"bank_free{i}") for i in range(BANKS)]

        xT = sb("xT", [P, KD, T2])
        hT = sb("hT", [P, KD, T2])
        par = sb("par", [P, PAR.n])
        con = sb("con", [P, CON.n])
        eps = sb("eps", [P, 1])
        one = sb("one", [P, 1])
        stat = sb("stat", [P, 2, T2])
        A1 = MIXER
        arena = sb("arena", [P, A1])

        def region(off, shape):
            n = int(np.prod(shape))
            ap = arena[:, off:off + n]
            if len(shape) == 2:
                ap = ap.rearrange("p (a b) -> p a b", a=shape[0])
            if len(shape) == 3:
                ap = ap.rearrange("p (a b c) -> p a b c", a=shape[0], b=shape[1])
            return ap

        def par_at(name, i=0, n=1):
            return par[:, PAR(name, i):PAR(name, i) + n]

        def con_at(name, n):
            return con[:, CON(name):CON(name) + n]

        ident = con_at("ident", 128)
        ones = con_at("ones", 128)

        o = Plan()
        for name, n in (("qk", 16 * T), ("x2", 2 * T), ("x3", 512), ("vn", 6 * T), ("vsw", 280), ("mixed", KD * T),
                        ("act", 32 * T), ("bias", 12 * 384), ("cbias", 128), ("hid", 64), ("hrow", 4 * 128), ("hidg", 64), ("lamp", 64), ("kc", 32), ("vc", 64),
                        ("s", 3 * 384), ("t", 4 * 384), ("pt", 2 * 384), ("st", 8 * NU), ("lam", 64),
                        ("relu", 2 * 512), ("par1", PAR1.n)):
            o.add(name, n)
        qk = region(o("qk"), (16, T))
        x2 = region(o("x2"), (2, T))
        x3 = region(o("x3"), (2, 16, 16))
        arow = region(o("x3"), (2, T))[0:2]
        vn = region(o("vn"), (3, 2, T))
        vsw = region(o("vsw"), (2, 140))
        mixed = region(o("mixed"), (KD, T))
        act = region(o("act"), (32, T))
        bias = region(o("bias"), (12, 384))
        cbias = region(o("cbias"), (4, 32))
        hid = region(o("hid"), (4, 16))
        hidg = region(o("hidg"), (4, 16))
        hrow = region(o("hrow"), (4, 128))[0:16]
        lamp = region(o("lamp"), (64,))
        kcT = region(o("kc"), (16,))
        vc = region(o("vc"), (64,))
        sbuf = region(o("s"), (3, 384))
        tbuf = region(o("t"), (4, 384))
        ptb = region(o("pt"), (2, 384))
        st = region(o("st"), (NU, 8))
        lam = region(o("lam"), (64,))
        xnat = region(o("act") + 4096, (4, D))
        hankel = region(o("s"), (12, T))
        side_slots = region(o("act"), (SIDE, SLOT))
        tz = region(o("mixed"), (4 * 353,)).rearrange("p (a b) -> p a b", a=4)
        relu = region(o("relu"), (2, 512))
        par1 = region(o("par1"), (PAR1.n,))
        assert o.n <= A1, o.n

        def par1_at(name, i=0, n=1):
            return par1[:, PAR1(name, i):PAR1(name, i) + n]

        halves = par1_at("halves", 0, 128)

        mod = sb("mod", [P, DEPTH, 96])
        cs = sb("cs", [P, 16])
        scrap = sb("scrap", [P, DEPTH])
        o = Plan()
        for name, n in (("xm", MK * T2), ("xc", MK * T2), ("v", MK * T2), ("qk", 4 * T2), ("P", 6 * T2),
                        ("rows", 3 * T2), ("aT", 4 * 64)):
            o.add(name, n)
        assert o.n <= A1, o.n
        xm = region(o("xm"), (MK, T2))
        hs = xm
        xc = region(o("xc"), (MK, T2))
        mv = region(o("v"), (4, MH * T2))
        mqk = region(o("qk"), (4, T2))
        og = mqk
        mP = region(o("P"), (2, 3 * T2))
        grow = region(o("P"), (6, T2))
        rows = region(o("rows"), (3, T2))
        aT = region(o("aT"), (4, 64))
        sq2 = region(o("xc"), (KD, T2))
        ctmp = region(o("xm"), (4, T2))
        graw = region(o("xm") + 4 * T2, (4, T2))
        fup = region(o("xm") + 8 * T2, (4, T2))
        ffa = region(o("xc") + KD * T2, (NFF, T2))
        o = Plan()
        for name, n in (("ckv", 2 * T2), ("cq", 3 * T), ("kr", T2), ("rt", 2 * T), ("kn", AH * T2), ("v", 4 * D), ("qn", AH * T),
                        ("qr", AH * T), ("oT", AH * T), ("ap", 3 * T2), ("apt", 2 * 4 * T), ("ast", 16 * 4),
                        ("cks", 3 * T2), ("osb", 2 * D)):
            o.add(name, n)
        assert o.n <= A1, o.n
        ckv = region(o("ckv"), (2, T2))
        cq = region(o("cq"), (3, T))
        krope = region(o("kr"), (T2,))
        rt = region(o("rt"), (2, T))
        kn = region(o("kn"), (AH, T2))
        av = region(o("v"), (4, D))
        qn = region(o("qn"), (AH, T))
        qr = region(o("qr"), (AH, T))
        aoT = region(o("oT"), (AH, T))
        ap_ = region(o("ap"), (3, T2))
        apt = region(o("apt"), (2, 4, T))
        ast = region(o("ast"), (16, 4))
        cks = region(o("cks"), (3, T2))
        osb = region(o("osb"), (2, D))

        cs_ready = sem("condition_ready")
        mod_rows = sem("modulation_rows_ready")
        conv_ready = sem("conv_ready")
        silu_ready = sem("silu_ready")
        lng_ready = sem("log_gate_terms_ready")
        rows_ready = sem("gate_rows_ready")
        floor_ready = sem("denominator_floor_ready")
        D_ready = sem("exponents_ready")
        E_ready = sem("decays_ready")
        rden_ready = sem("reciprocal_denominators_ready")
        W_ready = sem("mlstm_weights_ready")
        hs_ready = sem("mixer_output_ready")
        ln_ready = sem("layer_norm_ready")
        ffa_ready = sem("feed_forward_inner_ready")
        centre_ready = sem("centre_tap_ready")
        act_silu = sem("gate_silu_ready")
        ckn_ready = sem("latents_normed")
        amax_ready = sem("max_ready")
        aexp_ready = sem("attention_exp_ready")
        ap_ready = sem("attention_weights_ready")
        dma_x, dma_con, dma_par, dma_oh = sem("dma_x"), sem("dma_con"), sem("dma_par"), sem("dma_onehot")
        dma_bv, dma_bias, dma_out = sem("dma_bias_vector"), sem("dma_bias"), sem("dma_out")
        dve_own, act_own = sem("dve_own"), sem("act_own")
        small_ready = sem("small_constants_ready")
        cbias_ready = sem("compressed_bias_ready")
        sq_ready = sem("squares_ready")
        rstd_ready = sem("rstd_ready")
        h_ready = sem("h_ready")
        centred_ready = sem("centred_ready")
        scaled_ready = sem("residual_scaled")
        x3_ready = sem("x3_ready")
        hid_ready = sem("hidden_ready")
        logits_ready = sem("logits_ready")
        exp_ready = sem("exp_ready")
        arg_ready = sem("log_weights_ready")
        sb_ready = sem("stick_weights_ready")
        p_ready = sem("softmax_weights_ready")
        dfn_ready = sem("diff_normed")
        act_ready = sem("activations_ready")
        gate_exp = sem("gate_exp_ready")
        lam_sum = sem("lambda_sums_ready")
        lam_exp = sem("lambda_exp_ready")
        out_copied = sem("out_copied")

        def ps(n, lo=0, hi=512):
            return bank[n % BANKS][:, lo:hi]

        def side_at(j):
            return (j + 1) % SIDE

        SRC = {"mixed": mixed, "act": act, "xm": xm, "xc": xc, "hs": hs, "ckv": ckv, "cq": cq, "aoT": aoT}

        def source(g, k):
            if g.src in ("h", "ffa"):
                return (hT if g.src == "h" else ffa)[:, k, T2 - g.T:]
            return SRC[g.src][:, k, :]

        def split_x(q, i):
            return xs[:, i, ST.chunks[q][3] * T:ST.chunks[q][3] * T + ST.chunks[q][0].T]

        def chunk_end(q):
            g, k, raised = ST.chunks[q][:3]
            if k < g.K - 1:
                return chunk_done, raised
            n = N(g.name) + g.tickets - 1
            return bank_full[n % BANKS], n // BANKS + 1

        def follows(s_):
            return s_ + 1 < len(ST.split) and ST.split[s_ + 1][0] == ST.split[s_][0] + 1

        block = ctx.enter_context(nc.Block())

        @block.sync
        def _(sp):
            sp.dma_start(con[:, :], consts).then_inc(dma_con, 16)
            sp.dma_start(par[:, :], params).then_inc(dma_par, 16)
            sp.dma_start(par1, params1).then_inc(dma_par, 16)
            sp.dma_start(act.rearrange("p a b -> p (a b)")[0:33, 0:512], onehot).then_inc(dma_oh, 16)
            sp.dma_start(xnat, tokens.rearrange("(a p) d -> p a d", p=P)).then_inc(dma_x, 16)
            for i in range(R):
                sp.dma_start(ring[:, i, :], stream[i]).then_inc(slot_full[i], 16)
            sp.wait_ge(bank_free[N("bias") % BANKS], N("bias") // BANKS + 1)
            sp.dma_start(scratch, relu[0:12, 0, :]).then_inc(dma_bv, 16)
            sp.wait_ge(dma_bv, 16)
            for k in range(KD):
                sp.wait_ge(bank_free[N("xT", k) % BANKS], N("xT", k) // BANKS + 1)
            hnd = scratch.tensor
            sp.dma_start(hankel, bass.AP(tensor=hnd, offset=128, ap=[[1, P], [512, 12], [1, T]])).then_inc(dma_bias, 16)
            sp.dma_start(tz, bass.AP(tensor=hnd, offset=4 * 512, ap=[[1, P], [512, 4], [1, 353]])).then_inc(dma_bias, 16)
            def load(w):
                sp.wait_ge(slot_done, w - R + 1)
                sp.dma_start(ring[:, w % R, :], stream[w]).then_inc(slot_full[w % R], 16)

            def load_span(first, end):
                with sp.Fori(0, (end - first) // R) as turn:
                    for i in range(R):
                        sp.wait_ge(slot_done, turn * R + (first + i - R + 1))
                        sp.dma_start(ring[:, (first + i) % R, :], stream[turn * R + (first + i)]
                                     ).then_inc(slot_full[(first + i) % R], 16)
                for w in range(end - (end - first) % R, end):
                    load(w)

            def load_side(l, j):
                n = N(("rms1", l)) if j < SIDE else N(("hid", l), j - SIDE) if j < SIDE + CMP_W else N(("ada", l, j - SIDE - CMP_W))
                sp.wait_ge(bank_full[n % BANKS], n // BANKS + 1)
                sp.dma_start(side_slots[:, side_at(j), :], side[SIDE_W * l + j]).then_inc(side_full[side_at(j)], 16)

            at = R
            for l in range(DEPTH):
                first = ST.w[("proj", l, 0)] + 4
                load_span(at, first)
                for j in range(CMP_W):
                    for i in range(2):
                        load(first + 2 * j + i)
                    load_side(l, j)
                at = ST.w[("out", l)] + R
                for w in range(first + 2 * CMP_W, at):
                    load(w)
                for j in range(CMP_W, SIDE_W):
                    load_side(l, j)
            load_span(at, ST.n)
            sp.wait_ge(out_copied, 1)
            sp.dma_start(out.rearrange("b (a p) d -> p (b a) d", p=P), osb).then_inc(dma_out, 16)
            sp.wait_ge(dma_out, 16)

        @block.tensor
        def _(pe):
            seen = Count()
            mm = nc.tensor.matmul

            def slot(w, kc):
                n = SLOT // kc
                return ring[:, w % R, 0:kc * n].rearrange("p (k n) -> p k n", k=kc)

            def side_weights(l, j, kc):
                pe.wait_ge(side_full[side_at(j)], 16 * (SIDE_W // SIDE * l + j // SIDE + 1))
                return side_slots[:, side_at(j), :].rearrange("p (k n) -> p k n", k=kc)

            def linear(g, first=0, end=None):
                N0 = N(g.name)
                for k in range(first, g.K if end is None else end):
                    w, j, q = g.w0 + k // g.kc, k % g.kc, g.q0 + k
                    if j == 0:
                        pe.wait_ge(slot_done, w + 1)
                    pe.wait_ge(x_done, q + 1)
                    cols = SLOT // g.kc
                    a = [ws[:, (g.s0 + k // g.kc) % 2, i, j * cols:(j + 1) * cols] for i in range(2)]
                    x = [split_x(q, i) for i in range(2)]
                    for p in range(g.tickets):
                        n = N0 + p
                        if k == 0:
                            if n >= BANKS:
                                pe.wait_ge(bank_free[n % BANKS], n // BANKS)
                        for i, (wi, xi) in enumerate(((0, 0), (0, 1), (1, 0))):
                            first, last = k == i == 0, k == g.K - 1 and i == 2
                            if not g.natural:
                                ins = mm(ps(n, 0, g.T), a[wi][:, p * P:(p + 1) * P], x[xi], start=first, stop=last)
                            else:
                                nh = g.tickets // (g.T // P)
                                width = 396 if nh == 2 and g.T == T and p % 2 else 512
                                ins = mm(ps(n, 0, width), x[xi][:, (p // nh) * P:(p // nh + 1) * P],
                                         a[wi][:, (p % nh) * 512:(p % nh) * 512 + width], start=first, stop=last)
                        if k == g.K - 1:
                            ins.then_inc(bank_full[n % BANKS], 1)
                        elif p == g.tickets - 1:
                            ins.then_inc(chunk_done, 1)

            def sum_squares(n, src, chunks, cols, stationary, by_chunk=False):
                if not by_chunk:
                    pe.wait_ge(sq_ready, seen(sq_ready))
                if n >= BANKS:
                    pe.wait_ge(bank_free[n % BANKS], n // BANKS)
                for k in range(chunks):
                    if by_chunk:
                        pe.wait_ge(sq_ready, seen(sq_ready))
                    ins = mm(ps(n, 0, cols), stationary, src(k), start=(k == 0), stop=(k == chunks - 1))
                ins.then_inc(bank_full[n % BANKS], 1)

            pe.wait_ge(dma_con, 16)
            pe.wait_ge(dma_par, 32)
            pe.wait_ge(dma_oh, 16)
            oh = act.rearrange("p a b -> p (a b)")[0:33, 0:512]
            n = N("bias")
            if n >= BANKS:
                pe.wait_ge(bank_free[n % BANKS], n // BANKS)
            mm(bank[n % BANKS][0:12, :], par1[0:33, PAR1("table"):PAR1("table") + 12], oh, start=True, stop=True).then_inc(bank_full[n % BANKS], 1)
            pe.wait_ge(dma_x, 16)
            for k in range(KD):
                n = N("xT", k)
                if n >= BANKS:
                    pe.wait_ge(bank_free[n % BANKS], n // BANKS)
                for t in range(4):
                    ins = nc.tensor.transpose(ps(n, t * P, (t + 1) * P), xnat[:, t, k * P:(k + 1) * P], ident)
                ins.then_inc(bank_full[n % BANKS], 1)

            for l in range(DEPTH):
                sum_squares(N(("rms1", l)), lambda k: act[:, k, :], KD, T, ones, True)
                for i in range(3):
                    linear(G("proj", l, i))
                linear(G("nat", l))
                pe.wait_ge(x3_ready, seen(x3_ready))
                for i in range(4):
                    n = N(("hid", l), i)
                    wd = side_weights(l, i, 16)
                    if n >= BANKS:
                        pe.wait_ge(bank_free[n % BANKS], n // BANKS)
                    for j in range(16):
                        ins = mm(bank[n % BANKS][0:16, 0:P], x3[:, i // 2, j, :], wd[:, j, :], start=(j == 0), stop=(j == 15))
                    ins.then_inc(bank_full[n % BANKS], 1)
                n = N(("hidT", l))
                if n >= BANKS:
                    pe.wait_ge(bank_free[n % BANKS], n // BANKS)
                for i in range(4):
                    m = N(("hid", l), i)
                    pe.wait_ge(bank_free[m % BANKS], m // BANKS + 1)
                    ins = nc.tensor.transpose(ps(n, 16 * i, 16 * i + 16), hrow[:, i, :], ident[0:16, 0:16])
                ins.then_inc(bank_full[n % BANKS], 1)
                pe.wait_ge(hid_ready, seen(hid_ready, 4))
                n = N(("kc", l))
                if n >= BANKS:
                    pe.wait_ge(bank_free[n % BANKS], n // BANKS)
                for j in range(2):
                    ins = mm(ps(n, 0, 16), par1_at(("w2k", l), 128 * j, 128), hidg[:, j, :],
                             start=(j == 0), stop=(j == 1))
                ins.then_inc(bank_full[n % BANKS], 1)
                n = N(("vc", l))
                if n >= BANKS:
                    pe.wait_ge(bank_free[n % BANKS], n // BANKS)
                for j in range(2):
                    ins = mm(bank[n % BANKS][0:16, 0:64], hidg[:, 2 + j, :],
                             par1_at(("w2v", l), 64 * j, 64), start=(j == 0), stop=(j == 1))
                ins.then_inc(bank_full[n % BANKS], 1)
                for n in range(N(("vc", l)) - BANKS + 1, N(("vc", l)) + 1):
                    pe.wait_ge(bank_free[n % BANKS], n // BANKS + 1)
                for i in range(NU + 3):
                    if i < NU:
                        u, n = UNITS[i], N(("S", l, i))
                        lo, hi = u["r"], u["r"] + u["kk"]
                        if n >= BANKS:
                            pe.wait_ge(bank_free[n % BANKS], n // BANKS)
                        if u["kind"] == "cmp":
                            mm(ps(n, 0, 16), qk[lo:hi, u["q"], 0:128], kcT[lo:hi, :], start=True, stop=True)
                            ins = mm(ps(n, 16, 32), qk[lo:hi, u["q"], 128:256], kcT[lo:hi, :], start=True, stop=True)
                        else:
                            ins = mm(ps(n, 0, 128), qk[lo:hi, u["q"], 0:128], qk[lo:hi, u["k"], 0:128], start=True, stop=True)
                            ins = mm(ps(n, 128, 384), qk[lo:hi, u["q"], 128:256], qk[lo:hi, u["k"], :],
                                     start=True, stop=True)
                        ins.then_inc(bank_full[n % BANKS], 1)
                    if i <= ADA_W:
                        n = N(("ada", l, i))
                        if l == i == 0:
                            pe.wait_ge(cs_ready, seen(cs_ready))
                        if i < ADA_W:
                            wd = side_weights(l, CMP_W + i, KD)
                        if n >= BANKS:
                            pe.wait_ge(bank_free[n % BANKS], n // BANKS)
                        if i < ADA_W:
                            for k in range(KD):
                                ins = mm(bank[n % BANKS][0:2, 0:T], cs[:, 2 * k:2 * k + 2], wd[:, k, :],
                                         start=(k == 0), stop=(k == KD - 1))
                        if i:
                            pe.wait_ge(mod_rows, seen(mod_rows))
                            for g in range(2):
                                ins = nc.tensor.transpose(ps(n, T + 2 * g, T + 2 * g + 2),
                                                          arow[:, (i - 1) % 2, g * P:(g + 1) * P], ident[0:2, 0:2])
                        ins.then_inc(bank_full[n % BANKS], 1)
                    if 0 <= i - 2 < NU:
                        j = i - 2
                        u, n = UNITS[j], N(("PT", l, j))
                        pe.wait_ge(sb_ready if u["kind"] == "sb" else p_ready, seen(sb_ready if u["kind"] == "sb" else p_ready))
                        if n >= BANKS:
                            pe.wait_ge(bank_free[n % BANKS], n // BANKS)
                        s = sbuf[:, j % 3, :]
                        if u["kind"] == "cmp":
                            for t in range(2):
                                ins = nc.tensor.transpose(bank[n % BANKS][0:16, t * P:(t + 1) * P],
                                                          s[:, 16 * t:16 * t + 16], ident)
                        else:
                            for t in range(3):
                                ins = nc.tensor.transpose(ps(n, t * P, (t + 1) * P), s[:, t * P:(t + 1) * P], ident)
                        ins.then_inc(bank_full[n % BANKS], 1)
                    if 0 <= i - 3 < NU:
                        j = i - 3
                        u, n = UNITS[j], N(("O", l, j))
                        if u["first"]:
                            if n >= BANKS:
                                pe.wait_ge(bank_free[n % BANKS], n // BANKS)
                        pe.wait_ge(bank_free[N(("PT", l, j)) % BANKS], N(("PT", l, j)) // BANKS + 1)
                        pt = ptb[:, j % 2, :]
                        ob = bank[n % BANKS][u["row"]:u["row"] + 64, :]
                        if u["kind"] == "cmp":
                            ins = mm(ob[:, 0:256], vc[0:16, :], pt[0:16, 0:256], start=u["first"], stop=u["last"])
                        else:
                            if u["v"][0] == "vn":
                                v = [vn[:, u["v"][1], t, 64 * u["h"]:64 * u["h"] + 64] for t in range(2)]
                            else:
                                v0 = 0 if u["kind"] == "slc" else 64
                                v = [vsw[:, t, v0:v0 + 64] for t in range(2)]
                            mm(ob[:, 0:256], v[0], pt[:, 0:256], start=u["first"], stop=False)
                            ins = mm(ob[:, 128:256], v[1], pt[:, 256:384], start=False, stop=u["last"])
                        if u["last"]:
                            ins.then_inc(bank_full[n % BANKS], 1)
                n = N(("dfn", l))
                pe.wait_ge(sq_ready, seen(sq_ready))
                if n >= BANKS:
                    pe.wait_ge(bank_free[n % BANKS], n // BANKS)
                mm(ps(n), halves, relu[:, 0, :], start=True, stop=True).then_inc(bank_full[n % BANKS], 1)
                linear(G("out", l))
                sum_squares(N(("rms2", l)), lambda k: act[:, k, :], KD, T, ones, True)
                for i in range(4):
                    linear(G("up", l, i))
                linear(G("down", l))
            sum_squares(N("rmsf"), lambda k: act[:, k, :], KD, T, ones, True)

            for i in range(4):
                linear(G("m_up", i))
            n = N("m_gates")
            pe.wait_ge(slot_full[(W("m_gates")) % R], 16 * ((W("m_gates")) // R + 1))
            wd = slot(W("m_gates"), MK)
            if n >= BANKS:
                pe.wait_ge(bank_free[n % BANKS], n // BANKS)
            for k in range(MK):
                pe.wait_ge(silu_ready, seen(silu_ready))
                ins = mm(ps(n), wd[:, k, :], xc[:, k, :], start=(k == 0), stop=(k == MK - 1))
            ins.then_inc(bank_full[n % BANKS], 1)
            linear(G("m_v", 0))
            pe.wait_ge(rows_ready, seen(rows_ready))
            n = N("m_aT")
            if n >= BANKS:
                pe.wait_ge(bank_free[n % BANKS], n // BANKS)
            for t in range(4):
                ins = nc.tensor.transpose(ps(n, 64 * t, 64 * t + 64), grow[0:64, 5, t * P:(t + 1) * P], ident[0:64, 0:64])
            ins.then_inc(bank_full[n % BANKS], 1)
            for h in range(1, MH):
                linear(G("m_v", h))
            pe.wait_ge(bank_free[N("m_aT") % BANKS], N("m_aT") // BANKS + 1)
            for h in range(MH):
                for z in range(2):
                    n = N(("m_max", h), z)
                    if n >= BANKS:
                        pe.wait_ge(bank_free[n % BANKS], n // BANKS)
                    r = 32 * z + h
                    mm(ps(n), ident[0:64, r:r + 1].to_broadcast([64, P]), rows[0:64, 0, :], start=True, stop=True).then_inc(bank_full[n % BANKS], 1)
                linear(G("m_qk", h), 0, 4)
                if h:
                    sum_squares(N(("m_rms", h - 1)), lambda k: mqk[:, k, :], 4, T2, ones)
                linear(G("m_qk", h), 4)
                for n in range(N(("m_qk", h)), N(("m_qk", h)) + 4):
                    pe.wait_ge(bank_free[n % BANKS], n // BANKS + 1)
                for st_ in range(4):
                    n = N(("m_QK", h), st_)
                    if n >= BANKS:
                        pe.wait_ge(bank_free[n % BANKS], n // BANKS)
                    for c in range(2):
                        ins = mm(ps(n, 0, T2 - T_AT[st_]), mqk[:, 2 + c, st_ * P:(st_ + 1) * P], mqk[:, c, T_AT[st_]:],
                                 start=(c == 0), stop=(c == 1))
                    ins.then_inc(bank_full[n % BANKS], 1)
                linear(G("m_og", h), 0, 3)
                pe.wait_ge(bank_free[N(("m_QK", h), 3) % BANKS], N(("m_QK", h), 3) // BANKS + 1)
                n = N(("m_den", h))
                if n >= BANKS:
                    pe.wait_ge(bank_free[n % BANKS], n // BANKS)
                for z in range(2):
                    r = 32 * z + h
                    for st_ in range(4):
                        ins = mm(bank[n % BANKS][0:64, T_AT[st_]:T2], con[:, CON("pick") + 63 - r:CON("pick") + 127 - r],
                                 mP[:, z, OFF[st_]:OFF[st_] + T2 - T_AT[st_]], start=(z + st_ == 0), stop=(z == 1 and st_ == 3))
                ins.then_inc(bank_full[n % BANKS], 1)
                linear(G("m_og", h), 3, 5)
                pe.wait_ge(rden_ready, seen(rden_ready))
                for z in range(2):
                    n = N(("m_rec", h), z)
                    if n >= BANKS:
                        pe.wait_ge(bank_free[n % BANKS], n // BANKS)
                    r = 32 * z + h
                    mm(ps(n), ident[0:64, r:r + 1].to_broadcast([64, P]), rows[0:64, 2, :], start=True, stop=True).then_inc(bank_full[n % BANKS], 1)
                linear(G("m_og", h), 5)
                pe.wait_ge(W_ready, seen(W_ready))
                for e in range(4):
                    n = N(("m_PV", h), e)
                    if n >= BANKS:
                        pe.wait_ge(bank_free[n % BANKS], n // BANKS)
                    for st_ in range(4):
                        ins = mm(ps(n, T_AT[st_], T2), mv[:, st_, h * T2 + e * P:h * T2 + (e + 1) * P],
                                 mP[:, 0, OFF[st_]:OFF[st_] + T2 - T_AT[st_]], start=(st_ == 0), stop=(st_ == 3))
                    ins.then_inc(bank_full[n % BANKS], 1)
            sum_squares(N(("m_rms", MH - 1)), lambda k: mqk[:, k, :], 4, T2, ones)
            linear(G("m_out"))

            def layer_norm(i, lo, name):
                n = N(("mean", i))
                if n >= BANKS:
                    pe.wait_ge(bank_free[n % BANKS], n // BANKS)
                for k in range(KD):
                    pe.wait_ge(bank_free[N(name, k) % BANKS], N(name, k) // BANKS + 1)
                    ins = mm(ps(n, 0, T2 - lo), ones, xT[:, k, lo:], start=(k == 0), stop=(k == KD - 1))
                ins.then_inc(bank_full[n % BANKS], 1)
                sum_squares(N(("var", i)), lambda k: sq2[:, k, lo:], KD, T2 - lo, ones, True)

            def ffn(l):
                for i in range((NFF // 2, 6)[l]):
                    linear(G("ffn_in", l, i))
                linear(G("ffn_out", l))

            layer_norm(0, 0, "m_out")
            ffn(0)
            layer_norm(1, 0, ("ffn_out", 0))

            linear(G("a_dkv"))
            linear(G("a_dq"))
            sum_squares(N("a_kvn"), lambda k: cks[:, k, :], 2, T2, ones)
            sum_squares(N("a_qn"), lambda k: cks[:, k, 0:T], 3, T, ones)
            linear(G("a_ukv"))
            linear(G("a_v"))
            for i in range(2):
                linear(G("a_uq", i))
            pe.wait_ge(bank_free[N("a_dkv", 2) % BANKS], N("a_dkv", 2) // BANKS + 1)
            for n in range(N("a_v"), N("a_v", 8)):
                pe.wait_ge(bank_free[n % BANKS], n // BANKS + 1)
            for i in range(2 * AH + 4):
                if i < 2 * AH:
                    h, t = i // 2, i % 2
                    if t == 0:
                        for n in (N(("a_uq", 0), h), N(("a_uq", 1), h)):
                            pe.wait_ge(bank_free[n % BANKS], n // BANKS + 1)
                    n = N(("aS", i))
                    if n >= BANKS:
                        pe.wait_ge(bank_free[n % BANKS], n // BANKS)
                    mm(ps(n), qn[:, h, t * P:(t + 1) * P], kn[:, h, :], start=True, stop=False)
                    mm(ps(n), qr[0:64, h, t * P:(t + 1) * P], krope[0:64, :], start=False, stop=True).then_inc(bank_full[n % BANKS], 1)
                if 0 <= i - 2 < 2 * AH:
                    j = i - 2
                    n = N(("aPT", j))
                    pe.wait_ge(ap_ready, seen(ap_ready))
                    if n >= BANKS:
                        pe.wait_ge(bank_free[n % BANKS], n // BANKS)
                    for t in range(4):
                        ins = nc.tensor.transpose(ps(n, t * P, (t + 1) * P), ap_[:, j % 3, t * P:(t + 1) * P], ident)
                    ins.then_inc(bank_full[n % BANKS], 1)
                if i >= 4 and i % 2 == 0 and (i - 4) // 2 < AH:
                    h = (i - 4) // 2
                    n = N(("aO", h))
                    if n >= BANKS:
                        pe.wait_ge(bank_free[n % BANKS], n // BANKS)
                    pe.wait_ge(bank_free[N(("aPT", 2 * h)) % BANKS], N(("aPT", 2 * h)) // BANKS + 1)
                    pe.wait_ge(bank_free[N(("aPT", 2 * h + 1)) % BANKS], N(("aPT", 2 * h + 1)) // BANKS + 1)
                    for t in range(4):
                        ins = mm(ps(n, 0, T), av[:, t, h * P:(h + 1) * P], apt[:, h % 2, t, :], start=(t == 0), stop=(t == 3))
                    ins.then_inc(bank_full[n % BANKS], 1)
            linear(G("a_out"))
            layer_norm(2, LAT, "a_out")
            ffn(1)
            layer_norm(3, LAT, ("ffn_out", 1))
            pe.wait_ge(ln_ready, KD * 2 * DEPTH)
            for t in range(2):
                for c in range(2):
                    n = N("oT", 2 * t + c)
                    if n >= BANKS:
                        pe.wait_ge(bank_free[n % BANKS], n // BANKS)
                    for k in range(4):
                        ins = nc.tensor.transpose(ps(n, k * P, (k + 1) * P), xT[:, 4 * c + k, LAT + t * P:LAT + (t + 1) * P],
                                                  ident)
                    ins.then_inc(bank_full[n % BANKS], 1)

        @block.scalar
        def _(act_):
            seen = Count()
            own = Count()
            do = nc.scalar.activation
            act_.wait_ge(small_ready, 2)
            act_.wait_ge(dma_par, 32)

            fed = {"w": 0, "q": 0}

            def weights_to(s_):
                while fed["w"] <= s_:
                    i = fed["w"]
                    w = ST.split[i][0]
                    act_.wait_ge(slot_full[w % R], 16 * (w // R + 1))
                    if i >= 2:
                        act_.wait_ge(*chunk_end(ST.split[i - 2][1]))
                    for half in range(2):
                        c = slice(half * SLOT // 2, (half + 1) * SLOT // 2)
                        do(ws[:, i % 2, 0, c], ring[:, w % R, c], ACT.Copy).then_inc(w_high, 1)
                    fed["w"] += 1

            def feed_to(q_):
                while fed["q"] <= q_:
                    q = fed["q"]
                    g, k, _, _, before = ST.chunks[q]
                    s_ = g.s0 + k // g.kc
                    weights_to(s_)
                    if g.src == "ffa":
                        act_.wait_ge(ffa_ready, NFF * g.name[1] + k + 1)
                    elif g.fresh is not None:
                        act_.wait_ge(h_ready, KD * g.fresh + k + 1)
                    if before is not None:
                        act_.wait_ge(*chunk_end(before))
                    do(split_x(q, 0), source(g, k), ACT.Copy).then_inc(x_high, 1)
                    fed["q"] += 1
                    if (k % g.kc == 1 or k == g.K - 1) and follows(s_):
                        weights_to(s_ + 1)

            def feed(g, more=0):
                feed_to(g.q0 + g.K - 1 + more)

            def squares(dst, src):
                do(dst, src, ACT.Square).then_inc(sq_ready, 1)

            def norm_squares(name):
                for k in range(KD):
                    if name:
                        act_.wait_ge(bank_free[N(name, k) % BANKS], N(name, k) // BANKS + 1)
                    squares(act[:, k, :], xT[:, k, LAT:])

            def rstd(n, cols, count):
                act_.wait_ge(bank_full[n % BANKS], n // BANKS + 1)
                do(stat[:, 1, 0:cols], ps(n, 0, cols), ACT.Ln, bias=eps[:, :], scale=1.0 / count).then_inc(bank_free[n % BANKS], 1)
                act_.wait_ge(bank_free[n % BANKS], n // BANKS + 1)
                do(stat[:, 0, 0:cols], stat[:, 1, 0:cols], ACT.Exp, scale=-0.5).then_inc(rstd_ready, 1)

            act_.wait_ge(bank_full[N("bias") % BANKS], N("bias") // BANKS + 1)
            do(relu[0:12, 0, :], bank[N("bias") % BANKS][0:12, :], ACT.Copy).then_inc(bank_free[N("bias") % BANKS], 1)
            for k in range(KD):
                act_.wait_ge(bank_full[N("xT", k) % BANKS], N("xT", k) // BANKS + 1)
                do(xT[:, k, :], ps(N("xT", k)), ACT.Copy).then_inc(bank_free[N("xT", k) % BANKS], 1)
            act_.wait_ge(bank_free[N("xT", KD - 1) % BANKS], N("xT", KD - 1) // BANKS + 1)
            do(cs[:, :], par_at("cond", 0, 16), ACT.Silu).then_inc(cs_ready, 1)
            for l in range(DEPTH):
                norm_squares(("down", l - 1) if l else None)
                rstd(N(("rms1", l)), T, D)
                act_.wait_ge(lam_sum, seen(lam_sum))
                do(lam[:, 2:4], lam[:, 0:2], ACT.Exp).then_inc(lam_exp, 1)
                for i in range(3):
                    g = G("proj", l, i)
                    feed(g, 1)
                    for p in range(g.tickets):
                        n = N(g.name) + p
                        act_.wait_ge(bank_full[n % BANKS], n // BANKS + 1)
                        piece = 8 * i + p
                        if piece < 16:
                            do(qk[:, piece, :], ps(n, 0, T), ACT.Copy).then_inc(bank_free[n % BANKS], 1)
                        else:
                            do(x2[0:64, piece - 16, :], bank[n % BANKS][0:64, 0:T], ACT.Copy)
                            do(x2[64:128, piece - 16, 0:T - 1], bank[n % BANKS][64:128, 1:T], ACT.Copy).then_inc(bank_free[n % BANKS], 1)
                feed(G("nat", l))
                for t in range(2):
                    n = N(("nat", l), 2 * t)
                    act_.wait_ge(bank_full[n % BANKS], n // BANKS + 1)
                    do(vn[:, 0:2, t, :], ps(n).rearrange("p (a b) -> p a b", a=2), ACT.Copy).then_inc(bank_free[n % BANKS], 1)
                    n += 1
                    act_.wait_ge(bank_full[n % BANKS], n // BANKS + 1)
                    do(vn[:, 2, t, :], ps(n, 0, T), ACT.Copy)
                    do(vsw[:, t, :], ps(n, T, T + 140), ACT.Copy).then_inc(bank_free[n % BANKS], 1)
                act_.wait_ge(bank_free[N(("nat", l), 1) % BANKS], N(("nat", l), 1) // BANKS + 1)
                act_.wait_ge(bank_free[N(("nat", l), 3) % BANKS], N(("nat", l), 3) // BANKS + 1)
                do(lam[:, 16:40].rearrange("p (a b) -> p a b", a=2), vsw[:, :, 128:140], ACT.Exp, scale=-1.0
                   ).then_inc(gate_exp, 1)
                for i in range(4):
                    act_.wait_ge(bank_free[N(("hidT", l)) % BANKS], N(("hidT", l)) // BANKS + 1)
                    do(hidg[:, i, :], hid[:, i, :], ACT.Gelu_apprx_tanh, bias=hid[:, i, 15:16]).then_inc(hid_ready, 1)
                n = N(("kc", l))
                act_.wait_ge(bank_full[n % BANKS], n // BANKS + 1)
                do(kcT, ps(n, 0, 16), ACT.Copy).then_inc(bank_free[n % BANKS], 1)
                n = N(("vc", l))
                act_.wait_ge(bank_full[n % BANKS], n // BANKS + 1)
                do(vc[0:16, :], bank[n % BANKS][0:16, 0:64], ACT.Copy).then_inc(bank_free[n % BANKS], 1)
                for i in range(NU + 3):
                    if i < NU:
                        u, s, t = UNITS[i], sbuf[:, i % 3, :], tbuf[:, i % 2, :]
                        act_.wait_ge(logits_ready, seen(logits_ready))
                        if u["kind"] == "sb":
                            do(t, s, ACT.Abs).then_inc(act_own, 1)
                            act_.wait_ge(act_own, own(act_own))
                            do(t, t, ACT.Exp, scale=-1.0).then_inc(act_own, 1)
                            act_.wait_ge(act_own, own(act_own))
                            do(t, t, ACT.Ln, bias=one[:, :]).then_inc(exp_ready, 1)
                        elif u["kind"] == "cmp":
                            do(s[:, 0:16], s[:, 0:16], ACT.Exp, bias=st[:, i, 0:1])
                            do(s[:, 16:32], s[:, 16:32], ACT.Exp, bias=st[:, i, 1:2]).then_inc(exp_ready, 1)
                        else:
                            do(s[:, 0:128], s[:, 0:128], ACT.Exp, bias=st[:, i, 0:1], accum_out=st[:, i, 2:3])
                            do(s[:, 128:384], s[:, 128:384], ACT.Exp, bias=st[:, i, 1:2],
                               accum_out=st[:, i, 3:4]).then_inc(exp_ready, 1)
                    if i < ADA_W:
                        n = N(("ada", l, i))
                        act_.wait_ge(bank_full[n % BANKS], n // BANKS + 1)
                        do(arow[:, i % 2, :], bank[n % BANKS][0:2, 0:T], ACT.Copy).then_inc(mod_rows, 1)
                    if 0 <= i - 1 < NU and UNITS[i - 1]["kind"] == "sb":
                        s = sbuf[:, (i - 1) % 3, :]
                        act_.wait_ge(arg_ready, seen(arg_ready))
                        do(s, s, ACT.Exp).then_inc(sb_ready, 1)
                    if 0 <= i - 2 < NU:
                        j = i - 2
                        n = N(("PT", l, j))
                        act_.wait_ge(bank_full[n % BANKS], n // BANKS + 1)
                        if UNITS[j]["kind"] == "cmp":
                            do(ptb[0:16, j % 2, 0:256], bank[n % BANKS][0:16, 0:256], ACT.Copy).then_inc(bank_free[n % BANKS], 1)
                        else:
                            do(ptb[:, j % 2, :], ps(n, 0, 384), ACT.Copy).then_inc(bank_free[n % BANKS], 1)
                    if 0 <= i - 3 < NU and UNITS[i - 3]["last"]:
                        u, n = UNITS[i - 3], N(("O", l, i - 3))
                        act_.wait_ge(bank_full[n % BANKS], n // BANKS + 1)
                        half = slice(u["row"], u["row"] + 64)
                        do(mixed[half, u["chunk"], :], bank[n % BANKS][half, 0:T], ACT.Copy).then_inc(bank_free[n % BANKS], 1)
                act_.wait_ge(bank_free[N(("O", l, NU - 1)) % BANKS], N(("O", l, NU - 1)) // BANKS + 1)
                squares(relu[:, 0, :].rearrange("p (a b) -> p a b", a=2), mixed[:, 6:8, :])
                feed_to(G("out", l).q0 + 2)
                rstd(N(("dfn", l)), 512, HD)
                act_.wait_ge(dfn_ready, l + 1)
                feed(G("out", l))
                norm_squares(("out", l))
                rstd(N(("rms2", l)), T, D)
                for i in range(4):
                    g = G("up", l, i)
                    feed(g, int(i < 3))
                    for p in range(8):
                        n = N(g.name) + p
                        act_.wait_ge(bank_full[n % BANKS], n // BANKS + 1)
                        if 8 * i + p >= 4:
                            act_.wait_ge(act_ready, seen(act_ready))
                        do(relu[:, (p % 4) // 2, (p % 2) * T:(p % 2 + 1) * T], ps(n, 0, T), ACT.Relu).then_inc(bank_free[n % BANKS], 1)
                act_.wait_ge(act_ready, seen(act_ready, 4))
                feed(G("down", l))
            norm_squares(("down", DEPTH - 1))
            rstd(N("rmsf"), T, D)


            def scale_residual(fresh, lo, half):
                act_.wait_ge(h_ready, KD * (fresh + 1))
                x = xT[:, half * KD // 2:(half + 1) * KD // 2, lo:]
                do(x, x, ACT.Copy, scale=ALPHA).then_inc(scaled_ready, 1)

            def centre_tap(dst, n, cols, w, b):
                return do(dst, ps(n, 0, cols), ACT.Identity, scale=w[:, 1:2], bias=b)

            for i in range(5):
                if i < 4:
                    nxt = G("m_up", i)
                for k in range(KD):
                    if i < 4:
                        feed_to(nxt.q0 + k)
                    if i and 1 <= k < 3:
                        for p in range(2 * k - 2, 2 * k):
                            j = 4 * (i - 1) + p
                            n = N(("m_up", i - 1), p)
                            act_.wait_ge(bank_full[n % BANKS], n // BANKS + 1)
                            if j >= 4:
                                act_.wait_ge(silu_ready, j - 3)
                            centre_tap(mqk[:, j % 4, :], n, T2, par_at("mconv_w", 3 * j, 3), par_at("mconv_b", j))
                            do(xm[:, j, :], ps(n), ACT.Copy).then_inc(bank_free[n % BANKS], 1)
                    if i and 2 <= k < 6:
                        j = 4 * (i - 1) + k - 2
                        act_.wait_ge(conv_ready, seen(conv_ready))
                        do(xc[:, j, :], mqk[:, j % 4, :], ACT.Silu).then_inc(silu_ready, 1)
                    if i == 1 and k >= 6:
                        scale_residual(4, 0, k - 6)
            act_.wait_ge(bank_free[N("m_gates") % BANKS], N("m_gates") // BANKS + 1)
            do(grow[64:128, 1, :], grow[64:128, 0, :], ACT.Abs).then_inc(act_own, 1)
            act_.wait_ge(act_own, own(act_own))
            do(grow[64:128, 1, :], grow[64:128, 1, :], ACT.Exp, scale=-1.0).then_inc(act_own, 1)
            act_.wait_ge(act_own, own(act_own))
            do(grow[64:128, 1, :], grow[64:128, 1, :], ACT.Ln, bias=one[64:128, :]).then_inc(lng_ready, 1)
            feed_to(G("m_v", 0).q0 + 9)
            act_.wait_ge(rows_ready, seen(rows_ready))
            do(rows[0:64, 1, :], rows[0:64, 1, :], ACT.Exp, scale=-1.0).then_inc(floor_ready, 1)
            for h in range(MH):
                feed(G("m_v", h), 2)
                for t in range(4):
                    n = N(("m_v", h), t)
                    act_.wait_ge(bank_full[n % BANKS], n // BANKS + 1)
                    do(mv[:, t, h * T2:(h + 1) * T2], ps(n), ACT.Copy).then_inc(bank_free[n % BANKS], 1)
                if h == 0:
                    n = N("m_aT")
                    act_.wait_ge(bank_full[n % BANKS], n // BANKS + 1)
                    do(aT.rearrange("p a b -> p (a b)"), ps(n, 0, 256), ACT.Copy).then_inc(bank_free[n % BANKS], 1)
            for h in range(MH):
                g = G("m_qk", h)
                feed_to(g.q0 + 5)
                if h:
                    rstd(N(("m_rms", h - 1)), T2, T2)
                for z, spans in enumerate((((0, 512), (640, 1280), (1408, 1536)), ((0, 128), (256, 1152), (1280, 1536)))):
                    feed_to(g.q0 + 5 + 5 * z)
                    act_.wait_ge(D_ready, seen(D_ready))
                    for lo, hi in spans:
                        ins = do(mP[:, z, lo:hi], mP[:, z, lo:hi], ACT.Exp, scale=-1.0)
                    ins.then_inc(E_ready, 1)
                feed(g)
                for j in range(4):
                    n = N(("m_qk", h), j)
                    act_.wait_ge(bank_full[n % BANKS], n // BANKS + 1)
                    (do(mqk[:, j, :], ps(n), ACT.Copy, scale=1.0 if j < 2 else 1.0 / 16)).then_inc(bank_free[n % BANKS], 1)
                feed(G("m_og", h), int(h < 3))
                for j in range(4):
                    n = N(("m_og", h), j)
                    act_.wait_ge(bank_full[n % BANKS], n // BANKS + 1)
                    do(og[:, j, :], ps(n), ACT.Sigmoid).then_inc(bank_free[n % BANKS], 1)
                act_.wait_ge(bank_free[N(("m_PV", h), 3) % BANKS], N(("m_PV", h), 3) // BANKS + 1)
                do(mqk.rearrange("p a b -> p (a b)"), hs[:, 4 * h:4 * h + 4, :].rearrange("p a b -> p (a b)"), ACT.Square
                   ).then_inc(sq_ready, 1)
            rstd(N(("m_rms", MH - 1)), T2, T2)
            act_.wait_ge(hs_ready, 2 * MH)
            feed(G("m_out"))

            def layer_norm(i, lo):
                for k in range(KD):
                    act_.wait_ge(centred_ready, KD * i + k + 1)
                    squares(sq2[:, k, lo:], xT[:, k, lo:])
                rstd(N(("var", i)), T2 - lo, D)

            def ffn(l, lo):
                groups, per = ((NFF // 2, 2), (6, 4))[l]
                for i in range(groups + 1):
                    last = i == groups
                    nxt = G("ffn_out", l) if last else G("ffn_in", l, i)
                    before = G("ffn_in", l, i - 1).tickets // 2 if i else 0
                    start = int(l == 0 and not last)
                    for k in range(KD):
                        feed_to(nxt.q0 + k)
                        for p in range(before):
                            if k != start + 2 * p // before:
                                continue
                            j = per * (i - 1) + p
                            n = N(G("ffn_in", l, i - 1).name) + 2 * p
                            act_.wait_ge(bank_full[n % BANKS], n // BANKS + 1)
                            if j >= 4:
                                act_.wait_ge(ffa_ready, NFF * l + j - 3)
                            centre_tap(ctmp[:, j % 4, lo:], n, T2 - lo, par_at(("fconv_w", l), 3 * j, 3),
                                       par_at(("fconv_b", l), j)).then_inc(centre_ready, 1)
                            do(graw[:, j % 4, lo:], ps(n, 0, T2 - lo), ACT.Copy).then_inc(bank_free[n % BANKS], 1)
                            n += 1
                            act_.wait_ge(bank_full[n % BANKS], n // BANKS + 1)
                            do(fup[:, j % 4, lo:], ps(n, 0, T2 - lo), ACT.Copy).then_inc(bank_free[n % BANKS], 1)
                        if 2 <= k < 2 + before:
                            j = per * (i - 1) + k - 2
                            c = ctmp[:, j % 4, lo:]
                            act_.wait_ge(conv_ready, seen(conv_ready))
                            do(c, c, ACT.Silu).then_inc(act_silu, 1)
                        if i == 1 and k >= 6:
                            scale_residual((5, 7)[l], lo, k - 6)
                    if last:
                        feed(nxt)

            layer_norm(0, 0)
            ffn(0, 0)
            layer_norm(1, 0)

            feed(G("a_dkv"), 2)
            for j in range(2):
                n = N("a_dkv", j)
                act_.wait_ge(bank_full[n % BANKS], n // BANKS + 1)
                do(ckv[:, j, :], ps(n), ACT.Copy).then_inc(bank_free[n % BANKS], 1)
            act_.wait_ge(bank_free[n % BANKS], n // BANKS + 1)
            do(cks[:, 0:2, :], ckv, ACT.Square).then_inc(sq_ready, 1)
            feed(G("a_dq"))
            for j in range(3):
                n = N("a_dq", j)
                act_.wait_ge(bank_full[n % BANKS], n // BANKS + 1)
                do(cq[:, j, :], ps(n, 0, T), ACT.Copy).then_inc(bank_free[n % BANKS], 1)
            act_.wait_ge(bank_free[n % BANKS], n // BANKS + 1)
            rstd(N("a_kvn"), T2, T2 // 2)
            do(cks[:, :, 0:T], cq, ACT.Square).then_inc(sq_ready, 1)
            act_.wait_ge(ckn_ready, 1)
            rstd(N("a_qn"), T, 384)
            feed(G("a_ukv"), 1)
            for h in range(AH):
                n = N("a_ukv", h)
                act_.wait_ge(bank_full[n % BANKS], n // BANKS + 1)
                do(kn[:, h, :], ps(n), ACT.Copy).then_inc(bank_free[n % BANKS], 1)
            act_.wait_ge(ckn_ready, 2)
            feed(G("a_v"), 1)
            for t in range(4):
                for c in range(2):
                    n = N("a_v", 2 * t + c)
                    act_.wait_ge(bank_full[n % BANKS], n // BANKS + 1)
                    do(av[:, t, c * T2:(c + 1) * T2], ps(n), ACT.Copy).then_inc(bank_free[n % BANKS], 1)
            for half in range(2):
                scale_residual(6, LAT, half)
            feed(G("a_uq", 0), 1)
            for h in range(AH):
                n = N(("a_uq", 0), h)
                act_.wait_ge(bank_full[n % BANKS], n // BANKS + 1)
                do(qn[:, h, :], ps(n, 0, T), ACT.Copy).then_inc(bank_free[n % BANKS], 1)
            feed(G("a_uq", 1))
            for i in range(2 * AH + 4):
                if i < 2 * AH:
                    n = N(("aS", i))
                    act_.wait_ge(amax_ready, seen(amax_ready))
                    do(ap_[:, i % 3, :], ps(n), ACT.Exp, bias=ast[:, i, 1:2], scale=A_SCALE,
                               accum_out=ast[:, i, 2:3]).then_inc(bank_free[n % BANKS], 1)
                if 0 <= i - 2 < 2 * AH:
                    j = i - 2
                    n = N(("aPT", j))
                    act_.wait_ge(bank_full[n % BANKS], n // BANKS + 1)
                    do(apt[:, (j // 2) % 2, :, (j % 2) * P:(j % 2 + 1) * P], ps(n).rearrange("p (a b) -> p a b", a=4),
                               ACT.Copy).then_inc(bank_free[n % BANKS], 1)
                if i >= 4 and i % 2 == 0 and (i - 4) // 2 < AH:
                    h = (i - 4) // 2
                    n = N(("aO", h))
                    act_.wait_ge(bank_full[n % BANKS], n // BANKS + 1)
                    do(aoT[:, h, :], ps(n, 0, T), ACT.Copy).then_inc(bank_free[n % BANKS], 1)
            act_.wait_ge(bank_free[N(("aO", AH - 1)) % BANKS], N(("aO", AH - 1)) // BANKS + 1)
            feed(G("a_out"))
            layer_norm(2, LAT)
            ffn(1, LAT)
            layer_norm(3, LAT)
            for t in range(2):
                for c in range(2):
                    n = N("oT", 2 * t + c)
                    act_.wait_ge(bank_full[n % BANKS], n // BANKS + 1)
                    ins = do(osb[:, t, c * T2:(c + 1) * T2], ps(n), ACT.Copy)
            ins.then_inc(out_copied, 1)

        @block.vector
        def _(dve):
            seen = Count()
            own = Count()
            v = nc.vector
            stt = v.scalar_tensor_tensor

            fed = {"w": 0, "q": 0}

            def weights_to(s_):
                while fed["w"] <= s_:
                    i = fed["w"]
                    w = ST.split[i][0]
                    for half in range(2):
                        c = slice(half * SLOT // 2, (half + 1) * SLOT // 2)
                        dve.wait_ge(w_high, 2 * i + half + 1)
                        ins = v.tensor_tensor(ws[:, i % 2, 1, c], ring[:, w % R, c], ws[:, i % 2, 0, c].bitcast(F32), ALU.subtract)
                    ins.then_inc(slot_done, 1)
                    fed["w"] += 1

            def feed_to(q_):
                while fed["q"] <= q_:
                    q = fed["q"]
                    g, k, _, _, before = ST.chunks[q]
                    s_ = g.s0 + k // g.kc
                    weights_to(s_)
                    if g.src == "ffa":
                        dve.wait_ge(ffa_ready, NFF * g.name[1] + k + 1)
                    elif g.fresh is not None:
                        dve.wait_ge(h_ready, KD * g.fresh + k + 1)
                    dve.wait_ge(x_high, q + 1)
                    v.tensor_tensor(split_x(q, 1), source(g, k), split_x(q, 0).bitcast(F32),
                                    ALU.subtract).then_inc(x_done, 1)
                    fed["q"] += 1
                    if (k % g.kc == 1 or k == g.K - 1) and follows(s_):
                        weights_to(s_ + 1)

            def feed(g, more=0):
                feed_to(g.q0 + g.K - 1 + more)

            def normed(gain, g):
                dve.wait_ge(rstd_ready, seen(rstd_ready))
                for k in range(KD + 1):
                    if k < KD:
                        stt(hT[:, k, LAT:], xT[:, k, LAT:], par_at(gain, k), stat[:, 0, 0:T], ALU.mult, ALU.mult
                            ).then_inc(h_ready, 1)
                    if k:
                        feed_to(g.q0 + k - 1)

            v.memset(eps[:, :], EPS).then_inc(small_ready, 1)
            v.memset(one[:, :], 1.0).then_inc(small_ready, 1)
            v.memset(cbias, NEG).then_inc(dve_own, 1)
            dve.wait_ge(dve_own, own(dve_own))
            dve.wait_ge(dma_par, 32)
            dve.wait_ge(dma_con, 16)
            for l in range(DEPTH):
                lam_init = 0.8 - 0.6 * math.exp(-0.3 * l)
                dl = par1_at(("dlam", l), 0, 128).rearrange("p (a b c) -> p a b c", a=2, b=2)
                prod = lamp.rearrange("p (a c) -> p a c", a=2)
                v.tensor_tensor(prod, dl[:, :, 0, :], dl[:, :, 1, :], ALU.mult).then_inc(dve_own, 1)
                dve.wait_ge(dve_own, own(dve_own))
                v.tensor_reduce(lam[:, 0:2], prod, AX, ALU.add).then_inc(lam_sum, 1)
                normed(("g_attn", l), G("proj", l, 0))
                dve.wait_ge(lam_exp, seen(lam_exp))
                v.tensor_tensor(lam[:, 4:5], lam[:, 3:4], lam[:, 2:3], ALU.subtract).then_inc(dve_own, 1)
                dve.wait_ge(dve_own, own(dve_own))
                v.tensor_scalar(lam[:, 5:6], lam[:, 4:5], -lam_init, None, ALU.add).then_inc(dve_own, 1)
                dve.wait_ge(dve_own, own(dve_own))
                v.tensor_scalar(lam[:, 6:7], par_at(("subln", l)), 1.0 - lam_init, None, ALU.mult).then_inc(dve_own, 1)
                dve.wait_ge(dve_own, own(dve_own))
                for i in range(3):
                    feed(G("proj", l, i), 1)
                dve.wait_ge(bank_free[N(("proj", l, 2)) % BANKS], N(("proj", l, 2)) // BANKS + 1)
                dve.wait_ge(bank_free[N(("proj", l, 2), 1) % BANKS], N(("proj", l, 2), 1) // BANKS + 1)
                for b in range(2):
                    xv = x2[:, b, :].rearrange("p (c j e) -> p e j c", j=8, e=2)
                    v.tensor_copy(x3[:, b, 0:8, 0:CMP_N], xv[:, 0, :, 0:15])
                    v.tensor_copy(x3[:, b, 8:16, 0:CMP_N], xv[:, 0, :, 1:16])
                    ins = v.tensor_copy(x3[:, b, :, 15], par1_at(("pos", l), 16 * b, 16))
                ins.then_inc(x3_ready, 1)
                feed(G("nat", l))
                for i in range(4):
                    n = N(("hid", l), i)
                    dve.wait_ge(bank_full[n % BANKS], n // BANKS + 1)
                    v.tensor_copy(hrow[:, i, :], bank[n % BANKS][0:16, 0:P]).then_inc(bank_free[n % BANKS], 1)
                n = N(("hidT", l))
                dve.wait_ge(bank_full[n % BANKS], n // BANKS + 1)
                v.tensor_copy(hid.rearrange("p a b -> p (a b)"), ps(n, 0, 64)).then_inc(bank_free[n % BANKS], 1)
                dve.wait_ge(gate_exp, seen(gate_exp))
                v.tensor_scalar(lam[:, 16:40], lam[:, 16:40], 1.0, None, ALU.add).then_inc(dve_own, 1)
                dve.wait_ge(dve_own, own(dve_own))
                v.reciprocal(lam[:, 16:40], lam[:, 16:40]).then_inc(dve_own, 1)
                dve.wait_ge(dve_own, own(dve_own))
                gates = lam[:, 16:40].rearrange("p (a b) -> p a b", a=2)
                if l == 0:
                    dve.wait_ge(dma_bias, 32)
                    v.tensor_copy(bias[:, :, 0:128], hankel[:, :, 0:128][:, :, ::-1])
                    v.tensor_copy(bias[:, :, 128:384], hankel[:, :, ::-1])
                    for q in range(2):
                        ins = v.tensor_copy(cbias[:, :, 16 * q:16 * q + CMP_N], tz[:, :, P * q:P * q + 225:16][:, :, ::-1])
                    ins.then_inc(dve_own, 1)
                    dve.wait_ge(dve_own, own(dve_own))
                for i in range(NU + 1):
                    if i < NU:
                        u, s, n = UNITS[i], sbuf[:, i % 3, :], N(("S", l, i))
                    if 1 <= i <= ADA_W + 1:
                        n = N(("ada", l, i - 1))
                        dve.wait_ge(bank_full[n % BANKS], n // BANKS + 1)
                        if i <= ADA_W:
                            dve.wait_ge(mod_rows, seen(mod_rows))
                        if i == 1:
                            v.tensor_copy(scrap[:, 0:1], eps[:, :]).then_inc(bank_free[n % BANKS], 1)
                        else:
                            c = 4 * (i - 2)
                            v.tensor_tensor(mod[:, l, c:c + 4], ps(n, T, T + 4), par1_at(("ada_b", l), c, 4), ALU.add).then_inc(bank_free[n % BANKS], 1)
                    if i < NU:
                        n = N(("S", l, i))
                        scale = u["kk"] ** -0.5
                        dve.wait_ge(bank_full[n % BANKS], n // BANKS + 1)
                        if u["kind"] == "sb":
                            stt(s, ps(n, 0, 384), scale, par1_at("strict", 0, 384), ALU.mult, ALU.add).then_inc(bank_free[n % BANKS], 1)
                            dve.wait_ge(bank_free[n % BANKS], n // BANKS + 1)
                            v.tensor_scalar(tbuf[:, 2 + i % 2, :], s, 0.0, None, ALU.max).then_inc(logits_ready, 1)
                        elif u["kind"] == "cmp":
                            stt(s[:, 0:32], ps(n, 0, 32), scale, cbias[:, u["h"], :], ALU.mult, ALU.add).then_inc(bank_free[n % BANKS], 1)
                            dve.wait_ge(bank_free[n % BANKS], n // BANKS + 1)
                            v.tensor_reduce(st[:, i, 0:2], s[:, 0:32].rearrange("p (a b) -> p a b", a=2), AX, ALU.max,
                                            negate=True).then_inc(logits_ready, 1)
                        else:
                            stt(s, ps(n, 0, 384), scale, bias[:, u["bias"], :], ALU.mult, ALU.add).then_inc(bank_free[n % BANKS], 1)
                            dve.wait_ge(bank_free[n % BANKS], n // BANKS + 1)
                            v.tensor_reduce(st[:, i, 0:1], s[:, 0:128], AX, ALU.max, negate=True)
                            v.tensor_reduce(st[:, i, 1:2], s[:, 128:384], AX, ALU.max, negate=True
                                            ).then_inc(logits_ready, 1)
                    if i >= 1:
                        j = i - 1
                        u, s = UNITS[j], sbuf[:, j % 3, :]
                        dve.wait_ge(exp_ready, seen(exp_ready))
                        if u["kind"] == "sb":
                            t, m = tbuf[:, j % 2, :], tbuf[:, 2 + j % 2, :]
                            for lo, hi in ((0, 128), (128, 384)):
                                ins = v.tensor_tensor_scan(t[:, lo:hi][:, ::-1], m[:, lo:hi][:, ::-1],
                                                           t[:, lo:hi][:, ::-1], 0.0, ALU.add, ALU.add)
                            ins.then_inc(dve_own, 1)
                            dve.wait_ge(dve_own, own(dve_own))
                            v.tensor_tensor(s, s, t, ALU.subtract).then_inc(arg_ready, 1)
                            continue
                        w = 128
                        if u["kind"] == "cmp":
                            w = 16
                            v.tensor_tensor(s[:, 0:32], s[:, 0:32], par1_at("cmask", 0, 32), ALU.mult).then_inc(dve_own, 1)
                            dve.wait_ge(dve_own, own(dve_own))
                            v.tensor_reduce(st[:, j, 2:4], s[:, 0:32].rearrange("p (a b) -> p a b", a=2), AX,
                                                     ALU.add).then_inc(dve_own, 1)
                            dve.wait_ge(dve_own, own(dve_own))
                            v.tensor_scalar(st[:, j, 2:4], st[:, j, 2:4], 1e-30, None, ALU.max).then_inc(dve_own, 1)
                            dve.wait_ge(dve_own, own(dve_own))
                        v.reciprocal(st[:, j, 4:6], st[:, j, 2:4]).then_inc(dve_own, 1)
                        dve.wait_ge(dve_own, own(dve_own))
                        if "gate" in u:
                            v.tensor_tensor(st[:, j, 4:6], st[:, j, 4:6], gates[:, :, u["gate"]], ALU.mult).then_inc(dve_own, 1)
                            dve.wait_ge(dve_own, own(dve_own))
                        if u.get("c"):
                            v.tensor_scalar(st[:, j, 4:6], st[:, j, 4:6], lam[:, 5:6], None, ALU.mult).then_inc(dve_own, 1)
                            dve.wait_ge(dve_own, own(dve_own))
                        end = 32 if u["kind"] == "cmp" else 384
                        v.tensor_scalar(s[:, 0:w], s[:, 0:w], st[:, j, 4:5], None, ALU.mult)
                        v.tensor_scalar(s[:, w:end], s[:, w:end], st[:, j, 5:6], None, ALU.mult).then_inc(p_ready, 1)
                dve.wait_ge(bank_free[N(("ada", l, ADA_W)) % BANKS], N(("ada", l, ADA_W)) // BANKS + 1)
                for c in (16, 64):
                    ins = v.tensor_scalar(mod[:, l, c:c + 16], mod[:, l, c:c + 16], 1.0, None, ALU.add)
                ins.then_inc(dve_own, 1)
                dve.wait_ge(dve_own, own(dve_own))
                for n in range(N(("O", l, NU - 1)) - BANKS + 1, N(("O", l, NU - 1)) + 1):
                    dve.wait_ge(bank_free[n % BANKS], n // BANKS + 1)
                feed_to(G("out", l).q0 + 2)
                dve.wait_ge(rstd_ready, seen(rstd_ready))
                m = mixed[:, 6:8, :]
                stt(m, m, lam[:, 6:7], stat[:, 0, :].rearrange("p (a b) -> p a b", a=2), ALU.mult, ALU.mult).then_inc(dfn_ready, 1)
                dve.wait_ge(dfn_ready, own(dfn_ready))
                feed(G("out", l))

                def residual(name):
                    for g in range(KD):
                        n = N((name, l), g)
                        dve.wait_ge(bank_full[n % BANKS], n // BANKS + 1)
                        v.tensor_tensor(xT[:, g, LAT:], xT[:, g, LAT:], ps(n, 0, T), ALU.add).then_inc(bank_free[n % BANKS], 1)

                residual("out")
                normed(("g_mlp", l), G("up", l, 0))
                for i in range(4):
                    g = G("up", l, i)
                    feed(g, int(i < 3))
                    for p in range(8):
                        dve.wait_ge(bank_free[(N(g.name) + p) % BANKS], (N(g.name) + p) // BANKS + 1)
                        r = relu[:, (p % 4) // 2, (p % 2) * T:(p % 2 + 1) * T]
                        ins = v.tensor_tensor(act[:, 8 * i + p, :], r, r, ALU.mult)
                        if i == 3 and p == 7:
                            ins.then_inc(act_ready, 1)
                            dve.wait_ge(act_ready, own(act_ready))
                        else:
                            own(act_ready)
                            ins.then_inc(act_ready, 1)
                feed(G("down", l))
                residual("down")

            def mod_at(l, part, k, seg):
                c = 2 * (KD * part + k) + 1 - seg
                return mod[:, l, c:c + 1]

            def modulate(l, part, k, segs=(0, 1)):
                for seg in segs:
                    t = slice(seg * T, seg * T + T)
                    ins = v.tensor_scalar(hT[:, k, t], xT[:, k, t], mod_at(l, part + 1, k, seg), mod_at(l, part, k, seg),
                                          ALU.mult, ALU.add)
                ins.then_inc(h_ready, 1)

            def outer_taps(dst, src, w, segs):
                d3, s3 = (a.rearrange("p (a b) -> p a b", a=segs) for a in (dst, src))
                stt(d3[:, :, 1:T], s3[:, :, 0:T - 1], w[:, 0:1], d3[:, :, 1:T], ALU.mult, ALU.add).then_inc(dve_own, 1)
                dve.wait_ge(dve_own, own(dve_own))
                stt(d3[:, :, 0:T - 1], s3[:, :, 1:T], w[:, 2:3], d3[:, :, 0:T - 1], ALU.mult, ALU.add).then_inc(conv_ready, 1)

            dve.wait_ge(rstd_ready, seen(rstd_ready))
            for k in range(KD):
                stt(xT[:, k, LAT:], xT[:, k, LAT:], par_at("g_final", k), stat[:, 0, 0:T], ALU.mult, ALU.mult
                    ).then_inc(dve_own, 1)
                if k:
                    feed_to(G("m_up", 0).q0 + k - 1)
                dve.wait_ge(dve_own, own(dve_own))
                modulate(0, 0, k)
            for i in range(5):
                if i < 4:
                    nxt = G("m_up", i)
                for k in range(KD):
                    if i < 4:
                        feed_to(nxt.q0 + k)
                    if i and 1 <= k < 5:
                        j = 4 * (i - 1) + k - 1
                        n = N(("m_up", i - 1), k - 1)
                        dve.wait_ge(bank_free[n % BANKS], n // BANKS + 1)
                        outer_taps(mqk[:, j % 4, :], xm[:, j, :], par_at("mconv_w", 3 * j, 3), 2)
            n = N("m_gates")
            dve.wait_ge(bank_full[n % BANKS], n // BANKS + 1)
            v.tensor_scalar(grow[0:64, 0, :], bank[n % BANKS][0:64, :], par_at("b_gates")[0:64, :], None, ALU.add
                            ).then_inc(slot_done, 1)
            v.tensor_scalar(grow[64:128, 0, :], bank[n % BANKS][64:128, :], par_at("b_gates")[64:128, :], None,
                                    ALU.add).then_inc(bank_free[n % BANKS], 1)
            dve.wait_ge(bank_free[n % BANKS], n // BANKS + 1)
            v.tensor_scalar(grow[64:128, 2, :], grow[64:128, 0, :], 0.0, None, ALU.min).then_inc(dve_own, 1)
            dve.wait_ge(dve_own, own(dve_own))
            feed_to(G("m_v", 0).q0)
            dve.wait_ge(lng_ready, seen(lng_ready))

            q = G("m_v", 0).q0

            def both_ways(dst, a, b, base, op0, op1, q):
                f = slice(base, base + 32)
                g = slice(base + 32, base + 64)
                v.tensor_tensor_scan(dst[f, :], a[f, :], b[f, :], 0.0, op0, op1)
                v.tensor_tensor_scan(dst[g, 0:T][:, ::-1], a[g, 0:T][:, ::-1], b[g, 0:T][:, ::-1], 0.0, op0, op1).then_inc(dve_own, 1)
                feed_to(q + 1)
                dve.wait_ge(dve_own, own(dve_own))
                v.tensor_tensor_scan(dst[g, T:T2][:, ::-1], a[g, T:T2][:, ::-1], b[g, T:T2][:, ::-1], dst[g, 0:1],
                                              op0, op1).then_inc(dve_own, 1)
                feed_to(q + 2)
                dve.wait_ge(dve_own, own(dve_own))

            both_ways(grow[:, 3, :], grow[:, 2, :], grow[:, 1, :], 64, ALU.add, ALU.subtract, q)
            v.tensor_copy(grow[0:64, 4, :], grow[64:128, 3, :]).then_inc(dve_own, 1)
            feed_to(q + 3)
            dve.wait_ge(dve_own, own(dve_own))
            v.tensor_tensor(grow[0:64, 5, :], grow[0:64, 0, :], grow[0:64, 4, :], ALU.subtract).then_inc(dve_own, 1)
            feed_to(q + 4)
            dve.wait_ge(dve_own, own(dve_own))
            both_ways(rows[:, 0, :], grow[:, 5, :], grow[:, 5, :], 0, ALU.max, ALU.max, q + 4)
            v.tensor_tensor(rows[0:64, 1, :], grow[0:64, 4, :], rows[0:64, 0, :], ALU.add).then_inc(rows_ready, 1)
            for h in range(MH):
                feed(G("m_v", h), 2)
            dve.wait_ge(floor_ready, seen(floor_ready))
            dve.wait_ge(bank_free[N("m_aT") % BANKS], N("m_aT") // BANKS + 1)
            v.memset(mP[:, 1, 128:256], 0.0)
            v.memset(mP[:, 1, 1152:1280], 0.0).then_inc(dve_own, 1)
            dve.wait_ge(dve_own, own(dve_own))
            spans = (((0, 512), (128, 512), (256, 512), (384, 512)), ((0, 512), (0, 512), (256, 384), (256, 512)))

            def normed_head(h, half):
                if half == 0:
                    dve.wait_ge(rstd_ready, seen(rstd_ready))
                for k in range(4 * h + 2 * half, 4 * h + 2 * half + 2):
                    ins = stt(hs[:, k, :], hs[:, k, :], par_at("m_norm", k), stat[:, 0, :], ALU.mult, ALU.mult)
                ins.then_inc(hs_ready, 1)
                dve.wait_ge(hs_ready, own(hs_ready))

            for h in range(MH):
                g = G("m_qk", h)
                feed_to(g.q0 + 1)
                v.memset(mP[:, 0, 512:640], 0.0)
                v.memset(mP[:, 0, 1280:1408], 0.0).then_inc(dve_own, 1)
                dve.wait_ge(dve_own, own(dve_own))
                for z in range(2):
                    feed_to(g.q0 + 3 + 5 * z)
                    n = N(("m_max", h), z)
                    dve.wait_ge(bank_full[n % BANKS], n // BANKS + 1)
                    r = 32 * z + h
                    for s_ in range(4):
                        parts = [spans[z][s_]] if (z, s_) != (1, 0) else [(0, 128), (256, 512)]
                        for lo, hi in parts:
                            ins = v.tensor_scalar(mP[:, z, OFF[s_] + lo - T_AT[s_]:OFF[s_] + hi - T_AT[s_]], ps(n, lo, hi),
                                                  aT[:, s_, r:r + 1], 0.0, ALU.subtract, ALU.max)
                    ins.then_inc(bank_free[n % BANKS], 1)
                    dve.wait_ge(bank_free[n % BANKS], n // BANKS + 1)
                    feed_to(g.q0 + 4 + 5 * z)
                    for s_ in range(4):
                        d = OFF[s_] + s_ * P - T_AT[s_]
                        ins = v.tensor_tensor(mP[:, z, d:d + P], mP[:, z, d:d + P], con_at("tri", 256)[:, z * P:(z + 1) * P],
                                              ALU.max)
                    ins.then_inc(D_ready, 1)
                    feed_to(g.q0 + 5 + 5 * z)
                    if h and z == 0:
                        for half in range(2):
                            feed_to(g.q0 + 6 + half)
                            normed_head(h - 1, half)
                feed(g, 2)
                for z in range(2):
                    dve.wait_ge(E_ready, seen(E_ready))
                    for s_ in range(4):
                        n = N(("m_QK", h), s_)
                        if z == 0:
                            dve.wait_ge(bank_full[n % BANKS], n // BANKS + 1)
                        p_ = mP[:, z, OFF[s_]:OFF[s_] + T2 - T_AT[s_]]
                        ins = v.tensor_tensor(p_, p_, ps(n, 0, T2 - T_AT[s_]), ALU.mult)
                        if z == 1:
                            ins.then_inc(bank_free[n % BANKS], 1)
                dve.wait_ge(bank_free[n % BANKS], n // BANKS + 1)
                gates = G("m_og", h)
                feed_to(gates.q0 + 4)
                n = N(("m_den", h))
                dve.wait_ge(bank_full[n % BANKS], n // BANKS + 1)
                dn = bank[n % BANKS][0:64, :]
                stt(rows[0:64, 2, :], dn, -1.0, rows[0:64, 1, :], ALU.mult, ALU.max).then_inc(dve_own, 1)
                dve.wait_ge(dve_own, own(dve_own))
                v.tensor_tensor(rows[0:64, 2, :], dn, rows[0:64, 2, :], ALU.max).then_inc(bank_free[n % BANKS], 1)
                dve.wait_ge(bank_free[n % BANKS], n // BANKS + 1)
                v.reciprocal(rows[0:64, 2, :], rows[0:64, 2, :]).then_inc(rden_ready, 1)
                feed_to(gates.q0 + 5)
                for z in range(2):
                    n = N(("m_rec", h), z)
                    dve.wait_ge(bank_full[n % BANKS], n // BANKS + 1)
                    for s_ in range(4):
                        p_ = mP[:, z, OFF[s_]:OFF[s_] + T2 - T_AT[s_]]
                        ins = v.tensor_tensor(p_, p_, ps(n, T_AT[s_], T2), ALU.mult)
                    ins.then_inc(bank_free[n % BANKS], 1)
                    if z == 0:
                        feed_to(gates.q0 + 6)
                dve.wait_ge(bank_free[n % BANKS], n // BANKS + 1)
                v.tensor_tensor(mP[:, 0, :], mP[:, 0, :], mP[:, 1, :], ALU.add).then_inc(W_ready, 1)
                feed(gates, int(h < MH - 1))
                for e in range(4):
                    n = N(("m_PV", h), e)
                    dve.wait_ge(bank_full[n % BANKS], n // BANKS + 1)
                    dve.wait_ge(bank_free[N(("m_og", h), e) % BANKS], N(("m_og", h), e) // BANKS + 1)
                    v.tensor_tensor(hs[:, 4 * h + e, :], ps(n), og[:, e, :], ALU.mult).then_inc(bank_free[n % BANKS], 1)
            for half in range(2):
                normed_head(MH - 1, half)

            def residual2(name, l, part, segs):
                feed(G(*name) if isinstance(name, tuple) else G(name))
                dve.wait_ge(scaled_ready, seen(scaled_ready, 2))
                for g in range(KD):
                    n = N(name, g)
                    dve.wait_ge(bank_full[n % BANKS], n // BANKS + 1)
                    for seg in segs:
                        t = slice(seg * T, seg * T + T)
                        ins = stt(xT[:, g, t], ps(n, (seg - segs[0]) * T, (seg - segs[0] + 1) * T), mod_at(l, part, g, seg),
                                  xT[:, g, t], ALU.mult, ALU.add)
                    ins.then_inc(bank_free[n % BANKS], 1)
                dve.wait_ge(bank_free[n % BANKS], n // BANKS + 1)

            def layer_norm(i, l, s_, lo, mod_by=None, g=None):
                n = N(("mean", i))
                dve.wait_ge(bank_full[n % BANKS], n // BANKS + 1)
                for k in range(KD):
                    stt(xT[:, k, lo:], ps(n, 0, T2 - lo), -1.0 / D, xT[:, k, lo:], ALU.mult, ALU.add).then_inc(centred_ready, 1)
                dve.wait_ge(centred_ready, own(centred_ready, KD))
                v.tensor_copy(scrap[:, 0:1], ps(n, 0, 1)).then_inc(bank_free[n % BANKS], 1)
                dve.wait_ge(rstd_ready, seen(rstd_ready))
                for k in range(KD):
                    stt(xT[:, k, lo:], xT[:, k, lo:], par_at(("ln_g", l, s_), k), stat[:, 0, 0:T2 - lo], ALU.mult, ALU.mult
                        ).then_inc(dve_own, 1)
                    if k and g:
                        feed_to(g.q0 + k - 1)
                    dve.wait_ge(dve_own, own(dve_own))
                    v.tensor_scalar(xT[:, k, lo:], xT[:, k, lo:], par_at(("ln_b", l, s_), k), None, ALU.add
                                    ).then_inc(ln_ready, 1)
                    if g:
                        dve.wait_ge(ln_ready, own(ln_ready))
                        modulate(*mod_by, k, (0, 1) if lo == 0 else (1,))

            def ffn(l, segs):
                lo = segs[0] * T
                groups, per = ((NFF // 2, 2), (6, 4))[l]
                for i in range(groups + 1):
                    last = i == groups
                    nxt = G("ffn_out", l) if last else G("ffn_in", l, i)
                    before = G("ffn_in", l, i - 1).tickets // 2 if i else 0
                    for k in range(KD):
                        feed_to(nxt.q0 + k)
                        if 1 <= k < 1 + before:
                            j = per * (i - 1) + k - 1
                            n = N(G("ffn_in", l, i - 1).name) + 2 * (k - 1)
                            dve.wait_ge(centre_ready, seen(centre_ready))
                            dve.wait_ge(bank_free[n % BANKS], n // BANKS + 1)
                            outer_taps(ctmp[:, j % 4, lo:], graw[:, j % 4, lo:], par_at(("fconv_w", l), 3 * j, 3), len(segs))
                        if 3 <= k < 3 + before:
                            j = per * (i - 1) + k - 3
                            n = N(G("ffn_in", l, i - 1).name) + 2 * (k - 3) + 1
                            dve.wait_ge(act_silu, seen(act_silu))
                            dve.wait_ge(bank_free[n % BANKS], n // BANKS + 1)
                            v.tensor_tensor(ffa[:, j, lo:], ctmp[:, j % 4, lo:], fup[:, j % 4, lo:], ALU.mult
                                            ).then_inc(ffa_ready, 1)
            residual2("m_out", 0, 2, (0, 1))
            layer_norm(0, 0, 0, 0, (0, 3), G("ffn_in", 0, 0))
            ffn(0, (0, 1))
            residual2(("ffn_out", 0), 0, 5, (0, 1))
            layer_norm(1, 0, 1, 0, (1, 0), G("a_dkv"))

            feed(G("a_dkv"), 2)
            n = N("a_dkv", 2)
            dve.wait_ge(bank_full[n % BANKS], n // BANKS + 1)
            rope = con_at("rope", 256)

            def rotate(dst, n, lo):
                v.tensor_tensor(rt[0:64, 0, :], bank[n % BANKS][0:64, lo:lo + T], rope[0:64, :], ALU.mult)
                v.tensor_tensor(rt[0:64, 1, :], bank[n % BANKS][64:128, lo:lo + T], rope[64:128, :], ALU.mult).then_inc(dve_own, 1)
                dve.wait_ge(dve_own, own(dve_own))
                return v.tensor_tensor(dst, rt[0:64, 0, :], rt[0:64, 1, :], ALU.add)

            v.tensor_copy(krope[0:64, 0:T], bank[n % BANKS][0:64, 0:T])
            rotate(krope[0:64, T:T2], n, T).then_inc(bank_free[n % BANKS], 1)
            dve.wait_ge(bank_free[n % BANKS], n // BANKS + 1)
            feed(G("a_dq"))
            dve.wait_ge(rstd_ready, seen(rstd_ready))
            for k in range(2):
                ins = stt(ckv[:, k, :], ckv[:, k, :], par_at("kv_norm", k), stat[:, 0, :], ALU.mult, ALU.mult)
            ins.then_inc(ckn_ready, 1)
            dve.wait_ge(ckn_ready, own(ckn_ready))
            dve.wait_ge(rstd_ready, seen(rstd_ready))
            for k in range(3):
                ins = stt(cq[:, k, :], cq[:, k, :], par_at("q_norm", k), stat[:, 0, 0:T], ALU.mult, ALU.mult)
            ins.then_inc(ckn_ready, 1)
            dve.wait_ge(ckn_ready, own(ckn_ready))
            feed(G("a_ukv"), 1)
            feed(G("a_v"), 1)
            feed(G("a_uq", 0), 1)
            feed(G("a_uq", 1))
            for i in range(2 * AH + 1):
                for h in range(2 * i, min(2 * i + 2, AH)):
                    n = N(("a_uq", 1), h)
                    dve.wait_ge(bank_full[n % BANKS], n // BANKS + 1)
                    rotate(qr[0:64, h, :], n, 0).then_inc(bank_free[n % BANKS], 1)
                    dve.wait_ge(bank_free[n % BANKS], n // BANKS + 1)
                if i < 2 * AH:
                    n = N(("aS", i))
                    dve.wait_ge(bank_full[n % BANKS], n // BANKS + 1)
                    v.tensor_reduce(ast[:, i, 0:1], ps(n), AX, ALU.max, negate=True).then_inc(dve_own, 1)
                    dve.wait_ge(dve_own, own(dve_own))
                    v.tensor_scalar(ast[:, i, 1:2], ast[:, i, 0:1], A_SCALE, None, ALU.mult).then_inc(amax_ready, 1)
                if i:
                    j = i - 1
                    dve.wait_ge(bank_free[N(("aS", j)) % BANKS], N(("aS", j)) // BANKS + 1)
                    v.reciprocal(ast[:, j, 3:4], ast[:, j, 2:3]).then_inc(dve_own, 1)
                    dve.wait_ge(dve_own, own(dve_own))
                    v.tensor_scalar(ap_[:, j % 3, :], ap_[:, j % 3, :], ast[:, j, 3:4], None, ALU.mult).then_inc(ap_ready, 1)
            residual2("a_out", 1, 2, (1,))
            layer_norm(2, 1, 0, LAT, (1, 3), G("ffn_in", 1, 0))
            ffn(1, (1,))
            residual2(("ffn_out", 1), 1, 5, (1,))
            layer_norm(3, 1, 1, LAT)


def pack_constants():
    p = np.arange(P)[:, None]
    c = np.zeros((P, CON.n), np.float32)

    def put(name, a):
        c[:, CON(name):CON(name) + a.shape[1]] = a

    put("ident", np.eye(P))
    put("ones", np.ones((P, P)))
    keys = np.arange(T)[None, :]
    strict = np.where(np.concatenate([keys[:, :P] < p, keys < p + P], 1), 0.0, NEG)
    ends = 16 * np.arange(16)[None, :] + 31
    cmask = np.concatenate([(ends <= p + P * q) & (np.arange(16) < CMP_N) for q in range(2)], 1)
    keys = np.arange(P)[None, :]
    put("tri", np.concatenate([np.where(keys >= p, 0.0, -NEG), np.where(keys <= p, 0.0, -NEG)], 1))
    pick = np.zeros((P, 127))
    pick[:, 63] = 1
    put("pick", pick)
    t = np.arange(T)
    inv = np.float32(10000.0) ** (-np.arange(16, dtype=np.float32) / np.float32(16))
    ang = [(c.astype(np.float32)[None, :] * inv[:, None]).astype(np.float32) for c in (t // 64, t % 64)]
    cos = [np.cos(a) for a in ang for _ in range(2)]
    sin = [sign * np.sin(a) for a in ang for sign in (-1, 1)]
    put("rope", np.concatenate(cos + sin, 0))
    j = np.arange(512) - (T - 1)
    near = np.maximum(j, 1).astype(np.float32)
    far = 16 + (np.log(near / np.float32(16)) / np.float32(math.log(8)) * 16).astype(np.int32)
    bucket = np.where(j < 0, 32, np.where(j < 16, j, np.minimum(far, 31)))
    onehot = (np.arange(33)[:, None] == bucket[None, :]).astype(np.float32)
    return c, onehot, strict, cmask


def cols(v):
    return np.asarray(v).reshape(-1, P).T


def pack_params1(x, strict, cmask):
    a = np.zeros((P, PAR1.n), np.float32)

    def put(name, v):
        v = np.asarray(v)
        a[:v.shape[0], PAR1(name):PAR1(name) + v.shape[1]] = v

    for l in range(DEPTH):
        pos = [np.asarray(x[k][l]).reshape(16, P).T for k in ("cmp_pos_k", "cmp_pos_v")]
        put(("pos", l), np.concatenate(pos, 1))
        put(("ada_b", l), np.repeat(cols(x["ada_b_2"][l]), 2, 1))
        k2 = np.asarray(x["cmp_k_w2"][l]).reshape(2, P, HD)
        put(("w2k", l), np.concatenate([k2[0], k2[0], k2[1], k2[1]], 1))
        v2 = np.asarray(x["cmp_v_w2"][l]).reshape(2, P, HD)
        put(("w2v", l), np.concatenate([v2[0], v2[1]], 1))
        put(("dlam", l), np.broadcast_to(np.asarray(x["diff_lambda"][l]).reshape(1, 128), (P, 128)))
    put("table", np.concatenate([np.asarray(x["rel_bias"]), np.full((1, 12), NEG, np.float32)], 0))
    put("strict", strict)
    put("cmask", cmask)
    put("halves", np.kron(np.eye(2), np.ones((HD, HD))))
    return a


def pack_params(x):
    a = np.zeros((P, PAR.n), np.float32)

    def put(name, v):
        v = np.asarray(v)
        a[:v.shape[0], PAR(name):PAR(name) + v.shape[1]] = v

    for l in range(DEPTH):
        put(("g_attn", l), cols(x["norm_attn"][l]))
        put(("g_mlp", l), cols(x["norm_mlp"][l]))
        put(("subln", l), np.tile(x["diff_subln"][l], 2)[:, None])
    put("g_final", cols(x["final_norm"]))
    for l in range(DEPTH):
        for i in range(2):
            put(("ln_g", l, i), cols(x["ln_g_2"][l][i]))
            put(("ln_b", l, i), cols(x["ln_b_2"][l][i]))
        put(("fconv_w", l), np.asarray(x["ffn_conv_w_2"][l]).reshape(3, NFF, P).transpose(2, 1, 0).reshape(P, -1))
        put(("fconv_b", l), cols(x["ffn_conv_b_2"][l]))
    conds = np.stack([cols(x["c_2"][0]), cols(x["c_ctx_2"])], 2)
    put("cond", conds.reshape(P, 16))
    put("mconv_w", np.asarray(x["m_conv_w_2"][0]).reshape(3, MK, P).transpose(2, 1, 0).reshape(P, -1))
    put("mconv_b", cols(x["m_conv_b_2"][0]))
    bg = np.zeros((P, 1), np.float32)
    for z in range(2):
        for g in range(2):
            bg[64 * g + 32 * z:64 * g + 32 * z + MH, 0] = np.asarray(x["m_b_gates_2"])[0, z, g * MH:(g + 1) * MH]
    put("b_gates", bg)
    put("m_norm", cols(x["m_norm_g_2"][0]))
    put("q_norm", cols(x["a_q_norm_2"][0]))
    put("kv_norm", cols(x["a_kv_norm_2"][0]))
    return a


def pack_stream(x):
    s = np.zeros((ST.n, P, SLOT), np.float32)
    side = np.zeros((DEPTH * SIDE_W, P, SLOT), np.float32)

    def put(w, a, kc=None, s=s):
        k = a.shape[0] // P
        full = np.zeros((kc or k, P, SLOT // (kc or k)), np.float32)
        full[:k, :, :a.shape[1]] = a.reshape(k, P, a.shape[1])
        s[w] = full.transpose(1, 0, 2).reshape(P, SLOT)

    def group(name, *parts):
        g = ST.g[name]
        m = np.concatenate(parts, 1)
        for j in range(g.slots):
            rows = m[j * g.kc * P:(j + 1) * g.kc * P]
            put(g.w0 + j, rows, g.kc)

    for l in range(DEPTH):
        w = np.asarray(x["w_in"][l])

        def c(lo, n):
            return w[:, lo:lo + n]

        kc, vc, ks, vs, kw, vw = (c(1792 + 64 * i, 64) for i in range(6))
        df = 2188
        group(("proj", l, 0), c(0, 512), c(768, 512))
        group(("proj", l, 1), c(1536, 256), c(df, 512), ks, ks, kw, kw)
        group(("proj", l, 2), kc, kc, vc, vc)
        group(("nat", l), c(512, 256), c(1280, 256), c(df + 512, 256), vs, vw, c(2176, 12))
        for i, k in enumerate(("cmp_k_w1", "cmp_v_w1")):
            for h in range(2):
                put(SIDE_W * l + 2 * i + h, np.asarray(x[k][l])[:, P * h:P * h + P], s=side)
        a = np.asarray(x["ada_w_2"][l])
        for i in range(24):
            put(SIDE_W * l + CMP_W + i, a[:, T * i:T * (i + 1)], s=side)
        group(("out", l), np.asarray(x["w_out"][l]))
        for i in range(4):
            group(("up", l, i), np.asarray(x["w_up"][l])[:, D * i:D * (i + 1)])
        group(("down", l), np.asarray(x["w_down"][l]))
        f = np.asarray(x["ffn_w_in_2"][l])
        pairs = [f[:, P * (j + NFF * i):P * (j + NFF * i + 1)] for j in range(NFF) for i in range(2)]
        per = (4, 8)[l]
        for i in range(-(-2 * NFF // per)):
            group(("ffn_in", l, i), *pairs[per * i:per * (i + 1)])
        group(("ffn_out", l), np.asarray(x["ffn_w_out_2"][l]))
    a = np.asarray(x["m_w_up_2"][0])
    for i in range(4):
        group(("m_up", i), a[:, T2 * i:T2 * (i + 1)])
    gates = np.zeros((MK * P, P), np.float32)
    for z in range(2):
        for g in range(2):
            gates[:, 64 * g + 32 * z:64 * g + 32 * z + MH] = np.asarray(x["m_w_gates_2"])[0, z, :, g * MH:(g + 1) * MH]
    put(W("m_gates"), gates)
    wv, wqk, wog = (np.asarray(x[k][0]) for k in ("m_w_v_2", "m_w_qk_2", "m_w_og_2"))
    for h in range(MH):
        group(("m_v", h), wv[:, T2 * h:T2 * (h + 1)])
        group(("m_qk", h), wqk[:, T * h:T * (h + 1)], wqk[:, D + T * h:D + T * (h + 1)])
        group(("m_og", h), wog[:, T2 * h:T2 * (h + 1)])
    group("m_out", np.asarray(x["m_w_out_2"][0]))
    swap = np.concatenate([np.arange(16, 32), np.arange(16), np.arange(48, 64), np.arange(32, 48)])
    a = np.asarray(x["a_w_dkv_2"][0])
    group("a_dkv", a, a[:, T:][:, swap])
    group("a_dq", np.asarray(x["a_w_dq_2"][0]))
    a = np.asarray(x["a_w_ukv_2"][0]).reshape(2 * P, AH, 2, P)
    for i, name in enumerate(("a_ukv", "a_v")):
        group(name, a[:, :, i].reshape(2 * P, D))
    a = np.asarray(x["a_w_uq_2"][0]).reshape(3 * P, AH, 192)
    group(("a_uq", 0), a[:, :, :P].reshape(3 * P, D))
    r = a[:, :, P:]
    group(("a_uq", 1), np.concatenate([r, r[:, :, swap]], 2).reshape(3 * P, D))
    group("a_out", np.asarray(x["a_w_out_2"][0]))
    return s, side


def kernel(**inputs):
    import concourse.bacc as bacc
    from concourse.bass_utils import run_bass_kernel_spmd

    nc = bacc.Bacc("TRN2", target_bir_lowering=False, num_devices=1, dynamic_dma_scratch_size=1024)
    consts, onehot, strict, cmask = pack_constants()
    stream, side = pack_stream(inputs)
    arrays = {
        "in_tokens": np.concatenate([np.asarray(inputs["ctx_2"])[0], np.asarray(inputs["x"])[0]], 0),
        "in_stream": stream,
        "in_side": side,
        "in_params": pack_params(inputs),
        "in_params1": pack_params1(inputs, strict, cmask),
        "in_consts": consts,
        "in_onehot": onehot,
    }
    args = [nc.dram_tensor(name, a.shape, F32, kind="ExternalInput").ap() for name, a in arrays.items()]
    args.append(nc.dram_tensor("out_0", (1, T, D), F32, kind="ExternalOutput").ap())
    args.append(nc.dram_tensor("bias_vectors", (12, 512), F32, kind="Internal").ap())
    build(nc, *args)
    r = run_bass_kernel_spmd(nc, [arrays], core_ids=[0])
    return r.results[0]["out_0"]
```
